# Optimizing a Trainium2 kernel written in Bass

```python
import math
import jax, jax.numpy as jnp
from jax import lax
import numpy as np

D_MODEL = 2048
BATCH = 1
SEQ = 256
DEPTH = 1

D_MIX = D_MODEL
CONV_WIDTH = D_MIX // 4
CONV_GROUPS = 4
CONV_GROUP_DIM = CONV_WIDTH // CONV_GROUPS
CONV_K = 3
ATTN_HEAD_DIM = 64
ATTN_HEADS = (D_MIX // 4) // ATTN_HEAD_DIM
ATTN_KV_HEADS = 2
ATTN_WIDTH = ATTN_HEADS * ATTN_HEAD_DIM
ATTN_KV_WIDTH = ATTN_KV_HEADS * ATTN_HEAD_DIM
WINDOW = 128
ATTN_BLOCK = 128
GDN_HEAD_DIM = 128
GDN_WIDTH = D_MIX - CONV_WIDTH - ATTN_WIDTH
GDN_HEADS = GDN_WIDTH // GDN_HEAD_DIM
GDN_CONV_K = 4
GDN_CHUNK = 64
D_FF = 4 * D_MODEL
EPS = 1e-6

IN_SPLITS = (CONV_WIDTH, CONV_WIDTH, CONV_WIDTH,
             ATTN_WIDTH, ATTN_KV_WIDTH, ATTN_KV_WIDTH,
             GDN_WIDTH, GDN_WIDTH, GDN_WIDTH, GDN_WIDTH,
             GDN_HEADS, GDN_HEADS)
D_IN = sum(IN_SPLITS)

kernel_name = "hybrid_parallel_heads_conv_swa_gdn"

def rms_norm(x, g):
    xf = x.astype(jnp.float32)
    y = xf * lax.rsqrt(jnp.mean(xf * xf, axis=-1, keepdims=True) + EPS)
    return (y * g.astype(jnp.float32)).astype(x.dtype)

def l2_norm(x):
    return x * lax.rsqrt(jnp.sum(x * x, axis=-1, keepdims=True) + EPS)

def causal_depthwise_conv(x, w):
    K = w.shape[0]
    S = x.shape[1]
    xp = jnp.pad(x, ((0, 0), (K - 1, 0), (0, 0)))
    y = w[0] * xp[:, 0:S]
    for k in range(1, K):
        y = y + w[k] * xp[:, k:k + S]
    return y

def short_conv_mixer(b_gate, c_gate, x_in, conv_w):
    return b_gate * causal_depthwise_conv(c_gate * x_in, conv_w)

def sliding_window_attention(q, k, v, q_g, k_g, sinks):
    B, S, H, D = q.shape
    KV = k.shape[2]
    G = H // KV
    nb = S // ATTN_BLOCK
    q = rms_norm(q, q_g)
    k = rms_norm(k, k_g)
    qb = q.reshape(B, nb, ATTN_BLOCK, KV, G, D)
    pad = ((0, 0), (ATTN_BLOCK, 0), (0, 0), (0, 0))
    kp = jnp.pad(k, pad).reshape(B, nb + 1, ATTN_BLOCK, KV, D)
    vp = jnp.pad(v, pad).reshape(B, nb + 1, ATTN_BLOCK, KV, D)
    kb = jnp.concatenate([kp[:, :-1], kp[:, 1:]], axis=2)
    vb = jnp.concatenate([vp[:, :-1], vp[:, 1:]], axis=2)
    s = jnp.einsum('bnqkgd,bnskd->bnkgqs', qb, kb,
                   preferred_element_type=jnp.float32) * (D ** -0.5)
    qi = jnp.arange(ATTN_BLOCK)[:, None]
    si = jnp.arange(2 * ATTN_BLOCK)[None, :]
    rel = qi + ATTN_BLOCK - si
    band = (rel >= 0) & (rel < WINDOW)
    has_prev = (jnp.arange(nb) > 0)[:, None, None]
    valid = band[None] & (has_prev | (si >= ATTN_BLOCK)[None])
    s = jnp.where(valid[None, :, None, None], s, -jnp.inf)
    sink = sinks.astype(jnp.float32).reshape(KV, G)[None, None, :, :, None, None]
    m = jnp.maximum(jnp.max(s, axis=-1, keepdims=True), sink)
    p = jnp.exp(s - m)
    denom = jnp.sum(p, axis=-1, keepdims=True) + jnp.exp(sink - m)
    o = jnp.einsum('bnkgqs,bnskd->bnqkgd', p / denom, vb.astype(jnp.float32))
    return o.reshape(B, S, H, D).astype(q.dtype)

def gated_delta_rule(q, k, v, beta_logit, a_logit, A_log, dt_bias):
    dtype = v.dtype
    B, S, H, Dk = q.shape
    Dv = v.shape[-1]
    C = GDN_CHUNK
    nc = S // C
    f32 = jnp.float32
    q = l2_norm(q.astype(f32)) * (Dk ** -0.5)
    k = l2_norm(k.astype(f32))
    v = v.astype(f32)
    beta = jax.nn.sigmoid(beta_logit.astype(f32))
    g = -jnp.exp(A_log.astype(f32)) * jax.nn.softplus(a_logit.astype(f32) + dt_bias.astype(f32))

    def chunk4(t):
        return jnp.transpose(t.reshape(B, nc, C, H, t.shape[-1]), (0, 3, 1, 2, 4))

    def chunk3(t):
        return jnp.transpose(t.reshape(B, nc, C, H), (0, 3, 1, 2))

    qc, kc, vc = chunk4(q), chunk4(k), chunk4(v)
    bc, gc = chunk3(beta), jnp.cumsum(chunk3(g), axis=-1)
    tril = jnp.tril(jnp.ones((C, C), dtype=bool))
    strict = jnp.tril(jnp.ones((C, C), dtype=bool), -1)
    diff = gc[..., :, None] - gc[..., None, :]
    decay = jnp.where(tril, jnp.exp(jnp.where(tril, diff, 0.0)), 0.0)
    k_beta = kc * bc[..., None]
    A = jnp.where(strict, jnp.einsum('bhncd,bhnsd->bhncs', k_beta, kc) * decay, 0.0)
    T = jnp.eye(C, dtype=f32) + A
    w = lax.linalg.triangular_solve(T, k_beta * jnp.exp(gc)[..., None],
                                    left_side=True, lower=True, unit_diagonal=True)
    u = lax.linalg.triangular_solve(T, vc * bc[..., None],
                                    left_side=True, lower=True, unit_diagonal=True)
    qk = jnp.where(tril, jnp.einsum('bhncd,bhnsd->bhncs', qc, kc) * decay, 0.0)

    def to_scan(t):
        return jnp.moveaxis(t, 2, 0)

    def step(state, inp):
        q_i, k_i, w_i, u_i, qk_i, g_i = inp
        v_new = u_i - jnp.einsum('bhck,bhkv->bhcv', w_i, state)
        o = (jnp.einsum('bhck,bhkv->bhcv', q_i * jnp.exp(g_i)[..., None], state)
             + jnp.einsum('bhcs,bhsv->bhcv', qk_i, v_new))
        g_last = g_i[..., -1]
        state = (state * jnp.exp(g_last)[..., None, None]
                 + jnp.einsum('bhck,bhcv->bhkv', k_i * jnp.exp(g_last[..., None] - g_i)[..., None], v_new))
        return state, o

    state0 = jnp.zeros((B, H, Dk, Dv), f32)
    _, o = lax.scan(step, state0, (to_scan(qc), to_scan(kc), to_scan(w), to_scan(u),
                                   to_scan(qk), to_scan(gc)))
    o = jnp.transpose(o, (1, 0, 3, 2, 4)).reshape(B, S, H, Dv)
    return o.astype(dtype)

def hybrid_layer(x, norm1_g, w_in, conv_w, conv_out_g, q_norm_g, k_norm_g, attn_sinks, attn_out_g,
                 gdn_conv_w, gdn_A_log, gdn_dt_bias, gdn_norm_g, w_out, norm2_g, w_up, w_down):
    B, S, _ = x.shape
    h = rms_norm(x, norm1_g)
    proj = jnp.einsum('bsd,de->bse', h, w_in)
    split_points = np.cumsum(IN_SPLITS)[:-1].tolist()
    (cb, cc, cx, aq, ak, av, gq, gk, gv, gz, gb, ga) = jnp.split(proj, split_points, axis=-1)

    yc = short_conv_mixer(cb, cc, cx, conv_w)
    yc = rms_norm(yc.reshape(B, S, CONV_GROUPS, CONV_GROUP_DIM),
                  conv_out_g.reshape(CONV_GROUPS, CONV_GROUP_DIM)).reshape(B, S, CONV_WIDTH)

    ya = sliding_window_attention(aq.reshape(B, S, ATTN_HEADS, ATTN_HEAD_DIM),
                                  ak.reshape(B, S, ATTN_KV_HEADS, ATTN_HEAD_DIM),
                                  av.reshape(B, S, ATTN_KV_HEADS, ATTN_HEAD_DIM),
                                  q_norm_g, k_norm_g, attn_sinks)
    ya = rms_norm(ya, attn_out_g.reshape(ATTN_HEADS, ATTN_HEAD_DIM)).reshape(B, S, ATTN_WIDTH)

    qkv = jax.nn.silu(causal_depthwise_conv(jnp.concatenate([gq, gk, gv], axis=-1), gdn_conv_w))
    q_d, k_d, v_d = jnp.split(qkv, 3, axis=-1)
    hs = (B, S, GDN_HEADS, GDN_HEAD_DIM)
    o = gated_delta_rule(q_d.reshape(hs), k_d.reshape(hs), v_d.reshape(hs), gb, ga,
                         gdn_A_log, gdn_dt_bias)
    yg = (rms_norm(o, gdn_norm_g) * jax.nn.silu(gz.reshape(hs))).reshape(B, S, GDN_WIDTH)

    mix = jnp.concatenate([yc, ya, yg], axis=-1)
    x = x + jnp.einsum('bse,ed->bsd', mix, w_out)

    h2 = rms_norm(x, norm2_g)
    hid = jnp.square(jax.nn.relu(jnp.einsum('bsd,df->bsf', h2, w_up)))
    return x + jnp.einsum('bsf,fd->bsd', hid, w_down)

def setup_inputs(seed: int = 0) -> dict:
    key = jax.random.key(seed)
    ks = jax.random.split(key, 18)
    f32 = jnp.float32

    def nrm(k, shape, scale):
        return jax.random.normal(k, shape, f32) * scale

    def gain(k, shape):
        return 1.0 + 0.05 * jax.random.normal(k, shape, f32)

    dt = jnp.exp(jax.random.uniform(ks[12], (DEPTH, GDN_HEADS), f32, math.log(1e-3), math.log(1e-1)))
    return {
        "x": nrm(ks[0], (BATCH, SEQ, D_MODEL), 1.0),
        "norm1_g": gain(ks[1], (DEPTH, D_MODEL)),
        "w_in": nrm(ks[2], (DEPTH, D_MODEL, D_IN), D_MODEL ** -0.5),
        "conv_w": nrm(ks[3], (DEPTH, CONV_K, CONV_WIDTH), CONV_K ** -0.5),
        "conv_out_g": gain(ks[4], (DEPTH, CONV_WIDTH)),
        "q_norm_g": gain(ks[5], (DEPTH, ATTN_HEAD_DIM)),
        "k_norm_g": gain(ks[6], (DEPTH, ATTN_HEAD_DIM)),
        "attn_sinks": nrm(ks[7], (DEPTH, ATTN_HEADS), 1.0),
        "attn_out_g": gain(ks[8], (DEPTH, ATTN_WIDTH)),
        "gdn_conv_w": nrm(ks[9], (DEPTH, GDN_CONV_K, 3 * GDN_WIDTH), GDN_CONV_K ** -0.5),
        "gdn_A_log": jnp.log(jax.random.uniform(ks[10], (DEPTH, GDN_HEADS), f32, 1.0, 16.0)),
        "gdn_dt_bias": dt + jnp.log(-jnp.expm1(-dt)),
        "gdn_norm_g": gain(ks[11], (DEPTH, GDN_HEAD_DIM)),
        "w_out": nrm(ks[13], (DEPTH, D_MIX, D_MODEL), D_MIX ** -0.5),
        "norm2_g": gain(ks[14], (DEPTH, D_MODEL)),
        "w_up": nrm(ks[15], (DEPTH, D_MODEL, D_FF), D_MODEL ** -0.5),
        "w_down": nrm(ks[16], (DEPTH, D_FF, D_MODEL), D_FF ** -0.5),
    }

def reference(x, norm1_g, w_in, conv_w, conv_out_g, q_norm_g, k_norm_g, attn_sinks, attn_out_g,
              gdn_conv_w, gdn_A_log, gdn_dt_bias, gdn_norm_g, w_out, norm2_g, w_up, w_down):
    for l in range(DEPTH):
        x = hybrid_layer(x, norm1_g[l], w_in[l], conv_w[l], conv_out_g[l], q_norm_g[l], k_norm_g[l],
                         attn_sinks[l], attn_out_g[l], gdn_conv_w[l], gdn_A_log[l], gdn_dt_bias[l],
                         gdn_norm_g[l], w_out[l], norm2_g[l], w_up[l], w_down[l])
    return x


_drawn_inputs = setup_inputs


def setup_inputs(seed=0):
    import zlib

    import numpy as np

    out = dict(_drawn_inputs(seed))
    spreads = {}
    factors = {'conv_out_g': 2.78, 'attn_sinks': 64.0, 'attn_out_g': 2.87, 'gdn_norm_g': 2.981}
    for name, (base, spread) in spreads.items():
        noise = np.random.default_rng([zlib.crc32(name.encode()), seed]).standard_normal(out[name].shape)
        drawn = base * np.exp(spread * noise) if base else spread * noise
        out[name] = __import__('jax').numpy.asarray(drawn.astype(out[name].dtype))
    for name, factor in factors.items():
        out[name] = (out[name] * factor).astype(out[name].dtype)
    return out
```

```python
from contextlib import ExitStack
from math import log

import concourse.bass as bass
from concourse import mybir

F32 = mybir.dt.float32
F32R = mybir.dt.float32r
ALU = mybir.AluOpType
ACT = mybir.ActivationFunctionType
AX_X = mybir.AxisListType.X

P = 128
EPS = 1e-6
NEG = -1e30
LOWEST = -3e38
LN_EXP = "natural_log_exp_and_others"


def build(nc, x, norm1_g, w_in, conv_w, conv_out_g, q_norm_g, k_norm_g, attn_sinks, attn_out_g,
          gdn_conv_w, gdn_A_log, gdn_dt_bias, gdn_norm_g, w_out, norm2_g, w_up, w_down, out):
    S, D = x.shape[1], x.shape[2]
    FF = w_up.shape[2]
    MT = S // P
    KT = D // P
    NB = 512
    CT = NB // P
    KPC = 2
    CPB = KT // KPC
    RING = 4
    AHEAD = 3
    assert S == 256 and D == 2048 and FF % NB == 0 and MT == 2

    CONV_W = D // 4
    HA, DA = attn_sinks.shape[1], q_norm_g.shape[1]
    KV = 2
    HG, DG = gdn_A_log.shape[1], gdn_norm_g.shape[1]
    GDN_W = HG * DG
    assert DG == P and 2 * DA == P and HG == 8 and HA == 8 and CONV_W == NB and HA * DA == NB

    AT_Q = 3 * CONV_W
    AT_K = AT_Q + HA * DA
    KVW = 2 * KV * DA
    GD_Q = AT_K + KVW
    GD_K, GD_V, GD_Z = GD_Q + GDN_W, GD_Q + 2 * GDN_W, GD_Q + 3 * GDN_W
    GD_B = GD_Q + 4 * GDN_W
    BA = 2 * HG
    BLOCKS = [("kv", AT_K), ("aq", AT_Q),
              ("gk", GD_K), ("gq", GD_Q), ("gv", GD_V),
              ("gk", GD_K + NB), ("gq", GD_Q + NB), ("gv", GD_V + NB),
              ("cc", CONV_W), ("cx", 2 * CONV_W), ("cb", 0),
              ("gz", GD_Z), ("gz", GD_Z + NB)]
    NBLK = len(BLOCKS)
    AT_KV, AT_AQ, AT_CC, AT_CX, AT_CB, AT_Z = 0, 1, 8, 9, 10, 11
    QUADS = [1, 0, 2, 3]
    CPG = CT // KPC
    NCB = D // NB
    C_OUT = NBLK * CPB
    C_MLP = C_OUT + len(QUADS) * NCB * CPG
    C_LAST_QUAD = C_MLP - NCB * CPG
    FB = FF // NB
    C_LOOP = C_MLP + CPB
    PER = CPB + NCB * CPG
    TURNS = FB - 1
    C_LAST = C_LOOP + PER * TURNS
    CHUNKS = C_LAST + NCB * CPG
    G_MLP = len(QUADS) * NCB
    assert PER % RING == 0 and C_LOOP % RING == 0

    A_KV = CPB
    A_Q = 2 * CPB
    A_HEADS = A_Q + 3
    A_STEPS = 7
    A_NORM = A_HEADS + KV * A_STEPS
    GDN_START = [5 * CPB + 5, 5 * CPB + 5 + 28]
    SILU_AT = [5 * CPB + 4, 8 * CPB + 4]
    LEVELS = 7

    def after(b):
        return CPB * (b + 1)

    with ExitStack() as ctx:
        def sb(name, shape, dt=F32):
            return ctx.enter_context(nc.sbuf_tensor(name, shape, dt))

        def sem(name):
            return ctx.enter_context(nc.semaphore(name))

        raw = sb("raw", [P, RING, KPC, NB])
        w_hi = sb("w_hi", [P, RING, KPC, NB], F32R)
        w_lo = sb("w_lo", [P, RING, KPC, NB], F32R)
        x_sb = sb("x_sb", [P, MT, D])
        h_hi = sb("h_hi", [P, KT, S], F32R)
        h_lo = sb("h_lo", [P, KT, S], F32R)
        mix_hi = sb("mix_hi", [P, KT, S], F32R)
        mix_lo = sb("mix_lo", [P, KT, S], F32R)
        qkv = [[sb(f"gdn_{n}{b}", [P, CT, S]) for n in "kqv"] for b in range(2)]
        tok = sb("tok", [P, MT, NB])
        fm_a = sb("fm_a", [P, CT, S])
        fm_b = sb("fm_b", [P, CT, S])
        buf = [sb(f"buf{i}", [P, 2 * NB]) for i in range(4)]
        buf += [x_sb[:, i // 2, (i % 2) * 2 * NB:(i % 2 + 1) * 2 * NB] for i in range(4)]
        half = [sb(f"half{i}", [P, NB]) for i in range(6)]

        ident = sb("ident", [P, P])
        ones = sb("ones", [P, P])
        upper = sb("upper", [P, P])
        pair_ones = sb("pair_ones", [P, P])
        upper_add = sb("upper_add", [P, P])
        band = sb("band", [P, 2 * P])
        level = sb("level", [P, LEVELS, P])
        eps_col = sb("eps_col", [P, 1])
        q_scale = sb("q_scale", [P, 1])

        rows_a = half[0][0:96, 0:P]
        rows_b = half[0][0:56, P:2 * P]
        rows_n = half[0][0:KT, 2 * P:3 * P]
        cols_a = sb("cols_a", [P, 96])
        cols_b = sb("cols_b", [P, 56])
        heads_bc = sb("heads_bc", [P, 3, HG])
        ss = sb("ss", [P, MT, NCB])
        ssum = sb("ssum", [P, MT])
        rstd = sb("rstd", [P, MT])
        ba = sb("ba", [P, MT, BA])
        sc = [sb(f"sc{i}", [P, HG, MT]) for i in range(12)]
        e_alog = sb("e_alog", [P, HG])
        beta = sb("beta", [P, HG, MT])
        gate = sb("gate", [P, HG, MT])
        gcum = sb("gcum", [P, HG, MT])
        kdecay = sb("kdecay", [P, HG])
        kdiff = sb("kdiff", [P, HG])
        mx, mxs, nmx, esi, es, den, dsum, rden = (sb(n, [P, 8]) for n in (
            "mx", "mxs", "nmx", "esi", "es", "den", "dsum", "rden"))

        main = ctx.enter_context(nc.psum_tensor("main", [P, 2, MT, NB], F32))
        side = ctx.enter_context(nc.psum_tensor("side", [P, 4, NB], F32))

        N1, N2, CW, CO, AO, GN, QG, KG = KT + 23, 0, KT, KT + 12, KT + 16, KT + 20, KT + 21, KT + 22
        NROWS_B = KG + 1
        GC_TILES = 3 * GDN_W // P

        raw_loaded = [sem(f"raw_loaded{i}") for i in range(RING)]
        hi_ready, lo_ready, chunk_done = sem("hi_ready"), sem("lo_ready"), sem("chunk_done")
        x_loaded = [sem(f"x_loaded{i}") for i in range(NCB)]
        x_back, out_stored = sem("x_back"), sem("out_stored")
        rows_loaded, convw_loaded, heads_loaded = sem("rows_loaded"), sem("convw_loaded"), sem("heads_loaded")
        norm1_loaded = sem("norm1_loaded")
        const_step = sem("const_step")
        cols_turned, cols_ready = sem("cols_turned"), sem("cols_ready")
        ss_act, ss_dve, ssum_ready, rstd_ln, rstd_ready = (sem(n) for n in (
            "ss_act", "ss_dve", "ssum_ready", "rstd_ln", "rstd_ready"))
        h_turned, h_hi_ready, h_lo_ready = (sem(n) for n in ("h_turned", "h_hi_ready", "h_lo_ready"))
        blk_copied, blk_turned, pair_free, group_added = (sem(n) for n in (
            "blk_copied", "blk_turned", "pair_free", "group_added"))
        conv_first, conv_step, silu_done = sem("conv_first"), sem("conv_step"), sem("silu_done")
        gate_dve, gate_act, gate_pe = sem("gate_dve"), sem("gate_act"), sem("gate_pe")
        att_sq, att_sum, att_ln, att_rs, att_qk = (sem(n) for n in (
            "att_sq", "att_sum", "att_ln", "att_rs", "att_qk"))
        att_scores, att_sc, att_nm, att_exp, att_den, att_p = (sem(n) for n in (
            "att_scores", "att_sc", "att_nm", "att_exp", "att_den", "att_p"))
        att_pT, att_pT1, att_pT0, att_o, att_oe, att_on = (sem(n) for n in (
            "att_pT", "att_pT1", "att_pT0", "att_o", "att_oe", "att_on"))
        cm_a, cm_prod, cm_first, cm_step, cm_out, cm_sq, cm_sum, cm_ln, cm_rs, cm_on = (sem(n) for n in (
            "cm_a", "cm_prod", "cm_first", "cm_step", "cm_out", "cm_sq", "cm_sum", "cm_ln", "cm_rs", "cm_on"))
        z_silu, z_prod = sem("z_silu"), sem("z_prod")
        mix_hi_ready, mix_lo_ready = sem("mix_hi_ready"), sem("mix_lo_ready")
        (gdn_sq, gdn_sum, gdn_ln, gdn_rs, gdn_kn, gdn_qn, gdn_rows, gdn_grow, gdn_brow, gdn_rm, gdn_rm2,
         gdn_eg, gdn_dec, gdn_kb, gdn_vT, gdn_vb, gdn_kbe, gdn_gram, gdn_qk, gdn_AT, gdn_QKT, gdn_ktok,
         gdn_kdec, gdn_tmp, gdn_MT0, gdn_Mps, gdn_M0, gdn_Al, gdn_Y, gdn_Ysb, gdn_upd, gdn_M, gdn_MTd,
         gdn_v0ps, gdn_v0, gdn_Sps, gdn_S, gdn_o0, gdn_kSps, gdn_r1, gdn_v1ps, gdn_v1, gdn_o1ps, gdn_o1,
         gdn_osq, gdn_osum, gdn_oln, gdn_ors, gdn_on) = (sem("gdn_" + n) for n in (
            "sq", "sum", "ln", "rs", "kn", "qn", "rows", "grow", "brow", "rm", "rm2",
            "eg", "dec", "kb", "vT", "vb", "kbe", "gram", "qk", "AT", "QKT", "ktok",
            "kdec", "tmp", "MT0", "Mps", "M0", "Al", "Y", "Ysb", "upd", "M", "MTd",
            "v0ps", "v0", "Sps", "S", "o0", "kSps", "r1", "v1ps", "v1", "o1ps", "o1",
            "osq", "osum", "oln", "ors", "on"))
        hid_relu, hid_turned, hid_hi, hid_lo = (sem(n) for n in (
            "hid_relu", "hid_turned", "hid_hi", "hid_lo"))

        x_dram = x.rearrange("o (m p) d -> (o p) m d", p=P)
        out_dram = out.rearrange("o (m p) d -> (o p) m d", p=P)
        win_v = w_in.rearrange("o (t p) n -> (o p) t n", p=P)
        wout_v = w_out.rearrange("o (t p) n -> (o p) t n", p=P)
        wup_v = w_up.rearrange("o (t p) n -> (o p) t n", p=P)
        wdn_v = w_down.rearrange("o (t p) n -> (o p) t n", p=P)

        def flat(t):
            return t.rearrange("p a b -> p (a b)")

        def pair_ps(i):
            return main[:, i].rearrange("p m n -> p (m n)")

        def side_ps(i):
            return side[:, 2 * i:2 * i + 2].rearrange("p m n -> p (m n)")

        def tiles(t, n):
            return t.rearrange("p (a b) -> p a b", a=n)

        def over(t, n):
            return t.unsqueeze(1).to_broadcast([P, n, t.shape[1]])

        def along(t, w):
            return t.unsqueeze(2).to_broadcast([P, t.shape[1], w])

        att_k = buf[1][:, 0:NB]
        vals = tiles(buf[1][:, NB:NB + MT * KV * DA], MT)
        p1 = tiles(buf[2][:], 4)
        p0 = tiles(half[0][:], 4)

        def turn_ps(which, j):
            if which == 0:
                return (side_ps(0), pair_ps(1), side_ps(1), side_ps(0))[j]
            return side_ps(1)

        def tap(b, k, t):
            first = {"gq": 0, "gk": HG, "gv": 2 * HG}[BLOCKS[b][0]]
            return k * GC_TILES + first + CT * ((b - 2) // 3) + t

        def raw_value(c):
            return 16 * (c // RING + 1) + 16 * min(c // RING + 1, CPB // RING)

        block = ctx.enter_context(nc.Block())

        @block.sync
        def _(sp):
            def load(c, slot, src):
                if c is not None:
                    sp.wait_ge(lo_ready, c)
                sp.dma_start(raw[:, slot], src).then_inc(raw_loaded[slot], 16)

            for c in range(C_OUT):
                b, k = c // CPB, c % CPB
                kind, col = BLOCKS[b]
                rows = slice(KPC * k, KPC * (k + 1))
                if c < NCB:
                    sp.dma_start(x_sb[:, :, c * NB:(c + 1) * NB],
                                 x_dram[:, :, c * NB:(c + 1) * NB]).then_inc(x_loaded[c], 16)
                free = c - RING + 1 if c >= RING else None
                if kind == "kv":
                    if free is not None:
                        sp.wait_ge(lo_ready, free)
                    sp.dma_start(raw[:, c % RING, :, 0:KVW],
                                 win_v[:, rows, col:col + KVW]).then_inc(raw_loaded[c % RING], 16)
                    sp.dma_start(raw[:, c % RING, :, KVW:KVW + BA],
                                 win_v[:, rows, GD_B:GD_B + BA]).then_inc(raw_loaded[c % RING], 16)
                else:
                    load(free, c % RING, win_v[:, rows, col:col + NB])
            for c in range(C_OUT, C_MLP):
                g, k = (c - C_OUT) // CPG, (c - C_OUT) % CPG
                t = QUADS[g // NCB] * CT + k * KPC
                n = g % NCB
                load(c - RING + 1, c % RING, wout_v[:, t:t + KPC, n * NB:(n + 1) * NB])
            for c in range(C_MLP, C_LOOP):
                k = c - C_MLP
                load(c - RING + 1, c % RING, wup_v[:, KPC * k:KPC * (k + 1), 0:NB])
            with sp.Fori(0, TURNS) as it:
                for s in range(PER):
                    free = it * PER + (C_LOOP + s - RING + 1)
                    if s < CPB:
                        src = wup_v[:, KPC * s:KPC * (s + 1), bass.ds(it * NB + NB, NB)]
                    else:
                        n, k = (s - CPB) // CPG, (s - CPB) % CPG
                        src = wdn_v[:, bass.ds(it * CT + k * KPC, KPC), n * NB:(n + 1) * NB]
                    load(free, s % RING, src)
            for c in range(C_LAST, CHUNKS):
                n, k = (c - C_LAST) // CPG, (c - C_LAST) % CPG
                t = (FB - 1) * CT + k * KPC
                load(c - RING + 1, c % RING, wdn_v[:, t:t + KPC, n * NB:(n + 1) * NB])
            for n in range(NCB):
                sp.wait_ge(group_added, G_MLP + NCB * (FB - 1) + n + 1)
                sp.dma_start(out_dram[:, :, n * NB:(n + 1) * NB],
                             x_sb[:, :, n * NB:(n + 1) * NB]).then_inc(out_stored, 16)
            sp.wait_ge(out_stored, 16 * NCB)

        N_CONST = 16 + 3 * LEVELS

        @block.gpsimd
        def _(pool):
            steps = [0]

            def step(ins):
                steps[0] += 1
                ins.then_inc(const_step, 1)
                pool.wait_ge(const_step, steps[0])

            def where(t, base, pattern, mult, fill, op=ALU.is_ge):
                step(pool.affine_select(out=t, in_=t, compare_op=op, fill=fill, base=base,
                                        pattern=pattern, channel_multiplier=mult))

            step(pool.memset(ident[:], 1.0))
            where(ident[:], 0, [[-1, P]], 1, 0.0, ALU.is_equal)
            step(pool.memset(eps_col[:], EPS))
            for row, v in ((N2, norm2_g), (CO, conv_out_g), (AO, attn_out_g), (GN, gdn_norm_g)):
                n = v.shape[1] // P
                pool.dma_start(rows_b[row:row + n, :], v.rearrange("o (t n) -> (o t) n", n=P)).then_inc(rows_loaded, 16)
            pool.dma_start(rows_b[CW:CW + 3 * CT, :],
                           conv_w.rearrange("o k (t n) -> (o k t) n", n=P)).then_inc(rows_loaded, 16)
            for row, v in ((QG, q_norm_g), (KG, k_norm_g)):
                for j in range(2):
                    pool.dma_start(rows_b[row:row + 1, j * DA:(j + 1) * DA], v).then_inc(rows_loaded, 16)
            pool.dma_start(rows_a, gdn_conv_w.rearrange("o k (t n) -> (o k t) n", n=P)).then_inc(convw_loaded, 16)
            for i, v in enumerate((gdn_A_log, gdn_dt_bias, attn_sinks)):
                pool.dma_start(heads_bc[:, i], v[0].partition_broadcast(P)).then_inc(heads_loaded, 16)
            step(pool.memset(q_scale[:], -0.5 * log(DG)))
            step(pool.memset(ones[:], 1.0))
            step(pool.memset(upper[:], 1.0))
            where(upper[:], 0, [[1, P]], -1, 0.0)
            step(pool.memset(upper_add[:], 0.0))
            where(upper_add[:], 0, [[1, P]], -1, NEG)
            step(pool.memset(pair_ones[:], 0.0))
            step(pool.memset(pair_ones[0:DA, 0:DA], 1.0))
            step(pool.memset(pair_ones[DA:P, DA:P], 1.0))
            step(pool.memset(band[:], 0.0))
            where(band[:, 0:P], -1, [[1, P]], -1, NEG)
            where(band[:, P:2 * P], 0, [[-1, P]], 1, NEG)
            step(pool.memset(level[:], 0.0))
            for l in range(LEVELS):
                w = 2 ** l
                blocks = level[:, l].rearrange("p (n h w) -> p n h w", h=2, w=w)
                step(pool.memset(blocks[:, :, 1, :], 1.0))
                n = P // (2 * w)
                upper_half = blocks[:, :, 1, :]
                where(upper_half, 0, [[-2 * w, n], [0, w]], 1, 0.0)
                where(upper_half, w - 1, [[2 * w, n], [0, w]], -1, 0.0)

            for b in range(2):
                h = slice(4 * b, 4 * b + 4)
                units = 2 * CT
                pool.wait_ge(gate_dve, 13)
                if b == 0:
                    pool.wait_ge(att_scores, KV)
                    pool.wait_ge(att_o, KV)
                else:
                    pool.wait_ge(gdn_Y, 6 * b)
                pool.tensor_tensor(tiles(buf[0][:], units), over(upper[:], units),
                                   along(flat(gate[:, h]), P), ALU.mult)
                pool.tensor_tensor(tiles(buf[1][:], units), over(ident[:], units),
                                   along(flat(beta[:, h]), P), ALU.mult).then_inc(gdn_rows, 1)
                pool.wait_ge(gdn_rm, b + 1)
                pool.tensor_tensor(tiles(buf[0][:], units), tiles(buf[0][:], units),
                                   along(flat(gcum[:, h]), P), ALU.subtract).then_inc(gdn_rm2, 1)
                pool.wait_ge(gdn_AT, b + 1)
                pool.wait_ge(gdn_brow, b + 1)
                pool.tensor_tensor(tiles(buf[1][:], units), tiles(buf[4], units),
                                   over(level[:, 0], units), ALU.mult).then_inc(gdn_tmp, 1)
                pool.wait_ge(gdn_tmp, b + 1)
                pool.tensor_tensor(tiles(buf[7], units), over(ident[:], units),
                                   tiles(buf[1][:], units), ALU.subtract).then_inc(gdn_MT0, 1)
                for l in range(1, LEVELS):
                    if l == 1:
                        pool.wait_ge(gdn_MT0, b + 1)
                    elif l == 2:
                        pool.wait_ge(gdn_QKT, b + 1)
                    else:
                        pool.wait_ge(gdn_Y, 6 * b + l - 2)
                    pool.tensor_tensor(tiles(buf[l % 2][:], units), tiles(buf[4], units),
                                       over(level[:, l], units), ALU.mult).then_inc(gdn_Al, 1)

        @block.scalar
        def _(act):
            def hi(loaded, slot, n=NB, used=None):
                act.wait_ge(raw_loaded[slot], loaded)
                if used is not None:
                    act.wait_ge(chunk_done, used)
                act.activation(w_hi[:, slot, :, 0:n], raw[:, slot, :, 0:n], ACT.Copy).then_inc(hi_ready, 1)

            def hi_of(c):
                if c < CHUNKS:
                    hi(raw_value(c), c % RING, KVW + BA if c < CPB else NB, c - RING + 1 if c >= RING else None)

            def inverse_root(ps, tmp, scale, waited, value, ln_sem, out_sem, bias=0.0):
                act.wait_ge(waited, value)
                act.activation(tmp, ps, ACT.Ln, scale=scale, bias=eps_col[:, 0:1]).then_inc(ln_sem, 1)
                act.wait_ge(ln_sem, value)
                act.activation(tmp, tmp, ACT.Exp, scale=-0.5, bias=bias).then_inc(out_sem, 1)

            def square(which, n):
                q = which * NCB + n
                if which == 0:
                    act.wait_ge(x_loaded[n], 16)
                else:
                    act.wait_ge(group_added, G_MLP - NCB + n + 1)
                if q > 0:
                    act.wait_ge(ss_act, q)
                act.activation(fm_a[:, 0:2].rearrange("p a b -> p (a b)"), x_sb[:, 0, n * NB:(n + 1) * NB],
                               ACT.Square, accum_out=ss[:, 0, n:n + 1]).then_inc(ss_act, 1)

            def scale_of_tokens(which):
                act.wait_ge(ssum_ready, which + 1)
                act.activation(rstd[:], ssum[:], ACT.Ln, scale=1.0 / D, bias=eps_col[:, 0:1]).then_inc(rstd_ln, 1)
                act.wait_ge(rstd_ln, which + 1)
                act.activation(rstd[:], rstd[:], ACT.Exp, scale=-0.5).then_inc(rstd_ready, 1)

            def piece(which, j):
                act.wait_ge(h_turned, which * NCB + j + 1)
                ps = turn_ps(which, j)
                for t in range(CT):
                    k = CT * j + t
                    g = (N2 if which else N1) + k
                    last = act.activation(h_hi[:, k], ps[:, t * S:(t + 1) * S], ACT.Copy, scale=cols_b[:, g:g + 1])
                last.then_inc(h_hi_ready, 1)

            def mixed(order, first, src, gain, waited, value):
                act.wait_ge(waited, value)
                if gain is None:
                    act.activation(mix_hi[:, first:first + CT], src[:], ACT.Copy).then_inc(mix_hi_ready, 1)
                    return
                for t in range(CT):
                    last = act.activation(mix_hi[:, first + t], src[:, t], ACT.Copy,
                                          scale=cols_b[:, gain + t:gain + t + 1])
                last.then_inc(mix_hi_ready, 1)

            def copy_block(b):
                act.wait_ge(chunk_done, after(b))
                if b == 0:
                    act.wait_ge(rstd_ready, 1)
                for m in range(MT):
                    ps, scale = main[:, b % 2, m], rstd[:, m:m + 1]
                    if b == AT_KV:
                        keys = ps[:, 0:KV * DA].rearrange("p (k d) -> p k d", d=DA)
                        dup = tok[:, m, 0:KV * P].rearrange("p (k j d) -> p k j d", j=2, d=DA)
                        for j in range(2):
                            act.activation(dup[:, :, j], keys, ACT.Copy, scale=scale)
                        act.activation(vals[:, m], ps[:, KV * DA:KVW], ACT.Copy, scale=scale)
                        last = act.activation(ba[:, m], ps[:, KVW:KVW + BA], ACT.Copy, scale=scale)
                    else:
                        last = act.activation(tok[:, m], ps, ACT.Copy, scale=scale)
                last.then_inc(blk_copied, 1)

            def side_work(c):
                for b in range(NBLK):
                    if c == after(b):
                        copy_block(b)
                for n in range(NCB):
                    if c == C_LAST_QUAD + CPG * n + CPG - 1:
                        square(1, n)
                    if c == C_LAST_QUAD + CPG * n + CPG + 1:
                        piece(1, n)
                if c == C_MLP + 3:
                    scale_of_tokens(1)
                if c == A_KV + 1:
                    act.wait_ge(blk_turned, 1)
                    act.activation(buf[4][:, 0:NB], pair_ps(0)[:, 0:NB], ACT.Square).then_inc(att_sq, 1)
                if c == A_KV + 2:
                    inverse_root(side[:, 0], buf[4][:, 0:NB], 1.0 / DA, att_sum, 1, att_ln, att_rs)
                if c == A_KV + 3:
                    act.wait_ge(gate_dve, 3)
                    act.activation(sc[3][:], sc[0][:], ACT.Exp)
                    act.activation(sc[4][:], sc[2][:], ACT.Exp)
                    act.wait_ge(heads_loaded, 48)
                    act.activation(e_alog[:], heads_bc[:, 0], ACT.Exp).then_inc(gate_act, 1)
                if c == A_KV + 4:
                    act.wait_ge(gate_dve, 5)
                    act.activation(sc[7][:], sc[6][:], ACT.Ln).then_inc(gate_act, 1)
                if c == A_KV + 7:
                    act.wait_ge(gate_dve, 14)
                    act.activation(kdecay[:], kdiff[:], ACT.Exp).then_inc(gate_act, 1)
                if c == A_Q + 1:
                    act.wait_ge(blk_turned, 2)
                    act.activation(buf[4], pair_ps(1), ACT.Square).then_inc(att_sq, 1)
                if c == A_Q + 2:
                    inverse_root(side_ps(0), buf[4], 1.0 / DA, att_sum, 2, att_ln, att_rs)
                for kv in range(KV):
                    a = A_HEADS + A_STEPS * kv
                    if c == a + 2:
                        act.wait_ge(att_nm, 3 * (kv + 1))
                        for u in range(4):
                            act.activation(p1[:, u], p1[:, u], ACT.Exp, bias=nmx[:, u:u + 1], accum_out=den[:, u:u + 1])
                            act.activation(p0[:, u], p0[:, u], ACT.Exp, bias=nmx[:, 4 + u:5 + u],
                                           accum_out=den[:, 4 + u:5 + u])
                        act.activation(es[:], esi[:], ACT.Exp).then_inc(att_exp, 1)
                    if c == a + 5:
                        act.wait_ge(att_pT, kv + 1)
                        act.activation(buf[3][:], side_ps(0), ACT.Copy).then_inc(att_pT1, 1)
                    if c == a + 6:
                        act.wait_ge(att_o, kv + 1)
                        act.activation(fm_b[:, 2 * kv:2 * kv + 2].rearrange("p r (m q) -> p m r q", m=MT),
                                       side[:, 3].rearrange("p (m r q) -> p m r q", m=MT, r=2),
                                       ACT.Copy).then_inc(att_oe, 1)
                if c == A_NORM:
                    act.wait_ge(att_oe, KV)
                    act.activation(buf[4], flat(fm_b[:]), ACT.Square).then_inc(att_sq, 1)
                if c == A_NORM + 1:
                    inverse_root(side_ps(0), buf[4], 1.0 / DA, att_sum, 3, att_ln, att_rs)
                if c == A_NORM + 2:
                    mixed(0, CT, fm_b, AO, att_on, 1)
                for b in range(2, 8):
                    if c == after(b) + 1:
                        act.wait_ge(blk_turned, b + 1)
                        dst = qkv[(b - 2) // 3][(b - 2) % 3]
                        for t in range(CT):
                            w = tap(b, 3, t)
                            last = act.activation(dst[:, t], pair_ps(b % 2)[:, t * S:(t + 1) * S], ACT.Copy,
                                                  scale=cols_a[:, w:w + 1])
                        last.then_inc(conv_first, 1)
                for i in range(2):
                    if c == SILU_AT[i]:
                        act.wait_ge(conv_step, 9 * (i + 1))
                        for n in range(3):
                            act.activation(flat(qkv[i][n][:]), flat(qkv[i][n][:]), ACT.Silu).then_inc(silu_done, 1)
                        act.preload_act_table_set(LN_EXP)
                    gdn(i, c - GDN_START[i])
                if c == after(AT_CC) + 1:
                    act.wait_ge(blk_turned, AT_CC + 1)
                    act.activation(flat(fm_a[:]), pair_ps(AT_CC % 2), ACT.Copy).then_inc(cm_a, 1)
                if c == after(AT_CX) + 2:
                    act.wait_ge(cm_prod, 1)
                    for t in range(CT):
                        w = CW + 2 * CT + t
                        last = act.activation(fm_b[:, t], fm_a[:, t], ACT.Copy, scale=cols_b[:, w:w + 1])
                    last.then_inc(cm_first, 1)
                if c == after(AT_CB) + 1:
                    act.wait_ge(cm_out, 1)
                    act.activation(flat(tok[:]), flat(fm_b[:]), ACT.Square).then_inc(cm_sq, 1)
                if c == after(AT_CB) + 3:
                    act.wait_ge(cm_sum, 1)
                    act.activation(flat(tok[:]), pair_ps(AT_CB % 2), ACT.Ln, scale=1.0 / P,
                                   bias=eps_col[:, 0:1]).then_inc(cm_ln, 1)
                    act.wait_ge(cm_ln, 1)
                    act.activation(flat(tok[:]), flat(tok[:]), ACT.Exp, scale=-0.5).then_inc(cm_rs, 1)
                if c == after(AT_CB) + 5:
                    mixed(1, 0, fm_b, CO, cm_on, 1)
                for i in range(2):
                    b = AT_Z + i
                    if c == after(b) + 1:
                        act.wait_ge(blk_turned, b + 1)
                        if i == 1:
                            act.wait_ge(mix_lo_ready, 3)
                        act.activation(flat(fm_a[:]), pair_ps(b % 2), ACT.Silu).then_inc(z_silu, 1)
                        act.preload_act_table_set(LN_EXP)
                    if c == after(b) + 3:
                        mixed(2 + i, 2 * CT + CT * i, fm_a, None, z_prod, i + 1)
                if c == GDN_START[1] + 26:
                    act.wait_ge(gdn_o1ps, 2)
                    act.wait_ge(gdn_r1, 2)
                    act.dma_start(x_sb[:], x_dram).then_inc(x_back, 16)

            def gdn(i, s):
                k_t, q_t, v_t = qkv[i]
                if s == 0:
                    act.wait_ge(silu_done, 3 * (i + 1))
                    if i:
                        act.wait_ge(gdn_on, i)
                    act.activation(buf[2][:], flat(k_t[:]), ACT.Square).then_inc(gdn_sq, 1)
                    act.activation(buf[3][:], flat(q_t[:]), ACT.Square).then_inc(gdn_sq, 1)
                if s == 1:
                    inverse_root(side_ps(0), buf[2][:], 1.0, gdn_sum, 2 * i + 1, gdn_ln, gdn_rs)
                if s == 2:
                    inverse_root(side_ps(1), buf[3][:], 1.0, gdn_sum, 2 * i + 2, gdn_ln, gdn_rs, bias=q_scale[:, 0:1])
                if s == 3:
                    act.wait_ge(gdn_grow, i + 1)
                    act.activation(tiles(half[0][:], CT),
                                   side_ps(0).rearrange("p (h m t) -> p h m t", h=CT, m=MT)[:, :, 1],
                                   ACT.Exp).then_inc(gdn_eg, 1)
                if s == 5:
                    act.wait_ge(gdn_rm2, i + 1)
                    act.activation(buf[0][:], buf[0][:], ACT.Exp).then_inc(gdn_dec, 1)
                if s == 9:
                    act.wait_ge(gdn_Mps, i + 1)
                    act.wait_ge(gdn_kbe, 2 * i + 2)
                    act.activation(buf[3][:], side_ps(0), ACT.Copy).then_inc(gdn_M0, 1)
                for l in range(1, LEVELS):
                    if s == 8 + 2 * l:
                        act.wait_ge(gdn_Y, 6 * i + l)
                        act.activation(buf[2][:], side_ps(1), ACT.Copy).then_inc(gdn_Ysb, 1)
                if s == 22:
                    act.wait_ge(gdn_v0ps, i + 1)
                    act.activation(half[4][:], side[:, 0], ACT.Copy).then_inc(gdn_v0, 1)
                if s == 25:
                    act.wait_ge(gdn_v1ps, i + 1)
                    act.activation(half[4][:], side[:, 0], ACT.Copy).then_inc(gdn_v1, 1)
                if s == 26:
                    act.wait_ge(gdn_o1ps, i + 1)
                    act.activation(q_t[:, :, P:S], tiles(side[:, 1], CT), ACT.Copy).then_inc(gdn_o1, 1)
                    act.wait_ge(gdn_o1, i + 1)
                    act.wait_ge(gdn_o0, i + 1)
                    act.activation(buf[2][:], flat(q_t[:]), ACT.Square).then_inc(gdn_osq, 1)
                if s == 27:
                    inverse_root(side_ps(1), buf[2][:], 1.0 / DG, gdn_osum, i + 1, gdn_oln, gdn_ors)

            act.dma_start(rows_n, norm1_g.rearrange("o (t n) -> (o t) n", n=P)).then_inc(norm1_loaded, 16)
            act.preload_act_table_set(LN_EXP)
            hi_of(0)
            act.wait_ge(cols_ready, 1)
            for j in range(NCB):
                piece(0, j)
                if 0 < j < AHEAD:
                    hi_of(j)
            act.wait_ge(const_step, 3)
            for n in range(NCB):
                square(0, n)
            scale_of_tokens(0)
            for c in range(C_LOOP):
                hi_of(c + AHEAD)
                side_work(c)

            def relu(value):
                act.wait_ge(chunk_done, value)
                for m in range(MT):
                    last = act.activation(tok[:, m], side[:, m], ACT.Relu, scale=rstd[:, m:m + 1])
                last.then_inc(hid_relu, 1)

            def square_hidden(value):
                act.wait_ge(hid_turned, value)
                act.activation(flat(fm_a[:]), side_ps(1), ACT.Square)
                act.activation(mix_hi[:, 0:CT], tiles(side_ps(1), CT), ACT.Square).then_inc(hid_hi, 1)

            relu(C_LOOP)
            with act.Fori(0, TURNS) as it:
                for s in range(PER):
                    c = C_LOOP + s + AHEAD
                    hi(it * (16 * PER // RING) + raw_value(c), c % RING, NB, it * PER + (c - RING + 1))
                    if s == 0:
                        square_hidden(it + 1)
                    if s == CPB:
                        relu(it * PER + (C_LOOP + CPB))
            for c in range(C_LAST, CHUNKS):
                hi_of(c + AHEAD)
                if c == C_LAST:
                    square_hidden(FB)

        @block.vector
        def _(dve):
            def lo(ready, slot, n=NB):
                dve.wait_ge(hi_ready, ready)
                dve.tensor_tensor(w_lo[:, slot, :, 0:n], raw[:, slot, :, 0:n],
                                  w_hi[:, slot, :, 0:n].bitcast(F32), ALU.subtract).then_inc(lo_ready, 1)

            def lo_of(c):
                if c < CHUNKS:
                    lo(c + 1, c % RING, KVW + BA if c < CPB else NB)

            def square(which, n):
                q = which * NCB + n
                if which == 0:
                    dve.wait_ge(x_loaded[n], 16)
                else:
                    dve.wait_ge(group_added, G_MLP - NCB + n + 1)
                if q > 0:
                    dve.wait_ge(ss_dve, q)
                cols = x_sb[:, 1, n * NB:(n + 1) * NB]
                dve.tensor_tensor_reduce(fm_a[:, 2:4].rearrange("p a b -> p (a b)"), cols, cols, 1.0, 0.0,
                                         ALU.mult, ALU.add, ss[:, 1, n:n + 1]).then_inc(ss_dve, 1)

            def sum_of_squares(which):
                dve.wait_ge(ss_act, NCB * (which + 1))
                dve.wait_ge(ss_dve, NCB * (which + 1))
                dve.tensor_reduce(ssum[:], ss[:], AX_X, ALU.add).then_inc(ssum_ready, 1)

            def piece(which, j):
                dve.wait_ge(h_hi_ready, which * NCB + j + 1)
                ps = turn_ps(which, j)
                for t in range(CT):
                    k = CT * j + t
                    g = (N2 if which else N1) + k
                    last = dve.scalar_tensor_tensor(h_lo[:, k], ps[:, t * S:(t + 1) * S], cols_b[:, g:g + 1],
                                                    h_hi[:, k].bitcast(F32), ALU.mult, ALU.subtract)
                last.then_inc(h_lo_ready, 1)

            def mixed(order, first, src, gain):
                dve.wait_ge(mix_hi_ready, order + 1)
                if gain is None:
                    dve.tensor_tensor(mix_lo[:, first:first + CT], src[:],
                                      mix_hi[:, first:first + CT].bitcast(F32), ALU.subtract).then_inc(mix_lo_ready, 1)
                    return
                for t in range(CT):
                    last = dve.scalar_tensor_tensor(mix_lo[:, first + t], src[:, t], cols_b[:, gain + t:gain + t + 1],
                                                    mix_hi[:, first + t].bitcast(F32), ALU.mult, ALU.subtract)
                last.then_inc(mix_lo_ready, 1)

            def add_group(done, pair, n):
                dve.wait_ge(chunk_done, done)
                cols = x_sb[:, :, n * NB:(n + 1) * NB]
                dve.tensor_tensor(cols, main[:, pair], cols, ALU.add).then_inc(group_added, 1)

            def add_group_of(c):
                g = (c - C_OUT) // CPG
                add_group(c + 1, (g + 1) % 2, g % NCB)

            gates = [0]

            def gate_op(ins):
                gates[0] += 1
                ins.then_inc(gate_dve, 1)
                dve.wait_ge(gate_dve, gates[0])

            def side_work(c):
                if C_OUT <= c < C_MLP and c % CPG == CPG - 1:
                    if c == C_OUT + CPG - 1:
                        dve.wait_ge(x_back, 16)
                    add_group_of(c)
                for n in range(NCB):
                    if c == C_LAST_QUAD + CPG * n + CPG - 1:
                        square(1, n)
                    if c == C_LAST_QUAD + CPG * n + CPG + 1:
                        piece(1, n)
                if c == C_MLP + 2:
                    sum_of_squares(1)
                if c == 3:
                    dve.wait_ge(cols_turned, 3)
                    dve.tensor_copy(cols_b[:, 0:NROWS_B], side[:, 3, 0:NROWS_B]).then_inc(cols_ready, 1)
                    dve.tensor_copy(cols_a[:], side[:, 3, P:P + 96]).then_inc(cols_ready, 1)
                if c == A_KV + 2:
                    dve.wait_ge(att_rs, 1)
                    dve.scalar_tensor_tensor(att_k, pair_ps(0)[:, 0:NB], cols_b[:, KG:KG + 1], buf[4][:, 0:NB],
                                             ALU.mult, ALU.mult).then_inc(att_qk, 1)
                    dve.wait_ge(att_qk, 1)
                    dve.engine_nop().then_inc(pair_free, 1)
                if c == A_KV + 1:
                    dve.wait_ge(blk_copied, 1)
                    dve.wait_ge(heads_loaded, 48)
                    b_in = ba[:, :, 0:HG].rearrange("p m h -> p h m")
                    a_in = ba[:, :, HG:BA].rearrange("p m h -> p h m")
                    gate_op(dve.tensor_scalar(sc[0][:], b_in, -1.0, 87.0, ALU.mult, ALU.min))
                    gate_op(dve.tensor_tensor(sc[1][:], a_in, along(heads_bc[:, 1], MT), ALU.add))
                    gate_op(dve.scalar_tensor_tensor(sc[2][:], sc[1][:], -1.0, sc[1][:], ALU.mult, ALU.min))
                if c == A_KV + 3:
                    dve.wait_ge(gate_act, 1)
                    gate_op(dve.tensor_scalar(sc[5][:], sc[3][:], 1.0, None, ALU.add))
                    gate_op(dve.tensor_scalar(sc[6][:], sc[4][:], 1.0, None, ALU.add))
                    gate_op(dve.reciprocal(beta[:], sc[5][:]))
                    gate_op(dve.scalar_tensor_tensor(sc[8][:], sc[6][:], 1.0, sc[4][:], ALU.subtract, ALU.subtract))
                    gate_op(dve.reciprocal(sc[9][:], sc[6][:]))
                    gate_op(dve.tensor_tensor(sc[10][:], sc[8][:], sc[9][:], ALU.mult))
                if c == A_KV + 5:
                    dve.wait_ge(gate_act, 2)
                    gate_op(dve.tensor_tensor(sc[11][:], sc[7][:], sc[10][:], ALU.subtract))
                    gate_op(dve.scalar_tensor_tensor(sc[0][:], sc[1][:], 0.0, sc[11][:], ALU.max, ALU.add))
                    gate_op(dve.scalar_tensor_tensor(gate[:], sc[0][:], -1.0, along(e_alog[:], MT), ALU.mult, ALU.mult))
                if c == A_KV + 6:
                    dve.wait_ge(gate_pe, 1)
                    gate_op(dve.tensor_copy(flat(gcum[:]), side[:, 3, 0:HG * MT]))
                    gate_op(dve.tensor_tensor(kdiff[:], side[:, 3, HG * MT:HG * MT + HG], gcum[:, :, 0], ALU.subtract))
                if c == A_Q + 2:
                    dve.wait_ge(att_rs, 2)
                    dve.scalar_tensor_tensor(buf[0][:], pair_ps(1), cols_b[:, QG:QG + 1], buf[4],
                                             ALU.mult, ALU.mult).then_inc(att_qk, 1)
                    dve.wait_ge(att_qk, 2)
                    dve.engine_nop().then_inc(pair_free, 1)
                for kv in range(KV):
                    a = A_HEADS + A_STEPS * kv
                    sink = heads_bc[:, 2, 4 * kv:4 * kv + 4].rearrange("p (r a) -> p a r", a=2)
                    if c == a + 1:
                        dve.wait_ge(att_scores, kv + 1)
                        for u in range(4):
                            dve.tensor_tensor_reduce(p1[:, u], side[:, u // 2, (u % 2) * S:(u % 2 + 1) * S], band[:],
                                                     DA ** -0.5, LOWEST, ALU.add, ALU.max, mx[:, u:u + 1])
                            last = dve.tensor_tensor_reduce(p0[:, u], side[:, 2 + u // 2, (u % 2) * P:(u % 2 + 1) * P],
                                                            band[:, P:2 * P], DA ** -0.5, LOWEST, ALU.add, ALU.max,
                                                            mx[:, 4 + u:5 + u])
                        last.then_inc(att_sc, 1)
                    if c == a + 2:
                        dve.wait_ge(att_sc, kv + 1)
                        for m in range(MT):
                            last = dve.tensor_tensor(mxs[:, 4 * m:4 * m + 4].rearrange("p (a r) -> p a r", a=2),
                                                     mx[:, 4 * m:4 * m + 4].rearrange("p (a r) -> p a r", a=2),
                                                     sink, ALU.max)
                        last.then_inc(att_nm, 1)
                        dve.wait_ge(att_nm, 3 * kv + 1)
                        dve.tensor_scalar(nmx[:], mxs[:], -1.0, None, ALU.mult).then_inc(att_nm, 1)
                        dve.wait_ge(att_nm, 3 * kv + 2)
                        for m in range(MT):
                            last = dve.tensor_tensor(esi[:, 4 * m:4 * m + 4].rearrange("p (a r) -> p a r", a=2),
                                                     nmx[:, 4 * m:4 * m + 4].rearrange("p (a r) -> p a r", a=2),
                                                     sink, ALU.add)
                        last.then_inc(att_nm, 1)
                    if c == a + 3:
                        dve.wait_ge(att_exp, kv + 1)
                        dve.tensor_tensor(dsum[:], den[:], es[:], ALU.add).then_inc(att_den, 1)
                        dve.wait_ge(att_den, 2 * kv + 1)
                        dve.reciprocal(rden[:], dsum[:]).then_inc(att_den, 1)
                        dve.wait_ge(att_den, 2 * kv + 2)
                        dve.tensor_tensor(p1, p1, along(rden[:, 0:4], S), ALU.mult)
                        dve.tensor_tensor(p0, p0, along(rden[:, 4:8], P), ALU.mult).then_inc(att_p, 1)
                    if c == a + 5:
                        dve.wait_ge(att_pT, kv + 1)
                        dve.tensor_copy(half[1][:], side[:, 2]).then_inc(att_pT0, 1)
                if c == A_NORM + 1:
                    dve.wait_ge(att_rs, 3)
                    dve.tensor_tensor(flat(fm_b[:]), flat(fm_b[:]), buf[4], ALU.mult).then_inc(att_on, 1)
                if c == A_NORM + 2:
                    mixed(0, CT, fm_b, AO)
                for b in range(2, 8):
                    j = c - after(b)
                    if 1 <= j <= 3:
                        if j == 1:
                            dve.wait_ge(conv_first, b - 1)
                        else:
                            dve.wait_ge(conv_step, 3 * (b - 2) + j - 1)
                        dst = qkv[(b - 2) // 3][(b - 2) % 3]
                        for t in range(CT):
                            w = tap(b, 3 - j, t)
                            last = dve.scalar_tensor_tensor(dst[:, t, j:S], pair_ps(b % 2)[:, t * S:(t + 1) * S - j],
                                                            cols_a[:, w:w + 1], dst[:, t, j:S], ALU.mult, ALU.add)
                        last.then_inc(conv_step, 1)
                        if j == 3:
                            dve.wait_ge(conv_step, 3 * (b - 1))
                            dve.engine_nop().then_inc(pair_free, 1)
                for i in range(2):
                    gdn(i, c - GDN_START[i])
                if c == after(AT_CX) + 1:
                    dve.wait_ge(blk_turned, AT_CX + 1)
                    dve.wait_ge(cm_a, 1)
                    dve.tensor_tensor(flat(fm_a[:]), pair_ps(AT_CX % 2), flat(fm_a[:]), ALU.mult).then_inc(cm_prod, 1)
                    dve.wait_ge(cm_prod, 1)
                    dve.engine_nop().then_inc(pair_free, 1)
                for j in (1, 2):
                    if c == after(AT_CX) + 1 + j:
                        if j == 1:
                            dve.wait_ge(cm_first, 1)
                        else:
                            dve.wait_ge(cm_step, 1)
                        for t in range(CT):
                            w = CW + (2 - j) * CT + t
                            last = dve.scalar_tensor_tensor(fm_b[:, t, j:S], fm_a[:, t, 0:S - j], cols_b[:, w:w + 1],
                                                            fm_b[:, t, j:S], ALU.mult, ALU.add)
                        last.then_inc(cm_step, 1)
                if c == after(AT_CC) + 1:
                    dve.wait_ge(cm_a, 1)
                    dve.engine_nop().then_inc(pair_free, 1)
                if c == after(AT_CB) + 1:
                    dve.wait_ge(blk_turned, AT_CB + 1)
                    dve.wait_ge(cm_step, 2)
                    dve.tensor_tensor(flat(fm_b[:]), pair_ps(AT_CB % 2), flat(fm_b[:]), ALU.mult).then_inc(cm_out, 1)
                if c == after(AT_CB) + 4:
                    dve.wait_ge(cm_rs, 1)
                    dve.engine_nop().then_inc(pair_free, 1)
                    dve.tensor_tensor(flat(fm_b[:]), flat(fm_b[:]), flat(tok[:]), ALU.mult).then_inc(cm_on, 1)
                if c == after(AT_CB) + 5:
                    mixed(1, 0, fm_b, CO)
                for i in range(2):
                    b = AT_Z + i
                    if c == after(b) + 2:
                        dve.wait_ge(z_silu, i + 1)
                        dve.engine_nop().then_inc(pair_free, 1)
                        dve.wait_ge(gdn_on, i + 1)
                        dve.tensor_tensor(flat(fm_a[:]), flat(fm_a[:]), flat(qkv[i][1][:]), ALU.mult).then_inc(z_prod, 1)
                    if c == after(b) + 3:
                        mixed(2 + i, 2 * CT + CT * i, fm_a, None)

            def gdn(i, s):
                k_t, q_t, v_t = qkv[i]
                units = 2 * CT
                h = slice(4 * i, 4 * i + 4)
                if s == 2:
                    dve.wait_ge(gdn_rs, 2 * i + 1)
                    dve.tensor_tensor(flat(k_t[:]), flat(k_t[:]), buf[2][:], ALU.mult).then_inc(gdn_kn, 1)
                if s == 3:
                    dve.wait_ge(gdn_rs, 2 * i + 2)
                    dve.tensor_tensor(flat(q_t[:]), flat(q_t[:]), buf[3][:], ALU.mult).then_inc(gdn_qn, 1)
                    dve.wait_ge(gdn_eg, i + 1)
                    dve.tensor_tensor(tiles(buf[0][:], units), tiles(side_ps(0), units), over(upper_add[:], units),
                                      ALU.add).then_inc(gdn_rm, 1)
                if s == 4:
                    dve.wait_ge(gdn_brow, i + 1)
                    dve.wait_ge(gdn_kn, i + 1)
                    dve.wait_ge(gdn_qn, i + 1)
                    dve.tensor_tensor(buf[3][:], side_ps(1), flat(k_t[:]), ALU.mult).then_inc(gdn_kb, 1)
                if s == 5:
                    dve.wait_ge(gdn_vT, i + 1)
                    dve.tensor_tensor(tiles(buf[6], units), tiles(side_ps(0), units), along(flat(beta[:, h]), P),
                                      ALU.mult).then_inc(gdn_vb, 1)
                    dve.wait_ge(gdn_kb, i + 1)
                    dve.wait_ge(gdn_eg, i + 1)
                    kb = buf[3][:].rearrange("p (h m t) -> p h m t", h=CT, m=MT)[:, :, 1]
                    dve.tensor_tensor(tiles(half[1][:], CT), kb, tiles(half[0][:], CT), ALU.mult).then_inc(gdn_kbe, 1)
                    dve.tensor_tensor(tiles(half[2][:], CT), q_t[:, :, P:S], tiles(half[0][:], CT),
                                      ALU.mult).then_inc(gdn_kbe, 1)
                if s == 6:
                    dve.wait_ge(gdn_gram, i + 1)
                    dve.wait_ge(gdn_dec, i + 1)
                    dve.tensor_tensor(buf[4], side_ps(1), buf[0][:], ALU.mult).then_inc(gdn_AT, 1)
                if s == 7:
                    dve.wait_ge(gdn_qk, i + 1)
                    dve.tensor_tensor(buf[5], side_ps(0), buf[0][:], ALU.mult).then_inc(gdn_QKT, 1)
                if s == 8:
                    dve.wait_ge(gdn_ktok, i + 1)
                    dve.wait_ge(gate_act, 3)
                    dve.tensor_tensor(tiles(half[3][:], CT), tiles(side[:, 2], CT), along(kdecay[:, h], P),
                                      ALU.mult).then_inc(gdn_kdec, 1)
                for l in range(1, LEVELS):
                    if s == 9 + 2 * l:
                        dve.wait_ge(gdn_upd, 6 * i + l)
                        if l < LEVELS - 1:
                            if l == 1:
                                dve.wait_ge(gdn_M0, i + 1)
                            dve.tensor_tensor(buf[3][:], buf[3][:], side_ps(0), ALU.subtract).then_inc(gdn_M, 1)
                        dve.tensor_tensor(buf[7], buf[7], side_ps(1), ALU.subtract).then_inc(gdn_MTd, 1)
                if s == 23:
                    dve.wait_ge(gdn_Sps, i + 1)
                    dve.tensor_copy(half[5][:], side[:, 1]).then_inc(gdn_S, 1)
                    dve.tensor_copy(q_t[:, :, 0:P], tiles(side[:, 2], CT)).then_inc(gdn_o0, 1)
                if s == 24:
                    dve.wait_ge(gdn_kSps, i + 1)
                    vb = buf[6].rearrange("p (h m t) -> p h m t", h=CT, m=MT)[:, :, 1]
                    dve.tensor_tensor(tiles(half[0][:], CT), vb, tiles(side[:, 3], CT), ALU.subtract).then_inc(gdn_r1, 1)
                if s == 27:
                    dve.wait_ge(gdn_ors, i + 1)
                    dve.scalar_tensor_tensor(flat(q_t[:]), flat(q_t[:]), cols_b[:, GN:GN + 1], buf[2][:],
                                             ALU.mult, ALU.mult).then_inc(gdn_on, 1)

            dve.wait_ge(cols_turned, 1)
            dve.tensor_copy(cols_b[:, N1:N1 + KT], main[:, 0, 0, 0:KT]).then_inc(cols_ready, 1)
            lo_of(0)
            for j in range(NCB):
                piece(0, j)
                if 0 < j < AHEAD:
                    lo_of(j)
            for n in range(NCB):
                square(0, n)
            sum_of_squares(0)
            for c in range(C_LOOP):
                lo_of(c + AHEAD)
                side_work(c)

            def hidden_lo(value):
                dve.wait_ge(hid_hi, value)
                dve.tensor_tensor(mix_lo[:, 0:CT], fm_a[:], mix_hi[:, 0:CT].bitcast(F32),
                                  ALU.subtract).then_inc(hid_lo, 1)

            with dve.Fori(0, TURNS) as it:
                for s in range(PER):
                    lo(it * PER + (C_LOOP + s + AHEAD + 1), (s + AHEAD) % RING)
                    if s == 0:
                        hidden_lo(it + 1)
                    if s >= CPB and (s - CPB) % CPG == CPG - 1:
                        n = (s - CPB) // CPG
                        add_group(it * PER + (C_LOOP + s + 1), (G_MLP + n + 1) % 2, n)
            for c in range(C_LAST, CHUNKS):
                lo_of(c + AHEAD)
                if c == C_LAST:
                    hidden_lo(FB)
                if (c - C_LAST) % CPG == CPG - 1:
                    n = (c - C_LAST) // CPG
                    add_group(c + 1, (G_MLP + n + 1) % 2, n)

        @block.tensor
        def _(pe):
            def chunk(ready, slot, lhs, k, banks, n, first, last):
                hi_t, lo_t = lhs
                pe.wait_ge(lo_ready, ready)
                for j in range(KPC):
                    for m in range(MT):
                        a_hi = hi_t[:, k + j, m * P:(m + 1) * P]
                        a_lo = lo_t[:, k + j, m * P:(m + 1) * P]
                        w_h, w_l = w_hi[:, slot, j, 0:n], w_lo[:, slot, j, 0:n]
                        o = banks[:, m, 0:n]
                        end = last and j == KPC - 1
                        pe.matmul(o, a_hi, w_h, start=first and j == 0, stop=False)
                        pe.matmul(o, a_hi, w_l, start=False, stop=False)
                        ins = pe.matmul(o, a_lo, w_h, start=False, stop=end)
                ins.then_inc(chunk_done, 1)

            h_t, mix_t = (h_hi, h_lo), (mix_hi, mix_lo)

            def turn_piece(which, j):
                if which == 0:
                    pe.wait_ge(x_loaded[j], 16)
                    if j == 3:
                        pe.wait_ge(h_lo_ready, 1)
                else:
                    pe.wait_ge(group_added, G_MLP - NCB + j + 1)
                    if j > 0:
                        pe.wait_ge(h_lo_ready, NCB + j)
                ps = turn_ps(which, j)
                for t in range(CT):
                    for m in range(MT):
                        ins = pe.transpose(ps[:, t * S + m * P:t * S + (m + 1) * P],
                                           x_sb[:, m, (CT * j + t) * P:(CT * j + t + 1) * P], ident[:])
                ins.then_inc(h_turned, 1)

            def turn_block(b):
                pe.wait_ge(blk_copied, b + 1)
                ps = pair_ps(b % 2)
                if b == AT_KV:
                    for k in range(KV):
                        for m in range(MT):
                            ins = pe.transpose(ps[:, k * S + m * P:k * S + (m + 1) * P],
                                               tok[:, m, k * P:(k + 1) * P], ident[:])
                else:
                    for t in range(CT):
                        for m in range(MT):
                            ins = pe.transpose(ps[:, t * S + m * P:t * S + (m + 1) * P],
                                               tok[:, m, t * P:(t + 1) * P], ident[:])
                ins.then_inc(blk_turned, 1)

            def sums(ps, weights, src, n=2):
                for j in range(n):
                    ins = pe.matmul(ps[:, j * NB:(j + 1) * NB], weights[:], src[:, j * NB:(j + 1) * NB],
                                    start=True, stop=True)
                return ins

            def side_work(c):
                for b in range(NBLK):
                    if c == after(b):
                        turn_block(b)
                for n in range(NCB):
                    if c == C_LAST_QUAD + CPG * n + CPG:
                        turn_piece(1, n)
                if c == 2:
                    pe.wait_ge(h_lo_ready, 3)
                    pe.wait_ge(rows_loaded, 16 * 9)
                    pe.transpose(side[:, 3, 0:NROWS_B], rows_b[0:NROWS_B, :],
                                 ident[0:NROWS_B, 0:NROWS_B]).then_inc(cols_turned, 1)
                    pe.wait_ge(convw_loaded, 16)
                    pe.transpose(side[:, 3, P:P + 96], rows_a, ident[0:96, 0:96]).then_inc(cols_turned, 1)
                if c == A_KV + 1:
                    pe.wait_ge(att_sq, 1)
                    pe.wait_ge(const_step, N_CONST)
                    sums(side[:, 0], pair_ones, buf[4], 1).then_inc(att_sum, 1)
                if c == A_KV + 5:
                    pe.wait_ge(gate_dve, 12)
                    pe.matmul(side[:, 3, 0:HG * MT], upper[:], flat(gate[:]), start=True, stop=True)
                    pe.matmul(side[:, 3, HG * MT:HG * MT + HG], ones[:], gate[:, :, 0],
                              start=True, stop=True).then_inc(gate_pe, 1)
                if c == A_Q + 1:
                    pe.wait_ge(att_sq, 2)
                    pe.wait_ge(att_rs, 1)
                    sums(side_ps(0), pair_ones, buf[4]).then_inc(att_sum, 1)
                for kv in range(KV):
                    a = A_HEADS + A_STEPS * kv
                    q_fm = tiles(buf[0][:], CT)
                    if c == a:
                        pe.wait_ge(att_qk, 2)
                        if kv == 0:
                            pe.wait_ge(gate_dve, 14)
                        else:
                            pe.wait_ge(att_oe, kv)
                        for u in range(4):
                            par, pr = u // 2, u % 2
                            rows = slice(par * DA, (par + 1) * DA)
                            q_h = q_fm[rows, 2 * kv + pr]
                            pe.matmul(side[:, par, pr * S:(pr + 1) * S], q_h[:, P:S],
                                      att_k[rows, kv * S:(kv + 1) * S], start=True, stop=True)
                            ins = pe.matmul(side[:, 2 + par, pr * P:(pr + 1) * P], q_h[:, 0:P],
                                            att_k[rows, kv * S:kv * S + P], start=True, stop=True)
                        ins.then_inc(att_scores, 1)
                    if c == a + 4:
                        pe.wait_ge(att_p, kv + 1)
                        for u in range(4):
                            for kt in range(2):
                                pe.transpose(side[:, kt, u * P:(u + 1) * P], p1[:, u, kt * P:(kt + 1) * P], ident[:])
                            ins = pe.transpose(side[:, 2, u * P:(u + 1) * P], p0[:, u], ident[:])
                        ins.then_inc(att_pT, 1)
                    if c == a + 5:
                        pe.wait_ge(att_pT1, kv + 1)
                        pe.wait_ge(att_pT0, kv + 1)
                        pt1 = buf[3][:].rearrange("p (k u q) -> p k u q", k=2, u=4)
                        pt0 = tiles(half[1][:], 4)
                        for par in range(2):
                            o = side[par * DA:(par + 1) * DA, 3]
                            two = slice(2 * par, 2 * par + 2)
                            v_h = vals[:, :, kv * DA:(kv + 1) * DA]
                            pe.matmul(o[:, 0:S], v_h[:, 0], pt0[:, two], start=True, stop=True)
                            pe.matmul(o[:, S:2 * S], v_h[:, 0], pt1[:, 0, two], start=True, stop=False)
                            ins = pe.matmul(o[:, S:2 * S], v_h[:, 1], pt1[:, 1, two], start=False, stop=True)
                        ins.then_inc(att_o, 1)
                if c == A_NORM:
                    pe.wait_ge(att_sq, 3)
                    sums(side_ps(0), pair_ones, buf[4]).then_inc(att_sum, 1)
                for i in range(2):
                    gdn(i, c - GDN_START[i])
                if c == after(AT_CB) + 2:
                    pe.wait_ge(cm_sq, 1)
                    sums(pair_ps(AT_CB % 2), ones, flat(tok[:])).then_inc(cm_sum, 1)

            def gdn(i, s):
                k_t, q_t, v_t = qkv[i]
                units = [(h, m) for h in range(CT) for m in range(MT)]

                def unit(t, h, m):
                    return t[:, (2 * h + m) * P:(2 * h + m + 1) * P]

                def head(t, h):
                    return t[:, h * P:(h + 1) * P]

                if s == 0:
                    pe.wait_ge(gdn_sq, 2 * i + 1)
                    sums(side_ps(0), ones, buf[2]).then_inc(gdn_sum, 1)
                    pe.wait_ge(gdn_sq, 2 * i + 2)
                    sums(side_ps(1), ones, buf[3]).then_inc(gdn_sum, 1)
                if s == 2:
                    pe.wait_ge(gdn_rows, i + 1)
                    pe.wait_ge(gdn_ln, 2 * i + 1)
                    sums(side_ps(0), ones, buf[0]).then_inc(gdn_grow, 1)
                if s == 3:
                    pe.wait_ge(gdn_ln, 2 * i + 2)
                    sums(side_ps(1), ones, buf[1]).then_inc(gdn_brow, 1)
                if s == 4:
                    pe.wait_ge(gdn_rm, i + 1)
                    pe.wait_ge(gdn_eg, i + 1)
                    for h, m in units:
                        ins = pe.transpose(unit(side_ps(0), h, m), v_t[:, h, m * P:(m + 1) * P], ident[:])
                    ins.then_inc(gdn_vT, 1)
                if s == 5:
                    pe.wait_ge(gdn_kb, i + 1)
                    for h, m in units:
                        ins = pe.matmul(unit(side_ps(1), h, m), k_t[:, h, m * P:(m + 1) * P],
                                        unit(buf[3], h, m), start=True, stop=True)
                    ins.then_inc(gdn_gram, 1)
                if s == 6:
                    pe.wait_ge(gdn_vb, i + 1)
                    pe.wait_ge(gdn_qn, i + 1)
                    for h, m in units:
                        ins = pe.matmul(unit(side_ps(0), h, m), k_t[:, h, m * P:(m + 1) * P],
                                        q_t[:, h, m * P:(m + 1) * P], start=True, stop=True)
                    ins.then_inc(gdn_qk, 1)
                if s == 7:
                    pe.wait_ge(gdn_AT, i + 1)
                    for h in range(CT):
                        ins = pe.transpose(head(side[:, 2], h), k_t[:, h, 0:P], ident[:])
                    ins.then_inc(gdn_ktok, 1)
                if s == 8:
                    pe.wait_ge(gdn_MT0, i + 1)
                    pe.wait_ge(gdn_QKT, i + 1)
                    for h, m in units:
                        ins = pe.transpose(unit(side_ps(0), h, m), unit(buf[7], h, m), ident[:])
                    ins.then_inc(gdn_Mps, 1)
                for l in range(1, LEVELS):
                    if s == 7 + 2 * l:
                        if l == 1:
                            pe.wait_ge(gdn_M0, i + 1)
                            pe.wait_ge(gdn_kdec, i + 1)
                        else:
                            pe.wait_ge(gdn_M, 5 * i + l - 1)
                            pe.wait_ge(gdn_MTd, 6 * i + l - 1)
                        pe.wait_ge(gdn_Al, 6 * i + l)
                        for h, m in units:
                            ins = pe.matmul(unit(side_ps(1), h, m), unit(buf[l % 2], h, m), unit(buf[3], h, m),
                                            start=True, stop=True)
                        ins.then_inc(gdn_Y, 1)
                    if s == 8 + 2 * l:
                        pe.wait_ge(gdn_Ysb, 6 * i + l)
                        if l < LEVELS - 1:
                            for h, m in units:
                                pe.matmul(unit(side_ps(0), h, m), unit(buf[7], h, m), unit(buf[2], h, m),
                                          start=True, stop=True)
                        for h, m in units:
                            ins = pe.matmul(unit(side_ps(1), h, m), unit(buf[2], h, m), unit(buf[7], h, m),
                                            start=True, stop=True)
                        ins.then_inc(gdn_upd, 1)
                if s == 21:
                    pe.wait_ge(gdn_MTd, 6 * (i + 1))
                    for h in range(CT):
                        ins = pe.matmul(head(side[:, 0], h), unit(buf[7], h, 0), unit(buf[6], h, 0),
                                        start=True, stop=True)
                    ins.then_inc(gdn_v0ps, 1)
                if s == 22:
                    pe.wait_ge(gdn_v0, i + 1)
                    for h in range(CT):
                        pe.matmul(head(side[:, 1], h), head(half[3], h), head(half[4], h), start=True, stop=True)
                    for h in range(CT):
                        ins = pe.matmul(head(side[:, 2], h), head(half[4], h), unit(buf[5], h, 0),
                                        start=True, stop=True)
                    ins.then_inc(gdn_Sps, 1)
                if s == 23:
                    pe.wait_ge(gdn_S, i + 1)
                    for h in range(CT):
                        ins = pe.matmul(head(side[:, 3], h), head(half[1], h), head(half[5], h),
                                        start=True, stop=True)
                    ins.then_inc(gdn_kSps, 1)
                if s == 24:
                    pe.wait_ge(gdn_r1, i + 1)
                    for h in range(CT):
                        ins = pe.matmul(head(side[:, 0], h), unit(buf[7], h, 1), head(half[0], h),
                                        start=True, stop=True)
                    ins.then_inc(gdn_v1ps, 1)
                if s == 25:
                    pe.wait_ge(gdn_v1, i + 1)
                    for h in range(CT):
                        pe.matmul(head(side[:, 1], h), head(half[5], h), head(half[2], h), start=True, stop=False)
                        ins = pe.matmul(head(side[:, 1], h), head(half[4], h), unit(buf[5], h, 1),
                                        start=False, stop=True)
                    ins.then_inc(gdn_o1ps, 1)
                if s == 26:
                    pe.wait_ge(gdn_osq, i + 1)
                    sums(side_ps(1), ones, buf[2]).then_inc(gdn_osum, 1)

            pe.wait_ge(const_step, 2)
            pe.wait_ge(norm1_loaded, 16)
            pe.transpose(main[:, 0, 0, 0:KT], rows_n, ident[0:KT, 0:KT]).then_inc(cols_turned, 1)
            for j in range(NCB):
                turn_piece(0, j)
            pe.wait_ge(cols_ready, 1)
            for c in range(C_OUT):
                b, k = c // CPB, c % CPB
                if k == 0 and b >= 2:
                    pe.wait_ge(pair_free, b - 1)
                if b == 0:
                    pe.wait_ge(h_lo_ready, k * KPC // CT + 1)
                n = KVW + BA if b == AT_KV else NB
                chunk(c + 1, c % RING, h_t, k * KPC, main[:, b % 2], n, k == 0, k == CPB - 1)
                side_work(c)
            for c in range(C_OUT, C_MLP):
                g, k = (c - C_OUT) // CPG, (c - C_OUT) % CPG
                if k == 0:
                    if g < 2:
                        pe.wait_ge(pair_free, NBLK - 1 + g)
                    else:
                        pe.wait_ge(group_added, g - 1)
                    if g % NCB == 0:
                        pe.wait_ge(mix_lo_ready, g // NCB + 1)
                chunk(c + 1, c % RING, mix_t, QUADS[g // NCB] * CT + k * KPC, main[:, (g + 1) % 2], NB,
                      k == 0, k == CPG - 1)
                side_work(c)
            def turn_hidden(value):
                pe.wait_ge(hid_relu, value)
                for t in range(CT):
                    for m in range(MT):
                        ins = pe.transpose(side_ps(1)[:, t * S + m * P:t * S + (m + 1) * P],
                                           tok[:, m, t * P:(t + 1) * P], ident[:])
                ins.then_inc(hid_turned, 1)

            for k in range(CPB):
                pe.wait_ge(h_lo_ready, NCB + k * KPC // CT + 1)
                chunk(C_MLP + k + 1, (C_MLP + k) % RING, h_t, k * KPC, side[:, 0:2], NB, k == 0, k == CPB - 1)
                side_work(C_MLP + k)
            turn_hidden(1)
            with pe.Fori(0, TURNS) as it:
                pe.wait_ge(hid_relu, it + 1)
                for s in range(CPB):
                    chunk(it * PER + (C_LOOP + s + 1), s % RING, h_t, s * KPC, side[:, 0:2], NB,
                          s == 0, s == CPB - 1)
                pe.wait_ge(hid_lo, it + 1)
                for s in range(CPB, PER):
                    n, k = (s - CPB) // CPG, (s - CPB) % CPG
                    if k == 0:
                        pe.wait_ge(group_added, it * NCB + (G_MLP + n - 1))
                    chunk(it * PER + (C_LOOP + s + 1), s % RING, mix_t, k * KPC, main[:, (G_MLP + n + 1) % 2], NB,
                          k == 0, k == CPG - 1)
                turn_hidden(it + 2)
            pe.wait_ge(hid_lo, FB)
            for c in range(C_LAST, CHUNKS):
                n, k = (c - C_LAST) // CPG, (c - C_LAST) % CPG
                if k == 0:
                    pe.wait_ge(group_added, G_MLP + NCB * (FB - 1) + n - 1)
                chunk(c + 1, c % RING, mix_t, k * KPC, main[:, (G_MLP + n + 1) % 2], NB, k == 0, k == CPG - 1)


_INS = ["x", "norm1_g", "w_in", "conv_w", "conv_out_g", "q_norm_g", "k_norm_g", "attn_sinks", "attn_out_g",
        "gdn_conv_w", "gdn_A_log", "gdn_dt_bias", "gdn_norm_g", "w_out", "norm2_g", "w_up", "w_down"]


def kernel(**inputs):
    import numpy as np
    import concourse.bacc as bacc
    from concourse.bass_utils import run_bass_kernel_spmd

    nc = bacc.Bacc("TRN2", target_bir_lowering=False, num_devices=1)
    arrays, args = {}, []
    for name in _INS:
        a = np.ascontiguousarray(inputs[name])
        arrays[f"in_{name}"] = a
        args.append(nc.dram_tensor(f"in_{name}", a.shape, mybir.dt.from_np(a.dtype), kind="ExternalInput").ap())
    args.append(nc.dram_tensor("out_0", inputs["x"].shape, F32, kind="ExternalOutput").ap())
    build(nc, *args)
    r = run_bass_kernel_spmd(nc, [arrays], core_ids=[0])
    return r.results[0]["out_0"]
```

```python
from contextlib import ExitStack
from math import log

import concourse.bass as bass
from concourse import mybir

F32 = mybir.dt.float32
F32R = mybir.dt.float32r
ALU = mybir.AluOpType
ACT = mybir.ActivationFunctionType
AX_X = mybir.AxisListType.X

P = 128
EPS = 1e-6
NEG = -1e30
LOWEST = -3e38
LN_EXP = "natural_log_exp_and_others"
SILU = "silu_and_others"


def build(nc, x, norm1_g, w_in, conv_w, conv_out_g, q_norm_g, k_norm_g, attn_sinks, attn_out_g,
          gdn_conv_w, gdn_A_log, gdn_dt_bias, gdn_norm_g, w_out, norm2_g, w_up, w_down, out):
    S, D = x.shape[1], x.shape[2]
    FF = w_up.shape[2]
    MT = S // P
    KT = D // P
    NB = 512
    CT = NB // P
    KPC = 2
    CPB = KT // KPC
    RING = 4
    AHEAD = 3
    assert S == 256 and D == 2048 and FF % NB == 0 and MT == 2

    CONV_W = D // 4
    HA, DA = attn_sinks.shape[1], q_norm_g.shape[1]
    KV = 2
    HG, DG = gdn_A_log.shape[1], gdn_norm_g.shape[1]
    GDN_W = HG * DG
    assert DG == P and 2 * DA == P and HG == 8 and HA == 8 and CONV_W == NB and HA * DA == NB

    AT_Q = 3 * CONV_W
    AT_K = AT_Q + HA * DA
    KVW = 2 * KV * DA
    GD_Q = AT_K + KVW
    GD_K, GD_V, GD_Z = GD_Q + GDN_W, GD_Q + 2 * GDN_W, GD_Q + 3 * GDN_W
    GD_B = GD_Q + 4 * GDN_W
    BA = 2 * HG
    BLOCKS = [("kv", AT_K), ("aq", AT_Q),
              ("gk", GD_K), ("gq", GD_Q), ("gv", GD_V),
              ("gk", GD_K + NB), ("gq", GD_Q + NB), ("gv", GD_V + NB),
              ("cc", CONV_W), ("cx", 2 * CONV_W), ("cb", 0),
              ("gz", GD_Z), ("gz", GD_Z + NB)]
    NBLK = len(BLOCKS)
    AT_KV, AT_AQ, AT_CC, AT_CX, AT_CB, AT_Z = 0, 1, 8, 9, 10, 11
    QUADS = [1, 0, 2, 3]
    CPG = CT // KPC
    NCB = D // NB
    C_OUT = NBLK * CPB
    C_MLP = C_OUT + len(QUADS) * NCB * CPG
    C_LAST_QUAD = C_MLP - NCB * CPG
    FB = FF // NB
    C_LOOP = C_MLP + CPB
    PER = CPB + NCB * CPG
    TURNS = FB - 1
    C_LAST = C_LOOP + PER * TURNS
    CHUNKS = C_LAST + NCB * CPG
    G_MLP = len(QUADS) * NCB
    assert PER % RING == 0 and C_LOOP % RING == 0

    A_KV = CPB + 1
    A_Q = 2 * CPB
    A_HEADS = A_Q + 3
    A_STEPS = 8
    A_NORM = A_HEADS + KV * A_STEPS
    GDN_START = [5 * CPB + 6, 5 * CPB + 6 + 28]
    SILU_AT = [5 * CPB + 2, 8 * CPB + 2]
    LEVELS = 7
    HP = P // 2

    def after(b):
        return CPB * (b + 1)

    with ExitStack() as ctx:
        def sb(name, shape, dt=F32):
            return ctx.enter_context(nc.sbuf_tensor(name, shape, dt))

        def sem(name):
            return ctx.enter_context(nc.semaphore(name))

        raw = sb("raw", [P, RING, KPC, NB])
        w_hi = sb("w_hi", [P, RING, KPC, NB], F32R)
        w_lo = sb("w_lo", [P, RING, KPC, NB], F32R)
        x_sb = sb("x_sb", [P, MT, D])
        h_hi = sb("h_hi", [P, KT, S], F32R)
        h_lo = sb("h_lo", [P, KT, S], F32R)
        mix_hi = sb("mix_hi", [P, KT, S], F32R)
        mix_lo = sb("mix_lo", [P, KT, S], F32R)
        qkv = [[sb(f"gdn_{n}{b}", [P, CT, S]) for n in "kqv"] for b in range(2)]
        tok = sb("tok", [P, MT, NB])
        fm_a = sb("fm_a", [P, CT, S])
        fm_b = sb("fm_b", [P, CT, S])
        buf = [sb(f"buf{i}", [P, 2 * NB]) for i in range(4)]
        buf += [x_sb[:, i // 2, (i % 2) * 2 * NB:(i % 2 + 1) * 2 * NB] for i in range(4)]
        half = [sb(f"half{i}", [P, NB]) for i in range(6)]

        ident = sb("ident", [P, P])
        ones = sb("ones", [P, P])
        ones_r = sb("ones_r", [P, P], F32R)
        pair_ones_r = sb("pair_ones_r", [P, P], F32R)
        upper = sb("upper", [P, P])
        pair_ones = sb("pair_ones", [P, P])
        upper_add = sb("upper_add", [P, P])
        band = sb("band", [P, 2 * P])
        level = sb("level", [P, LEVELS - 1, P])
        eps_col = sb("eps_col", [P, 1])
        q_scale = sb("q_scale", [P, 1])

        rows_a = half[0][0:96, 0:P]
        rows_b = half[0][0:56, P:2 * P]
        rows_n = half[0][0:KT, 2 * P:3 * P]
        cols_a = sb("cols_a", [P, 96])
        cols_b = sb("cols_b", [P, 56])
        heads_bc = sb("heads_bc", [P, 3, HG])
        ss = sb("ss", [P, MT, NCB])
        ssum = sb("ssum", [P, MT])
        rstd = sb("rstd", [P, MT])
        ba = sb("ba", [P, MT, BA])
        sc = [sb(f"sc{i}", [P, HG, MT]) for i in range(12)]
        e_alog = sb("e_alog", [P, HG])
        beta = sb("beta", [P, HG, MT])
        gate = sb("gate", [P, HG, MT])
        gcum = sb("gcum", [P, HG, MT])
        kdecay = sb("kdecay", [P, HG])
        kdiff = sb("kdiff", [P, HG])
        mx, mxs, nmx, esi, es, den, dsum, rden = (sb(n, [P, 8]) for n in (
            "mx", "mxs", "nmx", "esi", "es", "den", "dsum", "rden"))

        main = ctx.enter_context(nc.psum_tensor("main", [P, 2, MT, NB], F32))
        side = ctx.enter_context(nc.psum_tensor("side", [P, 4, NB], F32))

        N1, N2, CW, CO, AO, GN, QG, KG = KT + 23, 0, KT, KT + 12, KT + 16, KT + 20, KT + 21, KT + 22
        NROWS_B = KG + 1
        GC_TILES = 3 * GDN_W // P

        raw_loaded = [sem(f"raw_loaded{i}") for i in range(RING)]
        hi_ready, lo_ready, chunk_done = sem("hi_ready"), sem("lo_ready"), sem("chunk_done")
        x_loaded = [sem(f"x_loaded{i}") for i in range(NCB)]
        x_back, out_stored = sem("x_back"), sem("out_stored")
        rows_loaded, convw_loaded, heads_loaded = sem("rows_loaded"), sem("convw_loaded"), sem("heads_loaded")
        norm1_loaded = sem("norm1_loaded")
        const_step = sem("const_step")
        cols_turned, cols_ready = sem("cols_turned"), sem("cols_ready")
        ss_act, ss_dve, ssum_ready, rstd_ln, rstd_ready = (sem(n) for n in (
            "ss_act", "ss_dve", "ssum_ready", "rstd_ln", "rstd_ready"))
        h_turned, h_hi_ready, h_lo_ready = (sem(n) for n in ("h_turned", "h_hi_ready", "h_lo_ready"))
        blk_copied, blk_turned, pair_free, group_added = (sem(n) for n in (
            "blk_copied", "blk_turned", "pair_free", "group_added"))
        conv_first, conv_step, silu_done = sem("conv_first"), sem("conv_step"), sem("silu_done")
        gate_dve, gate_act, gate_pe = sem("gate_dve"), sem("gate_act"), sem("gate_pe")
        att_sq, att_sum, att_ln, att_rs, att_qk = (sem(n) for n in (
            "att_sq", "att_sum", "att_ln", "att_rs", "att_qk"))
        att_scores, att_sc, att_nm, att_exp, att_den, att_p = (sem(n) for n in (
            "att_scores", "att_sc", "att_nm", "att_exp", "att_den", "att_p"))
        att_pT, att_pT1, att_pT0, att_o, att_oe, att_on = (sem(n) for n in (
            "att_pT", "att_pT1", "att_pT0", "att_o", "att_oe", "att_on"))
        cm_a, cm_prod, cm_first, cm_step, cm_out, cm_sq, cm_sum, cm_ln, cm_rs, cm_on = (sem(n) for n in (
            "cm_a", "cm_prod", "cm_first", "cm_step", "cm_out", "cm_sq", "cm_sum", "cm_ln", "cm_rs", "cm_on"))
        z_silu, z_prod = sem("z_silu"), sem("z_prod")
        ones_ready = sem("ones_ready")
        att_full, att_lo, cm_sqhi, cm_sqlo = (sem(n) for n in ("att_full", "att_lo", "cm_sqhi", "cm_sqlo"))
        mix_hi_ready, mix_lo_ready = sem("mix_hi_ready"), sem("mix_lo_ready")
        (gdn_sq, gdn_sqhi, gdn_sqlo, gdn_sum, gdn_ln, gdn_rs, gdn_kn, gdn_qn, gdn_grow, gdn_brow, gdn_rm, gdn_rm2,
         gdn_eg, gdn_dec, gdn_kb, gdn_vT, gdn_vb, gdn_kbe, gdn_gram, gdn_qk, gdn_AT, gdn_QKT, gdn_ktok,
         gdn_kdec, gdn_tmp, gdn_MT0, gdn_Mps, gdn_M0, gdn_Al, gdn_Y, gdn_Ysb, gdn_upd, gdn_M, gdn_MTps, gdn_MT, gdn_MTlast,
         gdn_v0ps, gdn_v0, gdn_Sps, gdn_S, gdn_o0, gdn_kSps, gdn_r1, gdn_v1ps, gdn_v1, gdn_o1ps, gdn_o1,
         gdn_osq, gdn_osqhi, gdn_osqlo, gdn_osum, gdn_oln, gdn_ors, gdn_on) = (sem("gdn_" + n) for n in (
            "sq", "sqhi", "sqlo", "sum", "ln", "rs", "kn", "qn", "grow", "brow", "rm", "rm2",
            "eg", "dec", "kb", "vT", "vb", "kbe", "gram", "qk", "AT", "QKT", "ktok",
            "kdec", "tmp", "MT0", "Mps", "M0", "Al", "Y", "Ysb", "upd", "M", "MTps", "MT", "MTlast",
            "v0ps", "v0", "Sps", "S", "o0", "kSps", "r1", "v1ps", "v1", "o1ps", "o1",
            "osq", "osqhi", "osqlo", "osum", "oln", "ors", "on"))
        hid_relu, hid_turned, hid_sq, hid_hi, hid_lo = (sem(n) for n in (
            "hid_relu", "hid_turned", "hid_sq", "hid_hi", "hid_lo"))

        x_dram = x.rearrange("o (m p) d -> (o p) m d", p=P)
        out_dram = out.rearrange("o (m p) d -> (o p) m d", p=P)
        win_v = w_in.rearrange("o (t p) n -> (o p) t n", p=P)
        wout_v = w_out.rearrange("o (t p) n -> (o p) t n", p=P)
        wup_v = w_up.rearrange("o (t p) n -> (o p) t n", p=P)
        wdn_v = w_down.rearrange("o (t p) n -> (o p) t n", p=P)

        def flat(t):
            return t.rearrange("p a b -> p (a b)")

        def pair_ps(i):
            return main[:, i].rearrange("p m n -> p (m n)")

        def side_ps(i):
            return side[:, 2 * i:2 * i + 2].rearrange("p m n -> p (m n)")

        def tiles(t, n):
            return t.rearrange("p (a b) -> p a b", a=n)

        def over(t, n):
            return t.unsqueeze(1).to_broadcast([P, n, t.shape[1]])

        def along(t, w):
            return t.unsqueeze(2).to_broadcast([P, t.shape[1], w])

        att_k = buf[1][:, 0:NB]
        vals = tiles(buf[1][:, NB:NB + MT * KV * DA], MT)
        p1 = tiles(buf[2][:], 4)
        p0 = tiles(half[0][:], 4)

        def turn_ps(which, j):
            if which == 0:
                return (side_ps(0), pair_ps(1), side_ps(1), side_ps(0))[j]
            return (side_ps(1), side_ps(0), side_ps(1), side_ps(1))[j]

        def turn_slot(n):
            return C_LAST_QUAD + CPG * n + CPG + (1 if n < NCB - 1 else 2)

        def sq_parts(quad):
            quad_tiles = slice(CT * quad, CT * (quad + 1))
            return flat(mix_hi[:, quad_tiles]), flat(mix_lo[:, quad_tiles])

        def block_ps(b):
            return side_ps(0) if b == NBLK - 1 else pair_ps(b % 2)

        def tap(b, k, t):
            first = {"gq": 0, "gk": HG, "gv": 2 * HG}[BLOCKS[b][0]]
            return k * GC_TILES + first + CT * ((b - 2) // 3) + t

        def raw_value(c):
            return 16 * (c // RING + 1) + 16 * min(c // RING + 1, CPB // RING)

        block = ctx.enter_context(nc.Block())

        @block.sync
        def _(sp):
            def load(c, slot, src):
                if c is not None:
                    sp.wait_ge(lo_ready, c)
                sp.dma_start(raw[:, slot], src).then_inc(raw_loaded[slot], 16)

            for c in range(C_OUT):
                b, k = c // CPB, c % CPB
                kind, col = BLOCKS[b]
                rows = slice(KPC * k, KPC * (k + 1))
                if c < NCB:
                    sp.dma_start(x_sb[:, :, c * NB:(c + 1) * NB],
                                 x_dram[:, :, c * NB:(c + 1) * NB]).then_inc(x_loaded[c], 16)
                free = c - RING + 1 if c >= RING else None
                if kind == "kv":
                    if free is not None:
                        sp.wait_ge(lo_ready, free)
                    sp.dma_start(raw[:, c % RING, :, 0:KVW],
                                 win_v[:, rows, col:col + KVW]).then_inc(raw_loaded[c % RING], 16)
                    sp.dma_start(raw[:, c % RING, :, KVW:KVW + BA],
                                 win_v[:, rows, GD_B:GD_B + BA]).then_inc(raw_loaded[c % RING], 16)
                else:
                    load(free, c % RING, win_v[:, rows, col:col + NB])
            for c in range(C_OUT, C_MLP):
                g, k = (c - C_OUT) // CPG, (c - C_OUT) % CPG
                t = QUADS[g // NCB] * CT + k * KPC
                n = g % NCB
                load(c - RING + 1, c % RING, wout_v[:, t:t + KPC, n * NB:(n + 1) * NB])
            for c in range(C_MLP, C_LOOP):
                k = c - C_MLP
                load(c - RING + 1, c % RING, wup_v[:, KPC * k:KPC * (k + 1), 0:NB])
            with sp.Fori(0, TURNS) as it:
                for s in range(PER):
                    free = it * PER + (C_LOOP + s - RING + 1)
                    if s < CPB:
                        src = wup_v[:, KPC * s:KPC * (s + 1), bass.ds(it * NB + NB, NB)]
                    else:
                        n, k = (s - CPB) // CPG, (s - CPB) % CPG
                        src = wdn_v[:, bass.ds(it * CT + k * KPC, KPC), n * NB:(n + 1) * NB]
                    load(free, s % RING, src)
            for c in range(C_LAST, CHUNKS):
                n, k = (c - C_LAST) // CPG, (c - C_LAST) % CPG
                t = (FB - 1) * CT + k * KPC
                load(c - RING + 1, c % RING, wdn_v[:, t:t + KPC, n * NB:(n + 1) * NB])
            for n in range(NCB - 1):
                sp.wait_ge(group_added, G_MLP + NCB * (FB - 1) + n + 1)
                sp.dma_start(out_dram[:, :, n * NB:(n + 1) * NB],
                             x_sb[:, :, n * NB:(n + 1) * NB]).then_inc(out_stored, 16)
            for m in range(MT):
                sp.wait_ge(group_added, G_MLP + NCB * FB + m)
                sp.dma_start(out_dram[:, m, D - NB:D], x_sb[:, m, D - NB:D]).then_inc(out_stored, 16)
            sp.wait_ge(out_stored, 16 * (NCB - 1 + MT))

        N_CONST = 16 + 3 * (LEVELS - 1)

        @block.gpsimd
        def _(pool):
            steps = [0]

            def step(ins):
                steps[0] += 1
                ins.then_inc(const_step, 1)
                pool.wait_ge(const_step, steps[0])

            def where(t, base, pattern, mult, fill, op=ALU.is_ge):
                step(pool.affine_select(out=t, in_=t, compare_op=op, fill=fill, base=base,
                                        pattern=pattern, channel_multiplier=mult))

            step(pool.memset(ident[:], 1.0))
            where(ident[:], 0, [[-1, P]], 1, 0.0, ALU.is_equal)
            step(pool.memset(eps_col[:], EPS))
            for row, v in ((N2, norm2_g), (CO, conv_out_g), (AO, attn_out_g), (GN, gdn_norm_g)):
                n = v.shape[1] // P
                pool.dma_start(rows_b[row:row + n, :], v.rearrange("o (t n) -> (o t) n", n=P)).then_inc(rows_loaded, 16)
            pool.dma_start(rows_b[CW:CW + 3 * CT, :],
                           conv_w.rearrange("o k (t n) -> (o k t) n", n=P)).then_inc(rows_loaded, 16)
            for row, v in ((QG, q_norm_g), (KG, k_norm_g)):
                for j in range(2):
                    pool.dma_start(rows_b[row:row + 1, j * DA:(j + 1) * DA], v).then_inc(rows_loaded, 16)
            pool.dma_start(rows_a, gdn_conv_w.rearrange("o k (t n) -> (o k t) n", n=P)).then_inc(convw_loaded, 16)
            for i, v in enumerate((gdn_A_log, gdn_dt_bias, attn_sinks)):
                pool.dma_start(heads_bc[:, i], v[0].partition_broadcast(P)).then_inc(heads_loaded, 16)
            step(pool.memset(q_scale[:], -0.5 * log(DG)))
            step(pool.memset(ones[:], 1.0))
            step(pool.memset(upper[:], 1.0))
            where(upper[:], 0, [[1, P]], -1, 0.0)
            step(pool.memset(upper_add[:], 0.0))
            where(upper_add[:], 0, [[1, P]], -1, NEG)
            step(pool.memset(pair_ones[:], 0.0))
            step(pool.memset(pair_ones[0:DA, 0:DA], 1.0))
            step(pool.memset(pair_ones[DA:P, DA:P], 1.0))
            step(pool.memset(band[:], 0.0))
            where(band[:, 0:P], -1, [[1, P]], -1, NEG)
            where(band[:, P:2 * P], 0, [[-1, P]], 1, NEG)
            step(pool.memset(level[:], 0.0))
            for l in range(LEVELS - 1):
                w = 2 ** l
                blocks = level[:, l].rearrange("p (n h w) -> p n h w", h=2, w=w)
                step(pool.memset(blocks[:, :, 1, :], 1.0))
                n = P // (2 * w)
                upper_half = blocks[:, :, 1, :]
                where(upper_half, 0, [[-2 * w, n], [0, w]], 1, 0.0)
                where(upper_half, w - 1, [[2 * w, n], [0, w]], -1, 0.0)

            def square_of(dst, src, out_sem):
                pool.tensor_tensor(dst, src, src, ALU.mult).then_inc(out_sem, 1)

            def squares_of_keys_and_queries(b):
                if b == 0:
                    pool.wait_ge(att_on, 1)
                    pool.wait_ge(att_scores, KV)
                else:
                    pool.wait_ge(gdn_Y, 6 * b)
                for n in range(2):
                    pool.wait_ge(silu_done, 3 * b + n + 1)
                    square_of((buf[4], buf[0][:])[n], flat(qkv[b][n][:]), gdn_sq)

            pool.wait_ge(att_oe, KV)
            square_of(buf[5], flat(fm_b[:]), att_full)
            squares_of_keys_and_queries(0)

            for b in range(2):
                h = slice(4 * b, 4 * b + 4)
                units = 2 * CT
                pool.wait_ge(gate_dve, 13)
                if b == 0:
                    pool.wait_ge(att_scores, KV)
                    pool.wait_ge(att_o, KV)
                else:
                    pool.wait_ge(gdn_Y, 6 * b)
                pool.wait_ge(gdn_rm, b + 1)
                pool.tensor_tensor(tiles(buf[0][:], units), tiles(buf[0][:], units),
                                   along(flat(gcum[:, h]), P), ALU.subtract).then_inc(gdn_rm2, 1)
                pool.wait_ge(gdn_AT, b + 1)
                pool.tensor_tensor(tiles(buf[1][:], units), tiles(buf[4], units),
                                   over(level[:, 0], units), ALU.mult).then_inc(gdn_tmp, 1)
                pool.wait_ge(gdn_tmp, b + 1)
                pool.tensor_tensor(tiles(buf[7], units), over(ident[:], units),
                                   tiles(buf[1][:], units), ALU.subtract).then_inc(gdn_MT0, 1)
                for l in range(1, LEVELS - 1):
                    if l == 1:
                        pool.wait_ge(gdn_MT0, b + 1)
                    elif l == 2:
                        pool.wait_ge(gdn_QKT, b + 1)
                    else:
                        pool.wait_ge(gdn_Y, 6 * b + l - 2)
                    pool.tensor_tensor(tiles(buf[l % 2][:], units), tiles(buf[4], units),
                                       over(level[:, l], units), ALU.mult).then_inc(gdn_Al, 1)
                if b == 1:
                    pool.wait_ge(cm_out, 1)
                    square_of(flat(fm_a[:]), flat(fm_b[:]), cm_sq)
                else:
                    squares_of_keys_and_queries(1)
                pool.wait_ge(gdn_o1, b + 1)
                pool.wait_ge(gdn_o0, b + 1)
                square_of(buf[1][:], flat(qkv[b][1][:]), gdn_osq)

        @block.scalar
        def _(act):
            def hi(loaded, slot, n=NB, used=None):
                act.wait_ge(raw_loaded[slot], loaded)
                if used is not None:
                    act.wait_ge(chunk_done, used)
                act.activation(w_hi[:, slot, :, 0:n], raw[:, slot, :, 0:n], ACT.Copy).then_inc(hi_ready, 1)

            def hi_of(c):
                if c < CHUNKS:
                    hi(raw_value(c), c % RING, KVW + BA if c < CPB else NB, c - RING + 1 if c >= RING else None)

            def inverse_root(ps, tmp, scale, waited, value, ln_sem, out_sem, bias=0.0):
                act.wait_ge(waited, value)
                act.activation(tmp, ps, ACT.Ln, scale=scale, bias=eps_col[:, 0:1]).then_inc(ln_sem, 1)
                act.wait_ge(ln_sem, value)
                act.activation(tmp, tmp, ACT.Exp, scale=-0.5, bias=bias).then_inc(out_sem, 1)

            def square(which, n):
                q = which * NCB + n
                if which == 0:
                    act.wait_ge(x_loaded[n], 16)
                else:
                    act.wait_ge(group_added, G_MLP - NCB + n + 1)
                if q > 0:
                    act.wait_ge(ss_act, q)
                act.activation(fm_a[:, 0:2].rearrange("p a b -> p (a b)"), x_sb[:, 0, n * NB:(n + 1) * NB],
                               ACT.Square, accum_out=ss[:, 0, n:n + 1]).then_inc(ss_act, 1)

            def scale_of_tokens(which):
                act.wait_ge(ssum_ready, which + 1)
                act.activation(rstd[:], ssum[:], ACT.Ln, scale=1.0 / D, bias=eps_col[:, 0:1]).then_inc(rstd_ln, 1)
                act.wait_ge(rstd_ln, which + 1)
                act.activation(rstd[:], rstd[:], ACT.Exp, scale=-0.5).then_inc(rstd_ready, 1)

            def piece(which, j):
                act.wait_ge(h_turned, which * NCB + j + 1)
                ps = turn_ps(which, j)
                for t in range(CT):
                    k = CT * j + t
                    g = (N2 if which else N1) + k
                    last = act.activation(h_hi[:, k], ps[:, t * S:(t + 1) * S], ACT.Copy, scale=cols_b[:, g:g + 1])
                    if t % KPC == KPC - 1:
                        last.then_inc(h_hi_ready, 1)

            def mixed(order, first, src, gain, waited, value):
                act.wait_ge(waited, value)
                if gain is None:
                    act.activation(mix_hi[:, first:first + CT], src[:], ACT.Copy).then_inc(mix_hi_ready, 1)
                    return
                for t in range(CT):
                    last = act.activation(mix_hi[:, first + t], src[:, t], ACT.Copy,
                                          scale=cols_b[:, gain + t:gain + t + 1])
                last.then_inc(mix_hi_ready, 1)

            def copy_block(b):
                act.wait_ge(chunk_done, after(b))
                if b == 0:
                    act.wait_ge(rstd_ready, 1)
                for m in range(MT):
                    ps, scale = main[:, b % 2, m], rstd[:, m:m + 1]
                    if b == AT_KV:
                        keys = ps[:, 0:KV * DA].rearrange("p (k d) -> p k d", d=DA)
                        dup = tok[:, m, 0:KV * P].rearrange("p (k j d) -> p k j d", j=2, d=DA)
                        for j in range(2):
                            act.activation(dup[:, :, j], keys, ACT.Copy, scale=scale)
                        act.activation(vals[:, m], ps[:, KV * DA:KVW], ACT.Copy, scale=scale)
                        last = act.activation(ba[:, m], ps[:, KVW:KVW + BA], ACT.Copy, scale=scale)
                    else:
                        last = act.activation(tok[:, m], ps, ACT.Copy, scale=scale)
                last.then_inc(blk_copied, 1)

            def side_work(c):
                for b in range(NBLK):
                    if c == after(b):
                        copy_block(b)
                for n in range(NCB):
                    if c == C_LAST_QUAD + CPG * n + CPG - 1:
                        square(1, n)
                    if c == turn_slot(n) + 1:
                        piece(1, n)
                if c == C_MLP + 3:
                    scale_of_tokens(1)
                if c == A_KV + 1:
                    act.wait_ge(blk_turned, 1)
                    act.activation(buf[4][:, 0:NB], pair_ps(0)[:, 0:NB], ACT.Square).then_inc(att_sq, 1)
                if c == A_KV + 2:
                    inverse_root(side[:, 0], buf[4][:, 0:NB], 1.0 / DA, att_sum, 1, att_ln, att_rs)
                if c == A_KV + 3:
                    act.wait_ge(gate_dve, 3)
                    act.activation(sc[3][:], sc[0][:], ACT.Exp)
                    act.activation(sc[4][:], sc[2][:], ACT.Exp)
                    act.wait_ge(heads_loaded, 48)
                    act.activation(e_alog[:], heads_bc[:, 0], ACT.Exp).then_inc(gate_act, 1)
                if c == A_KV + 4:
                    act.wait_ge(gate_dve, 5)
                    act.activation(sc[7][:], sc[6][:], ACT.Ln).then_inc(gate_act, 1)
                if c == A_KV + 7:
                    act.wait_ge(gate_dve, 14)
                    act.activation(kdecay[:], kdiff[:], ACT.Exp).then_inc(gate_act, 1)
                if c == A_Q + 1:
                    act.wait_ge(blk_turned, 2)
                    act.activation(buf[4], pair_ps(1), ACT.Square).then_inc(att_sq, 1)
                if c == A_Q + 2:
                    inverse_root(side_ps(0), buf[4], 1.0 / DA, att_sum, 2, att_ln, att_rs)
                for kv in range(KV):
                    a = A_HEADS + A_STEPS * kv
                    if c == a + 2:
                        act.wait_ge(att_nm, 3 * (kv + 1))
                        for u in range(4):
                            act.activation(p1[:, u], p1[:, u], ACT.Exp, bias=nmx[:, u:u + 1], accum_out=den[:, u:u + 1])
                    if c == a + 3:
                        for u in range(4):
                            act.activation(p0[:, u], p0[:, u], ACT.Exp, bias=nmx[:, 4 + u:5 + u],
                                           accum_out=den[:, 4 + u:5 + u])
                        act.activation(es[:], esi[:], ACT.Exp).then_inc(att_exp, 1)
                    if c == a + 6:
                        act.wait_ge(att_pT, kv + 1)
                        act.activation(buf[3][:], side_ps(0), ACT.Copy).then_inc(att_pT1, 1)
                    if c == a + 7:
                        act.wait_ge(att_o, kv + 1)
                        act.activation(fm_b[:, 2 * kv:2 * kv + 2].rearrange("p r (m q) -> p m r q", m=MT),
                                       side[:, 3].rearrange("p (m r q) -> p m r q", m=MT, r=2),
                                       ACT.Copy).then_inc(att_oe, 1)
                if c == A_NORM:
                    act.wait_ge(att_oe, KV)
                    act.activation(sq_parts(3)[0], flat(fm_b[:]), ACT.Square).then_inc(att_sq, 1)
                if c == A_NORM + 2:
                    inverse_root(side_ps(0), buf[4], 1.0 / DA, att_sum, 3, att_ln, att_rs)
                if c == A_NORM + 3:
                    mixed(0, CT, fm_b, AO, att_on, 1)
                for b in range(2, 8):
                    if c == after(b) + 1:
                        act.wait_ge(blk_turned, b + 1)
                        dst = qkv[(b - 2) // 3][(b - 2) % 3]
                        for t in range(CT):
                            w = tap(b, 3, t)
                            last = act.activation(dst[:, t], pair_ps(b % 2)[:, t * S:(t + 1) * S], ACT.Copy,
                                                  scale=cols_a[:, w:w + 1])
                        last.then_inc(conv_first, 1)
                for i in range(2):
                    if c == SILU_AT[i] - 3:
                        act.preload_act_table_set(SILU)
                    for n in range(3):
                        if c == SILU_AT[i] + n:
                            act.wait_ge(conv_step, 9 * i + 3 * (n + 1))
                            act.activation(flat(qkv[i][n][:]), flat(qkv[i][n][:]), ACT.Silu).then_inc(silu_done, 1)
                    for n in range(2):
                        if c == SILU_AT[i] + n + 1:
                            act.wait_ge(silu_done, 3 * i + n + 1)
                            act.activation(sq_parts(2 + n)[0], flat(qkv[i][n][:]), ACT.Square).then_inc(gdn_sqhi, 1)
                    if c == SILU_AT[i] + 4:
                        act.preload_act_table_set(LN_EXP)
                    gdn(i, c - GDN_START[i])
                if c == after(AT_CC) + 1:
                    act.wait_ge(blk_turned, AT_CC + 1)
                    act.activation(flat(fm_a[:]), pair_ps(AT_CC % 2), ACT.Copy).then_inc(cm_a, 1)
                if c == after(AT_CX) + 2:
                    act.wait_ge(cm_prod, 1)
                    for t in range(CT):
                        w = CW + 2 * CT + t
                        last = act.activation(fm_b[:, t], fm_a[:, t], ACT.Copy, scale=cols_b[:, w:w + 1])
                    last.then_inc(cm_first, 1)
                if c == after(AT_CB) + 1:
                    act.wait_ge(cm_out, 1)
                    act.activation(sq_parts(3)[0], flat(fm_b[:]), ACT.Square).then_inc(cm_sqhi, 1)
                if c == after(AT_CB) + 3:
                    act.wait_ge(cm_sum, 1)
                    act.activation(flat(tok[:]), pair_ps(AT_CB % 2), ACT.Ln, scale=1.0 / P,
                                   bias=eps_col[:, 0:1]).then_inc(cm_ln, 1)
                    act.wait_ge(cm_ln, 1)
                    act.activation(flat(tok[:]), flat(tok[:]), ACT.Exp, scale=-0.5).then_inc(cm_rs, 1)
                if c == after(AT_CB) + 5:
                    mixed(1, 0, fm_b, CO, cm_on, 1)
                for i in range(2):
                    b = AT_Z + i
                    if c == after(b) + 1:
                        act.wait_ge(blk_turned, b + 1)
                        if i == 1:
                            act.wait_ge(mix_lo_ready, 3)
                        act.activation(flat(fm_a[:]), block_ps(b), ACT.Silu).then_inc(z_silu, 1)
                    if c == after(b) - (3, 1)[i]:
                        act.preload_act_table_set(SILU)
                    if c == after(b) + 2 + 3 * i:
                        act.preload_act_table_set(LN_EXP)
                    if c == after(b) + 3:
                        mixed(2 + i, 2 * CT + CT * i, fm_a, None, z_prod, i + 1)
                if c == GDN_START[1] + 26:
                    act.wait_ge(gdn_o1ps, 2)
                    act.wait_ge(gdn_r1, 2)
                    act.dma_start(x_sb[:], x_dram).then_inc(x_back, 16)

            def gdn(i, s):
                k_t, q_t, v_t = qkv[i]
                if s == 1:
                    if i:
                        act.wait_ge(gdn_on, i)
                    inverse_root(side_ps(0), buf[2][:], 1.0, gdn_sum, 2 * i + 1, gdn_ln, gdn_rs)
                if s == 2:
                    inverse_root(side_ps(1), buf[3][:], 1.0, gdn_sum, 2 * i + 2, gdn_ln, gdn_rs, bias=q_scale[:, 0:1])
                if s == 3:
                    act.wait_ge(gdn_grow, i + 1)
                    act.activation(tiles(half[0][:], CT),
                                   side_ps(0).rearrange("p (h m t) -> p h m t", h=CT, m=MT)[:, :, 1],
                                   ACT.Exp).then_inc(gdn_eg, 1)
                if s == 5:
                    act.wait_ge(gdn_rm2, i + 1)
                    act.activation(buf[0][:], buf[0][:], ACT.Exp).then_inc(gdn_dec, 1)
                if s == 9:
                    act.wait_ge(gdn_Mps, i + 1)
                    act.wait_ge(gdn_kbe, 2 * i + 2)
                    act.activation(buf[3][:], side_ps(0), ACT.Copy).then_inc(gdn_M0, 1)
                for l in range(1, LEVELS):
                    if s == 8 + 2 * l:
                        if l > 1:
                            act.wait_ge(gdn_MTps, 5 * i + l - 1)
                            act.activation(buf[7], side_ps(1), ACT.Copy).then_inc(gdn_MT, 1)
                        act.wait_ge(gdn_Y, 6 * i + l)
                        if l < LEVELS - 1:
                            act.activation(buf[2][:], side_ps(0), ACT.Copy).then_inc(gdn_Ysb, 1)
                        else:
                            act.activation(buf[2][HP:P, 0:NB], side[HP:P, 0], ACT.Copy).then_inc(gdn_Ysb, 1)
                if s == 22:
                    act.wait_ge(gdn_v0ps, i + 1)
                    act.activation(half[4][:], side[:, 0], ACT.Copy).then_inc(gdn_v0, 1)
                if s == 25:
                    act.wait_ge(gdn_v1ps, i + 1)
                    act.activation(half[4][:], side[:, 0], ACT.Copy).then_inc(gdn_v1, 1)
                if s == 26:
                    act.wait_ge(gdn_o1ps, i + 1)
                    act.activation(q_t[:, :, P:S], tiles(side[:, 1], CT), ACT.Copy).then_inc(gdn_o1, 1)
                    act.wait_ge(gdn_o1, i + 1)
                    act.wait_ge(gdn_o0, i + 1)
                    act.activation(sq_parts(3 * i)[0], flat(q_t[:]), ACT.Square).then_inc(gdn_osqhi, 1)
                if s == 28:
                    inverse_root(side_ps(1), buf[2][:], 1.0 / DG, gdn_osum, i + 1, gdn_oln, gdn_ors)

            act.dma_start(rows_n, norm1_g.rearrange("o (t n) -> (o t) n", n=P)).then_inc(norm1_loaded, 16)
            act.preload_act_table_set(LN_EXP)
            hi_of(0)
            act.wait_ge(cols_ready, 1)
            for j in range(2):
                piece(0, j)
                hi_of(j + 1)
            act.wait_ge(const_step, 3)
            for c in range(C_LOOP):
                if c < CPB or c >= C_OUT:
                    hi_of(c + AHEAD)
                if c < NCB - 2:
                    piece(0, c + 2)
                if 2 <= c < NCB + 2:
                    square(0, c - 2)
                if c == NCB + 3:
                    scale_of_tokens(0)
                side_work(c)
                if CPB <= c < C_OUT:
                    hi_of(c + AHEAD)

            def relu(value):
                act.wait_ge(chunk_done, value)
                for m in range(MT):
                    last = act.activation(tok[:, m], side[:, m], ACT.Relu, scale=rstd[:, m:m + 1])
                last.then_inc(hid_relu, 1)

            def square_hidden(value):
                act.wait_ge(hid_turned, value)
                act.activation(flat(fm_a[:]), side_ps(1), ACT.Square).then_inc(hid_sq, 1)

            def hidden_hi(value):
                act.wait_ge(hid_sq, value)
                act.activation(mix_hi[:, 0:CT], fm_a[:], ACT.Copy).then_inc(hid_hi, 1)

            relu(C_LOOP)
            square_hidden(1)

            def turn(it, last=False):
                for s in range(PER):
                    c = C_LOOP + s + AHEAD
                    hi(it * (16 * PER // RING) + raw_value(c), c % RING, NB, it * PER + (c - RING + 1))
                    if s == 0:
                        hidden_hi(it + 1)
                    if s == CPB:
                        relu(it * PER + (C_LOOP + CPB))
                    if s == CPB + 4:
                        act.wait_ge(hid_lo, it + 1)
                        square_hidden(it + 2)
                    if last and s == CPB + 5:
                        act.wait_ge(hid_sq, FB)
                        act.activation(mix_hi[:, CT:2 * CT], fm_a[:], ACT.Copy).then_inc(hid_hi, 1)

            with act.Fori(0, TURNS - 1) as it:
                turn(it)
            turn(TURNS - 1, last=True)
            for c in range(C_LAST, CHUNKS):
                hi_of(c + AHEAD)

        @block.vector
        def _(dve):
            def lo(ready, slot, n=NB):
                dve.wait_ge(hi_ready, ready)
                dve.tensor_tensor(w_lo[:, slot, :, 0:n], raw[:, slot, :, 0:n],
                                  w_hi[:, slot, :, 0:n].bitcast(F32), ALU.subtract).then_inc(lo_ready, 1)

            def lo_of(c):
                if c < CHUNKS:
                    lo(c + 1, c % RING, KVW + BA if c < CPB else NB)

            def square(which, n):
                q = which * NCB + n
                if which == 0:
                    dve.wait_ge(x_loaded[n], 16)
                else:
                    dve.wait_ge(group_added, G_MLP - NCB + n + 1)
                if q > 0:
                    dve.wait_ge(ss_dve, q)
                cols = x_sb[:, 1, n * NB:(n + 1) * NB]
                dve.tensor_tensor_reduce(fm_a[:, 2:4].rearrange("p a b -> p (a b)"), cols, cols, 1.0, 0.0,
                                         ALU.mult, ALU.add, ss[:, 1, n:n + 1]).then_inc(ss_dve, 1)

            def sum_of_squares(which):
                dve.wait_ge(ss_act, NCB * (which + 1))
                dve.wait_ge(ss_dve, NCB * (which + 1))
                dve.tensor_reduce(ssum[:], ss[:], AX_X, ALU.add).then_inc(ssum_ready, 1)

            def piece(which, j):
                ps = turn_ps(which, j)
                for t in range(CT):
                    k = CT * j + t
                    if t % KPC == 0:
                        dve.wait_ge(h_hi_ready, which * CPB + k // KPC + 1)
                    g = (N2 if which else N1) + k
                    last = dve.scalar_tensor_tensor(h_lo[:, k], ps[:, t * S:(t + 1) * S], cols_b[:, g:g + 1],
                                                    h_hi[:, k].bitcast(F32), ALU.mult, ALU.subtract)
                    if t % KPC == KPC - 1:
                        last.then_inc(h_lo_ready, 1)

            def mixed(order, first, src, gain):
                dve.wait_ge(mix_hi_ready, order + 1)
                if gain is None:
                    dve.tensor_tensor(mix_lo[:, first:first + CT], src[:],
                                      mix_hi[:, first:first + CT].bitcast(F32), ALU.subtract).then_inc(mix_lo_ready, 1)
                    return
                for t in range(CT):
                    last = dve.scalar_tensor_tensor(mix_lo[:, first + t], src[:, t], cols_b[:, gain + t:gain + t + 1],
                                                    mix_hi[:, first + t].bitcast(F32), ALU.mult, ALU.subtract)
                last.then_inc(mix_lo_ready, 1)

            def add_group(done, pair, n):
                dve.wait_ge(chunk_done, done)
                cols = x_sb[:, :, n * NB:(n + 1) * NB]
                dve.tensor_tensor(cols, main[:, pair], cols, ALU.add).then_inc(group_added, 1)

            def add_group_of(c):
                g = (c - C_OUT) // CPG
                add_group(c + 1, (g + 1) % 2, g % NCB)

            gates = [0]

            def gate_op(ins):
                gates[0] += 1
                ins.then_inc(gate_dve, 1)
                dve.wait_ge(gate_dve, gates[0])

            def side_work(c):
                if C_OUT <= c < C_MLP and c % CPG == CPG - 1:
                    if c == C_OUT + CPG - 1:
                        dve.wait_ge(x_back, 16)
                    add_group_of(c)
                for n in range(NCB):
                    if c == C_LAST_QUAD + CPG * n + CPG - 1:
                        square(1, n)
                    if c == turn_slot(n) + 1:
                        piece(1, n)
                if c == C_MLP + 2:
                    sum_of_squares(1)
                if c == 7:
                    dve.wait_ge(cols_turned, 3)
                    dve.tensor_copy(cols_b[:, 0:NROWS_B], side[:, 3, 0:NROWS_B]).then_inc(cols_ready, 1)
                    dve.tensor_copy(cols_a[:], side[:, 3, P:P + 96]).then_inc(cols_ready, 1)
                if c == A_KV + 2:
                    dve.wait_ge(att_rs, 1)
                    dve.scalar_tensor_tensor(att_k, pair_ps(0)[:, 0:NB], cols_b[:, KG:KG + 1], buf[4][:, 0:NB],
                                             ALU.mult, ALU.mult).then_inc(att_qk, 1)
                    dve.wait_ge(att_qk, 1)
                    dve.engine_nop().then_inc(pair_free, 1)
                if c == A_KV + 8:
                    dve.tensor_copy(ones_r[:], ones[:])
                    dve.tensor_copy(pair_ones_r[:], pair_ones[:]).then_inc(ones_ready, 1)
                if c == A_KV + 1:
                    dve.wait_ge(blk_copied, 1)
                    dve.wait_ge(heads_loaded, 48)
                    b_in = ba[:, :, 0:HG].rearrange("p m h -> p h m")
                    a_in = ba[:, :, HG:BA].rearrange("p m h -> p h m")
                    gate_op(dve.tensor_scalar(sc[0][:], b_in, -1.0, 87.0, ALU.mult, ALU.min))
                    gate_op(dve.tensor_tensor(sc[1][:], a_in, along(heads_bc[:, 1], MT), ALU.add))
                    gate_op(dve.scalar_tensor_tensor(sc[2][:], sc[1][:], -1.0, sc[1][:], ALU.mult, ALU.min))
                if c == A_KV + 3:
                    dve.wait_ge(gate_act, 1)
                    gate_op(dve.tensor_scalar(sc[5][:], sc[3][:], 1.0, None, ALU.add))
                    gate_op(dve.tensor_scalar(sc[6][:], sc[4][:], 1.0, None, ALU.add))
                    gate_op(dve.reciprocal(beta[:], sc[5][:]))
                    gate_op(dve.scalar_tensor_tensor(sc[8][:], sc[6][:], 1.0, sc[4][:], ALU.subtract, ALU.subtract))
                    gate_op(dve.reciprocal(sc[9][:], sc[6][:]))
                    gate_op(dve.tensor_tensor(sc[10][:], sc[8][:], sc[9][:], ALU.mult))
                if c == A_KV + 5:
                    dve.wait_ge(gate_act, 2)
                    gate_op(dve.tensor_tensor(sc[11][:], sc[7][:], sc[10][:], ALU.subtract))
                    gate_op(dve.scalar_tensor_tensor(sc[0][:], sc[1][:], 0.0, sc[11][:], ALU.max, ALU.add))
                    gate_op(dve.scalar_tensor_tensor(gate[:], sc[0][:], -1.0, along(e_alog[:], MT), ALU.mult, ALU.mult))
                if c == A_KV + 6:
                    dve.wait_ge(gate_pe, 1)
                    gate_op(dve.tensor_copy(flat(gcum[:]), side[:, 3, 0:HG * MT]))
                    gate_op(dve.tensor_tensor(kdiff[:], side[:, 3, HG * MT:HG * MT + HG], gcum[:, :, 0], ALU.subtract))
                if c == A_Q + 2:
                    dve.wait_ge(att_rs, 2)
                    dve.scalar_tensor_tensor(buf[0][:], pair_ps(1), cols_b[:, QG:QG + 1], buf[4],
                                             ALU.mult, ALU.mult).then_inc(att_qk, 1)
                    dve.wait_ge(att_qk, 2)
                    dve.engine_nop().then_inc(pair_free, 1)
                for kv in range(KV):
                    a = A_HEADS + A_STEPS * kv
                    sink = heads_bc[:, 2, 4 * kv:4 * kv + 4].rearrange("p (r a) -> p a r", a=2)
                    if c == a + 1:
                        dve.wait_ge(att_scores, kv + 1)
                        for u in range(4):
                            dve.tensor_tensor_reduce(p1[:, u], side[:, u // 2, (u % 2) * S:(u % 2 + 1) * S], band[:],
                                                     DA ** -0.5, LOWEST, ALU.add, ALU.max, mx[:, u:u + 1])
                            last = dve.tensor_tensor_reduce(p0[:, u], side[:, 2 + u // 2, (u % 2) * P:(u % 2 + 1) * P],
                                                            band[:, P:2 * P], DA ** -0.5, LOWEST, ALU.add, ALU.max,
                                                            mx[:, 4 + u:5 + u])
                        last.then_inc(att_sc, 1)
                    if c == a + 2:
                        dve.wait_ge(att_sc, kv + 1)
                        for m in range(MT):
                            last = dve.tensor_tensor(mxs[:, 4 * m:4 * m + 4].rearrange("p (a r) -> p a r", a=2),
                                                     mx[:, 4 * m:4 * m + 4].rearrange("p (a r) -> p a r", a=2),
                                                     sink, ALU.max)
                        last.then_inc(att_nm, 1)
                        dve.wait_ge(att_nm, 3 * kv + 1)
                        dve.tensor_scalar(nmx[:], mxs[:], -1.0, None, ALU.mult).then_inc(att_nm, 1)
                        dve.wait_ge(att_nm, 3 * kv + 2)
                        for m in range(MT):
                            last = dve.tensor_tensor(esi[:, 4 * m:4 * m + 4].rearrange("p (a r) -> p a r", a=2),
                                                     nmx[:, 4 * m:4 * m + 4].rearrange("p (a r) -> p a r", a=2),
                                                     sink, ALU.add)
                        last.then_inc(att_nm, 1)
                    if c == a + 4:
                        dve.wait_ge(att_exp, kv + 1)
                        dve.tensor_tensor(dsum[:], den[:], es[:], ALU.add).then_inc(att_den, 1)
                        dve.wait_ge(att_den, 2 * kv + 1)
                        dve.reciprocal(rden[:], dsum[:]).then_inc(att_den, 1)
                        dve.wait_ge(att_den, 2 * kv + 2)
                        dve.tensor_tensor(p1, p1, along(rden[:, 0:4], S), ALU.mult)
                        dve.tensor_tensor(p0, p0, along(rden[:, 4:8], P), ALU.mult).then_inc(att_p, 1)
                    if c == a + 6:
                        dve.wait_ge(att_pT, kv + 1)
                        dve.tensor_copy(half[1][:], side[:, 2]).then_inc(att_pT0, 1)
                if c == A_NORM + 1:
                    dve.wait_ge(att_full, 1)
                    dve.wait_ge(att_sq, 3)
                    rounded, rest = sq_parts(3)
                    dve.tensor_tensor(rest, buf[5], rounded.bitcast(F32), ALU.subtract).then_inc(att_lo, 1)
                if c == A_NORM + 2:
                    dve.wait_ge(att_rs, 3)
                    dve.tensor_tensor(flat(fm_b[:]), flat(fm_b[:]), buf[4], ALU.mult).then_inc(att_on, 1)
                if c == A_NORM + 3:
                    mixed(0, CT, fm_b, AO)
                for i in (1, 0):
                    gdn(i, c - GDN_START[i])
                for b in range(2, 8):
                    j = c - after(b)
                    if 1 <= j <= 3:
                        if j == 1:
                            dve.wait_ge(conv_first, b - 1)
                        else:
                            dve.wait_ge(conv_step, 3 * (b - 2) + j - 1)
                        dst = qkv[(b - 2) // 3][(b - 2) % 3]
                        for t in range(CT):
                            w = tap(b, 3 - j, t)
                            last = dve.scalar_tensor_tensor(dst[:, t, j:S], pair_ps(b % 2)[:, t * S:(t + 1) * S - j],
                                                            cols_a[:, w:w + 1], dst[:, t, j:S], ALU.mult, ALU.add)
                        last.then_inc(conv_step, 1)
                        if j == 3:
                            dve.wait_ge(conv_step, 3 * (b - 1))
                            dve.engine_nop().then_inc(pair_free, 1)
                if c == after(AT_CX) + 1:
                    dve.wait_ge(blk_turned, AT_CX + 1)
                    dve.wait_ge(cm_a, 1)
                    dve.tensor_tensor(flat(fm_a[:]), pair_ps(AT_CX % 2), flat(fm_a[:]), ALU.mult).then_inc(cm_prod, 1)
                    dve.wait_ge(cm_prod, 1)
                    dve.engine_nop().then_inc(pair_free, 1)
                for j in (1, 2):
                    if c == after(AT_CX) + 1 + j:
                        if j == 1:
                            dve.wait_ge(cm_first, 1)
                        else:
                            dve.wait_ge(cm_step, 1)
                        for t in range(CT):
                            w = CW + (2 - j) * CT + t
                            last = dve.scalar_tensor_tensor(fm_b[:, t, j:S], fm_a[:, t, 0:S - j], cols_b[:, w:w + 1],
                                                            fm_b[:, t, j:S], ALU.mult, ALU.add)
                        last.then_inc(cm_step, 1)
                if c == after(AT_CC) + 1:
                    dve.wait_ge(cm_a, 1)
                    dve.engine_nop().then_inc(pair_free, 1)
                if c == after(AT_CB) + 1:
                    dve.wait_ge(blk_turned, AT_CB + 1)
                    dve.wait_ge(cm_step, 2)
                    dve.tensor_tensor(flat(fm_b[:]), pair_ps(AT_CB % 2), flat(fm_b[:]), ALU.mult).then_inc(cm_out, 1)
                if c == after(AT_CB) + 2:
                    dve.wait_ge(cm_sqhi, 1)
                    dve.wait_ge(cm_sq, 1)
                    rounded, rest = sq_parts(3)
                    dve.tensor_tensor(rest, flat(fm_a[:]), rounded.bitcast(F32), ALU.subtract).then_inc(cm_sqlo, 1)
                if c == after(AT_CB) + 4:
                    dve.wait_ge(cm_rs, 1)
                    dve.engine_nop().then_inc(pair_free, 1)
                    dve.tensor_tensor(flat(fm_b[:]), flat(fm_b[:]), flat(tok[:]), ALU.mult).then_inc(cm_on, 1)
                if c == after(AT_CB) + 5:
                    mixed(1, 0, fm_b, CO)
                for i in range(2):
                    b = AT_Z + i
                    if b == NBLK - 1 and c == after(b):
                        dve.wait_ge(blk_copied, NBLK)
                        dve.engine_nop().then_inc(pair_free, 1)
                    if c == after(b) + 2:
                        dve.wait_ge(z_silu, i + 1)
                        if b < NBLK - 1:
                            dve.engine_nop().then_inc(pair_free, 1)
                        dve.wait_ge(gdn_on, i + 1)
                        dve.tensor_tensor(flat(fm_a[:]), flat(fm_a[:]), flat(qkv[i][1][:]), ALU.mult).then_inc(z_prod, 1)
                    if c == after(b) + 3:
                        mixed(2 + i, 2 * CT + CT * i, fm_a, None)

            def gdn(i, s):
                k_t, q_t, v_t = qkv[i]
                units = 2 * CT
                h = slice(4 * i, 4 * i + 4)
                if s == 0:
                    for n in range(2):
                        rounded, rest = sq_parts(2 + n)
                        dve.wait_ge(gdn_sq, 2 * i + n + 1)
                        dve.wait_ge(gdn_sqhi, 2 * i + n + 1)
                        dve.tensor_tensor(rest, (buf[4], buf[0][:])[n], rounded.bitcast(F32), ALU.subtract).then_inc(gdn_sqlo, 1)
                if s == 2:
                    dve.wait_ge(gdn_rs, 2 * i + 1)
                    dve.tensor_tensor(flat(k_t[:]), flat(k_t[:]), buf[2][:], ALU.mult).then_inc(gdn_kn, 1)
                if s == 3:
                    dve.wait_ge(gdn_rs, 2 * i + 2)
                    dve.tensor_tensor(flat(q_t[:]), flat(q_t[:]), buf[3][:], ALU.mult).then_inc(gdn_qn, 1)
                    dve.wait_ge(gdn_eg, i + 1)
                    if i == 0:
                        dve.wait_ge(att_scores, KV)
                    else:
                        dve.wait_ge(gdn_Y, 6 * i)
                    dve.tensor_tensor(tiles(buf[0][:], units), tiles(side_ps(0), units), over(upper_add[:], units),
                                      ALU.add).then_inc(gdn_rm, 1)
                if s == 4:
                    dve.wait_ge(gdn_brow, i + 1)
                    dve.wait_ge(gdn_kn, i + 1)
                    dve.wait_ge(gdn_qn, i + 1)
                    dve.tensor_tensor(buf[3][:], side_ps(1), flat(k_t[:]), ALU.mult).then_inc(gdn_kb, 1)
                if s == 5:
                    dve.wait_ge(gdn_vT, i + 1)
                    dve.tensor_tensor(tiles(buf[6], units), tiles(side_ps(0), units), along(flat(beta[:, h]), P),
                                      ALU.mult).then_inc(gdn_vb, 1)
                    dve.wait_ge(gdn_kb, i + 1)
                    dve.wait_ge(gdn_eg, i + 1)
                    kb = buf[3][:].rearrange("p (h m t) -> p h m t", h=CT, m=MT)[:, :, 1]
                    dve.tensor_tensor(tiles(half[1][:], CT), kb, tiles(half[0][:], CT), ALU.mult).then_inc(gdn_kbe, 1)
                    dve.tensor_tensor(tiles(half[2][:], CT), q_t[:, :, P:S], tiles(half[0][:], CT),
                                      ALU.mult).then_inc(gdn_kbe, 1)
                if s == 6:
                    dve.wait_ge(gdn_gram, i + 1)
                    dve.wait_ge(gdn_dec, i + 1)
                    dve.tensor_tensor(buf[4], side_ps(1), buf[0][:], ALU.mult).then_inc(gdn_AT, 1)
                if s == 7:
                    dve.wait_ge(gdn_qk, i + 1)
                    dve.tensor_tensor(buf[5], side_ps(0), buf[0][:], ALU.mult).then_inc(gdn_QKT, 1)
                if s == 8:
                    dve.wait_ge(gdn_ktok, i + 1)
                    dve.wait_ge(gate_act, 3)
                    dve.tensor_tensor(tiles(half[3][:], CT), tiles(side[:, 2], CT), along(kdecay[:, h], P),
                                      ALU.mult).then_inc(gdn_kdec, 1)
                for l in range(1, LEVELS):
                    if s == 9 + 2 * l:
                        dve.wait_ge(gdn_upd, 6 * i + l)
                        if l < LEVELS - 1:
                            if l == 1:
                                dve.wait_ge(gdn_M0, i + 1)
                            dve.tensor_tensor(buf[3][:], buf[3][:], side_ps(1), ALU.subtract).then_inc(gdn_M, 1)
                        else:
                            dve.tensor_scalar(tiles(buf[7], units)[0:HP, :, HP:P], tiles(side[:, 2], units)[0:HP],
                                              -1.0, None, ALU.mult).then_inc(gdn_MTlast, 1)
                if s == 23:
                    dve.wait_ge(gdn_Sps, i + 1)
                    dve.tensor_copy(half[5][:], side[:, 1]).then_inc(gdn_S, 1)
                    dve.tensor_copy(q_t[:, :, 0:P], tiles(side[:, 2], CT)).then_inc(gdn_o0, 1)
                if s == 24:
                    dve.wait_ge(gdn_kSps, i + 1)
                    vb = buf[6].rearrange("p (h m t) -> p h m t", h=CT, m=MT)[:, :, 1]
                    dve.tensor_tensor(tiles(half[0][:], CT), vb, tiles(side[:, 3], CT), ALU.subtract).then_inc(gdn_r1, 1)
                if s == 27:
                    dve.wait_ge(gdn_osq, i + 1)
                    dve.wait_ge(gdn_osqhi, i + 1)
                    rounded, rest = sq_parts(3 * i)
                    dve.tensor_tensor(rest, buf[1][:], rounded.bitcast(F32), ALU.subtract).then_inc(gdn_osqlo, 1)
                if s == 28:
                    dve.wait_ge(gdn_ors, i + 1)
                    dve.scalar_tensor_tensor(flat(q_t[:]), flat(q_t[:]), cols_b[:, GN:GN + 1], buf[2][:],
                                             ALU.mult, ALU.mult).then_inc(gdn_on, 1)

            dve.wait_ge(cols_turned, 1)
            dve.tensor_copy(cols_b[:, N1:N1 + KT], main[:, 0, 0, 0:KT]).then_inc(cols_ready, 1)
            lo_of(0)
            for j in range(2):
                piece(0, j)
                lo_of(j + 1)
            for c in range(C_LOOP):
                if c < CPB or c >= C_OUT:
                    lo_of(c + AHEAD)
                if c < NCB - 2:
                    piece(0, c + 2)
                if 2 <= c < NCB + 2:
                    square(0, c - 2)
                if c == NCB + 2:
                    sum_of_squares(0)
                side_work(c)
                if CPB <= c < C_OUT:
                    lo_of(c + AHEAD)

            def hidden_lo(value):
                dve.wait_ge(hid_hi, value)
                dve.tensor_tensor(mix_lo[:, 0:CT], fm_a[:], mix_hi[:, 0:CT].bitcast(F32),
                                  ALU.subtract).then_inc(hid_lo, 1)

            def turn(it, last=False):
                for s in range(PER):
                    lo(it * PER + (C_LOOP + s + AHEAD + 1), (s + AHEAD) % RING)
                    if s == 0:
                        hidden_lo(it + 1)
                    if s >= CPB and (s - CPB) % CPG == CPG - 1:
                        n = (s - CPB) // CPG
                        add_group(it * PER + (C_LOOP + s + 1), (G_MLP + n + 1) % 2, n)
                    if last and s == CPB + 6:
                        dve.wait_ge(hid_hi, FB)
                        dve.tensor_tensor(mix_lo[:, CT:2 * CT], fm_a[:], mix_hi[:, CT:2 * CT].bitcast(F32),
                                          ALU.subtract).then_inc(hid_lo, 1)

            with dve.Fori(0, TURNS - 1) as it:
                turn(it)
            turn(TURNS - 1, last=True)
            for c in range(C_LAST, CHUNKS):
                lo_of(c + AHEAD)
                n = (c - C_LAST) // CPG
                if (c - C_LAST) % CPG == CPG - 1 and n < NCB - 1:
                    add_group(c + 1, (G_MLP + n + 1) % 2, n)
            dve.wait_ge(chunk_done, CHUNKS)
            for m in range(MT):
                cols = x_sb[:, m, D - NB:D]
                dve.tensor_tensor(cols, main[:, (G_MLP + NCB) % 2, m], cols, ALU.add).then_inc(group_added, 1)

        @block.tensor
        def _(pe):
            def chunk(ready, slot, lhs, k, banks, n, first, last):
                hi_t, lo_t = lhs
                pe.wait_ge(lo_ready, ready)
                for j in range(KPC):
                    for m in range(MT):
                        a_hi = hi_t[:, k + j, m * P:(m + 1) * P]
                        a_lo = lo_t[:, k + j, m * P:(m + 1) * P]
                        w_h, w_l = w_hi[:, slot, j, 0:n], w_lo[:, slot, j, 0:n]
                        o = banks[:, m, 0:n]
                        end = last and j == KPC - 1
                        pe.matmul(o, a_hi, w_h, start=first and j == 0, stop=False)
                        pe.matmul(o, a_hi, w_l, start=False, stop=False)
                        ins = pe.matmul(o, a_lo, w_h, start=False, stop=end)
                ins.then_inc(chunk_done, 1)

            h_t, mix_t = (h_hi, h_lo), (mix_hi, mix_lo)

            def turn_piece(which, j):
                if which == 0:
                    pe.wait_ge(x_loaded[j], 16)
                    if j == 3:
                        pe.wait_ge(h_lo_ready, CPG)
                else:
                    pe.wait_ge(group_added, G_MLP - NCB + j + 1)
                    if j == 1:
                        pe.wait_ge(z_silu, 2)
                    if j > 1:
                        pe.wait_ge(h_lo_ready, CPB + CPG * (j - (j == 2)))
                ps = turn_ps(which, j)
                for t in range(CT):
                    for m in range(MT):
                        ins = pe.transpose(ps[:, t * S + m * P:t * S + (m + 1) * P],
                                           x_sb[:, m, (CT * j + t) * P:(CT * j + t + 1) * P], ident[:])
                ins.then_inc(h_turned, 1)

            def turn_block(b):
                pe.wait_ge(blk_copied, b + 1)
                if b == NBLK - 1:
                    pe.wait_ge(gdn_o1, 2)
                ps = block_ps(b)
                if b == AT_KV:
                    for k in range(KV):
                        for m in range(MT):
                            ins = pe.transpose(ps[:, k * S + m * P:k * S + (m + 1) * P],
                                               tok[:, m, k * P:(k + 1) * P], ident[:])
                else:
                    for t in range(CT):
                        for m in range(MT):
                            ins = pe.transpose(ps[:, t * S + m * P:t * S + (m + 1) * P],
                                               tok[:, m, t * P:(t + 1) * P], ident[:])
                ins.then_inc(blk_turned, 1)

            def sums(ps, weights, src, n=2):
                for j in range(n):
                    ins = pe.matmul(ps[:, j * NB:(j + 1) * NB], weights[:], src[:, j * NB:(j + 1) * NB],
                                    start=True, stop=True)
                return ins

            def split_sums(ps, weights, hi_part, lo_part):
                for j in range(2):
                    cols = slice(j * NB, (j + 1) * NB)
                    pe.matmul(ps[:, cols], weights[:], hi_part[:, cols],
                              start=True, stop=False)
                    ins = pe.matmul(ps[:, cols], weights[:], lo_part[:, cols],
                                    start=False, stop=True)
                return ins

            def side_work(c):
                for b in range(NBLK):
                    if c == (A_KV if b == AT_KV else after(b)):
                        turn_block(b)
                for n in range(NCB):
                    if c == turn_slot(n):
                        turn_piece(1, n)
                if c < NCB - 2:
                    turn_piece(0, c + 2)
                if c == 6:
                    pe.wait_ge(h_lo_ready, 3 * CPG)
                    pe.wait_ge(rows_loaded, 16 * 9)
                    pe.transpose(side[:, 3, 0:NROWS_B], rows_b[0:NROWS_B, :],
                                 ident[0:NROWS_B, 0:NROWS_B]).then_inc(cols_turned, 1)
                    pe.wait_ge(convw_loaded, 16)
                    pe.transpose(side[:, 3, P:P + 96], rows_a, ident[0:96, 0:96]).then_inc(cols_turned, 1)
                if c == A_KV + 1:
                    pe.wait_ge(att_sq, 1)
                    pe.wait_ge(const_step, N_CONST)
                    sums(side[:, 0], pair_ones, buf[4], 1).then_inc(att_sum, 1)
                if c == A_KV + 5:
                    pe.wait_ge(gate_dve, 12)
                    pe.matmul(side[:, 3, 0:HG * MT], upper[:], flat(gate[:]), start=True, stop=True)
                    pe.matmul(side[:, 3, HG * MT:HG * MT + HG], ones[:], gate[:, :, 0],
                              start=True, stop=True).then_inc(gate_pe, 1)
                if c == A_Q + 1:
                    pe.wait_ge(att_sq, 2)
                    pe.wait_ge(att_rs, 1)
                    sums(side_ps(0), pair_ones, buf[4]).then_inc(att_sum, 1)
                for kv in range(KV):
                    a = A_HEADS + A_STEPS * kv
                    q_fm = tiles(buf[0][:], CT)
                    if c == a:
                        pe.wait_ge(att_qk, 2)
                        if kv == 0:
                            pe.wait_ge(gate_dve, 14)
                        else:
                            pe.wait_ge(att_oe, kv)
                        for u in range(4):
                            par, pr = u // 2, u % 2
                            rows = slice(par * DA, (par + 1) * DA)
                            q_h = q_fm[rows, 2 * kv + pr]
                            pe.matmul(side[:, par, pr * S:(pr + 1) * S], q_h[:, P:S],
                                      att_k[rows, kv * S:(kv + 1) * S], start=True, stop=True)
                            ins = pe.matmul(side[:, 2 + par, pr * P:(pr + 1) * P], q_h[:, 0:P],
                                            att_k[rows, kv * S:kv * S + P], start=True, stop=True)
                        ins.then_inc(att_scores, 1)
                    if c == a + 5:
                        pe.wait_ge(att_p, kv + 1)
                        for u in range(4):
                            for kt in range(2):
                                pe.transpose(side[:, kt, u * P:(u + 1) * P], p1[:, u, kt * P:(kt + 1) * P], ident[:])
                            ins = pe.transpose(side[:, 2, u * P:(u + 1) * P], p0[:, u], ident[:])
                        ins.then_inc(att_pT, 1)
                    if c == a + 6:
                        pe.wait_ge(att_pT1, kv + 1)
                        pe.wait_ge(att_pT0, kv + 1)
                        pt1 = buf[3][:].rearrange("p (k u q) -> p k u q", k=2, u=4)
                        pt0 = tiles(half[1][:], 4)
                        for par in range(2):
                            o = side[par * DA:(par + 1) * DA, 3]
                            two = slice(2 * par, 2 * par + 2)
                            v_h = vals[:, :, kv * DA:(kv + 1) * DA]
                            pe.matmul(o[:, 0:S], v_h[:, 0], pt0[:, two], start=True, stop=True)
                            pe.matmul(o[:, S:2 * S], v_h[:, 0], pt1[:, 0, two], start=True, stop=False)
                            ins = pe.matmul(o[:, S:2 * S], v_h[:, 1], pt1[:, 1, two], start=False, stop=True)
                        ins.then_inc(att_o, 1)
                if c == A_NORM + 1:
                    pe.wait_ge(att_lo, 1)
                    pe.wait_ge(ones_ready, 1)
                    split_sums(side_ps(0), pair_ones_r, *sq_parts(3)).then_inc(att_sum, 1)
                for i in range(2):
                    gdn(i, c - GDN_START[i])
                if c == after(AT_CB) + 2:
                    pe.wait_ge(cm_sqlo, 1)
                    split_sums(pair_ps(AT_CB % 2), ones_r, *sq_parts(3)).then_inc(cm_sum, 1)

            def gdn(i, s):
                k_t, q_t, v_t = qkv[i]
                units = [(h, m) for h in range(CT) for m in range(MT)]

                def unit(t, h, m):
                    return t[:, (2 * h + m) * P:(2 * h + m + 1) * P]

                def head(t, h):
                    return t[:, h * P:(h + 1) * P]

                def column(t, h, m):
                    return t[:, 4 * i + h, m:m + 1].to_broadcast([P, P])

                if s == 0:
                    if i:
                        pe.wait_ge(gdn_oln, i)
                    pe.wait_ge(gdn_sqlo, 2 * i + 1)
                    split_sums(side_ps(0), ones_r, *sq_parts(2)).then_inc(gdn_sum, 1)
                    pe.wait_ge(gdn_sqlo, 2 * i + 2)
                    split_sums(side_ps(1), ones_r, *sq_parts(3)).then_inc(gdn_sum, 1)
                if s == 2:
                    pe.wait_ge(gate_dve, 13)
                    pe.wait_ge(gdn_ln, 2 * i + 1)
                    for h, m in units:
                        ins = pe.transpose(unit(side_ps(0), h, m), column(gcum, h, m), ident[:])
                    ins.then_inc(gdn_grow, 1)
                if s == 3:
                    pe.wait_ge(gdn_ln, 2 * i + 2)
                    for h, m in units:
                        ins = pe.transpose(unit(side_ps(1), h, m), column(beta, h, m), ident[:])
                    ins.then_inc(gdn_brow, 1)
                if s == 4:
                    pe.wait_ge(gdn_rm, i + 1)
                    pe.wait_ge(gdn_eg, i + 1)
                    for h, m in units:
                        ins = pe.transpose(unit(side_ps(0), h, m), v_t[:, h, m * P:(m + 1) * P], ident[:])
                    ins.then_inc(gdn_vT, 1)
                if s == 5:
                    pe.wait_ge(gdn_kb, i + 1)
                    for h, m in units:
                        ins = pe.matmul(unit(side_ps(1), h, m), k_t[:, h, m * P:(m + 1) * P],
                                        unit(buf[3], h, m), start=True, stop=True)
                    ins.then_inc(gdn_gram, 1)
                if s == 6:
                    pe.wait_ge(gdn_vb, i + 1)
                    pe.wait_ge(gdn_qn, i + 1)
                    for h, m in units:
                        ins = pe.matmul(unit(side_ps(0), h, m), k_t[:, h, m * P:(m + 1) * P],
                                        q_t[:, h, m * P:(m + 1) * P], start=True, stop=True)
                    ins.then_inc(gdn_qk, 1)
                if s == 7:
                    pe.wait_ge(gdn_AT, i + 1)
                    for h in range(CT):
                        ins = pe.transpose(head(side[:, 2], h), k_t[:, h, 0:P], ident[:])
                    ins.then_inc(gdn_ktok, 1)
                if s == 8:
                    pe.wait_ge(gdn_MT0, i + 1)
                    pe.wait_ge(gdn_QKT, i + 1)
                    for h, m in units:
                        ins = pe.transpose(unit(side_ps(0), h, m), unit(buf[7], h, m), ident[:])
                    ins.then_inc(gdn_Mps, 1)
                for l in range(1, LEVELS):
                    if s == 7 + 2 * l:
                        if l == 1:
                            pe.wait_ge(gdn_M0, i + 1)
                        else:
                            pe.wait_ge(gdn_M, 5 * i + l - 1)
                            for h, m in units:
                                ins = pe.transpose(unit(side_ps(1), h, m), unit(buf[3], h, m), ident[:])
                            ins.then_inc(gdn_MTps, 1)
                        if l < LEVELS - 1:
                            pe.wait_ge(gdn_Al, 5 * i + l)
                            for h, m in units:
                                ins = pe.matmul(unit(side_ps(0), h, m), unit(buf[l % 2], h, m), unit(buf[3], h, m),
                                                start=True, stop=True)
                        else:
                            for u, (h, m) in enumerate(units):
                                ins = pe.matmul(side[HP:P, 0, u * HP:(u + 1) * HP], unit(buf[4], h, m)[0:HP, HP:P],
                                                unit(buf[3], h, m)[0:HP, 0:HP], start=True, stop=True)
                        ins.then_inc(gdn_Y, 1)
                    if s == 8 + 2 * l:
                        if l == 1:
                            pe.wait_ge(gdn_kdec, i + 1)
                        else:
                            pe.wait_ge(gdn_MT, 5 * i + l - 1)
                        pe.wait_ge(gdn_Ysb, 6 * i + l)
                        if l < LEVELS - 1:
                            for h, m in units:
                                ins = pe.matmul(unit(side_ps(1), h, m), unit(buf[7], h, m), unit(buf[2], h, m),
                                                start=True, stop=True)
                        else:
                            for u, (h, m) in enumerate(units):
                                ins = pe.matmul(side[0:HP, 2, u * HP:(u + 1) * HP], buf[2][HP:P, u * HP:(u + 1) * HP],
                                                unit(buf[7], h, m)[HP:P, HP:P], start=True, stop=True)
                        ins.then_inc(gdn_upd, 1)
                if s == 21:
                    pe.wait_ge(gdn_MTlast, i + 1)
                    for h in range(CT):
                        ins = pe.matmul(head(side[:, 0], h), unit(buf[7], h, 0), unit(buf[6], h, 0),
                                        start=True, stop=True)
                    ins.then_inc(gdn_v0ps, 1)
                if s == 22:
                    pe.wait_ge(gdn_v0, i + 1)
                    for h in range(CT):
                        pe.matmul(head(side[:, 1], h), head(half[3], h), head(half[4], h), start=True, stop=True)
                    for h in range(CT):
                        ins = pe.matmul(head(side[:, 2], h), head(half[4], h), unit(buf[5], h, 0),
                                        start=True, stop=True)
                    ins.then_inc(gdn_Sps, 1)
                if s == 23:
                    pe.wait_ge(gdn_S, i + 1)
                    for h in range(CT):
                        ins = pe.matmul(head(side[:, 3], h), head(half[1], h), head(half[5], h),
                                        start=True, stop=True)
                    ins.then_inc(gdn_kSps, 1)
                if s == 24:
                    pe.wait_ge(gdn_r1, i + 1)
                    for h in range(CT):
                        ins = pe.matmul(head(side[:, 0], h), unit(buf[7], h, 1), head(half[0], h),
                                        start=True, stop=True)
                    ins.then_inc(gdn_v1ps, 1)
                if s == 25:
                    pe.wait_ge(gdn_v1, i + 1)
                    for h in range(CT):
                        pe.matmul(head(side[:, 1], h), head(half[5], h), head(half[2], h), start=True, stop=False)
                        ins = pe.matmul(head(side[:, 1], h), head(half[4], h), unit(buf[5], h, 1),
                                        start=False, stop=True)
                    ins.then_inc(gdn_o1ps, 1)
                if s == 27:
                    pe.wait_ge(gdn_osqlo, i + 1)
                    split_sums(side_ps(1), ones_r, *sq_parts(3 * i)).then_inc(gdn_osum, 1)

            pe.wait_ge(const_step, 2)
            turn_piece(0, 0)
            pe.wait_ge(norm1_loaded, 16)
            pe.transpose(main[:, 0, 0, 0:KT], rows_n, ident[0:KT, 0:KT]).then_inc(cols_turned, 1)
            turn_piece(0, 1)
            pe.wait_ge(cols_ready, 1)
            for c in range(C_OUT):
                b, k = c // CPB, c % CPB
                if k == 0 and b >= 2:
                    pe.wait_ge(pair_free, b - 1)
                if b == 0:
                    pe.wait_ge(h_lo_ready, k + 1)
                n = KVW + BA if b == AT_KV else NB
                chunk(c + 1, c % RING, h_t, k * KPC, main[:, b % 2], n, k == 0, k == CPB - 1)
                side_work(c)
            for c in range(C_OUT, C_MLP):
                g, k = (c - C_OUT) // CPG, (c - C_OUT) % CPG
                if k == 0:
                    if g < 2:
                        pe.wait_ge(pair_free, NBLK - 1 + g)
                    else:
                        pe.wait_ge(group_added, g - 1)
                    if g % NCB == 0:
                        pe.wait_ge(mix_lo_ready, g // NCB + 1)
                chunk(c + 1, c % RING, mix_t, QUADS[g // NCB] * CT + k * KPC, main[:, (g + 1) % 2], NB,
                      k == 0, k == CPG - 1)
                side_work(c)
            def turn_hidden(value):
                pe.wait_ge(hid_relu, value)
                for t in range(CT):
                    for m in range(MT):
                        ins = pe.transpose(side_ps(1)[:, t * S + m * P:t * S + (m + 1) * P],
                                           tok[:, m, t * P:(t + 1) * P], ident[:])
                ins.then_inc(hid_turned, 1)

            for k in range(CPB):
                pe.wait_ge(h_lo_ready, CPB + max(k + 1, 2 * CPG))
                chunk(C_MLP + k + 1, (C_MLP + k) % RING, h_t, k * KPC, side[:, 0:2], NB, k == 0, k == CPB - 1)
                side_work(C_MLP + k)
            turn_hidden(1)
            with pe.Fori(0, TURNS) as it:
                pe.wait_ge(hid_relu, it + 1)
                for s in range(CPB):
                    chunk(it * PER + (C_LOOP + s + 1), s % RING, h_t, s * KPC, side[:, 0:2], NB,
                          s == 0, s == CPB - 1)
                pe.wait_ge(hid_lo, it + 1)
                for s in range(CPB, PER):
                    n, k = (s - CPB) // CPG, (s - CPB) % CPG
                    if k == 0:
                        pe.wait_ge(group_added, it * NCB + (G_MLP + n - 1))
                    chunk(it * PER + (C_LOOP + s + 1), s % RING, mix_t, k * KPC, main[:, (G_MLP + n + 1) % 2], NB,
                          k == 0, k == CPG - 1)
                    if s == CPB + 2:
                        turn_hidden(it + 2)
            pe.wait_ge(hid_lo, FB)
            for c in range(C_LAST, CHUNKS):
                n, k = (c - C_LAST) // CPG, (c - C_LAST) % CPG
                if k == 0:
                    pe.wait_ge(group_added, G_MLP + NCB * (FB - 1) + n - 1)
                chunk(c + 1, c % RING, mix_t, CT + k * KPC, main[:, (G_MLP + n + 1) % 2], NB, k == 0, k == CPG - 1)


_INS = ["x", "norm1_g", "w_in", "conv_w", "conv_out_g", "q_norm_g", "k_norm_g", "attn_sinks", "attn_out_g",
        "gdn_conv_w", "gdn_A_log", "gdn_dt_bias", "gdn_norm_g", "w_out", "norm2_g", "w_up", "w_down"]


def kernel(**inputs):
    import numpy as np
    import concourse.bacc as bacc
    from concourse.bass_utils import run_bass_kernel_spmd

    nc = bacc.Bacc("TRN2", target_bir_lowering=False, num_devices=1)
    arrays, args = {}, []
    for name in _INS:
        a = np.ascontiguousarray(inputs[name])
        arrays[f"in_{name}"] = a
        args.append(nc.dram_tensor(f"in_{name}", a.shape, mybir.dt.from_np(a.dtype), kind="ExternalInput").ap())
    args.append(nc.dram_tensor("out_0", inputs["x"].shape, F32, kind="ExternalOutput").ap())
    build(nc, *args)
    r = run_bass_kernel_spmd(nc, [arrays], core_ids=[0])
    return r.results[0]["out_0"]
```

```python
from contextlib import ExitStack
from math import log

import concourse.bass as bass
from concourse import mybir

F32 = mybir.dt.float32
F32R = mybir.dt.float32r
ALU = mybir.AluOpType
ACT = mybir.ActivationFunctionType
AX_X = mybir.AxisListType.X

P = 128
EPS = 1e-6
NEG = -1e30
LOWEST = -3e38
LN_EXP = "natural_log_exp_and_others"
SILU = "silu_and_others"


def build(nc, x, norm1_g, w_in, conv_w, conv_out_g, q_norm_g, k_norm_g, attn_sinks, attn_out_g,
          gdn_conv_w, gdn_A_log, gdn_dt_bias, gdn_norm_g, w_out, norm2_g, w_up, w_down, out):
    S, D = x.shape[1], x.shape[2]
    FF = w_up.shape[2]
    MT = S // P
    KT = D // P
    NB = 512
    CT = NB // P
    KPC = 2
    CPB = KT // KPC
    RING = 4
    AHEAD = 3
    assert S == 256 and D == 2048 and FF % NB == 0 and MT == 2

    CONV_W = D // 4
    HA, DA = attn_sinks.shape[1], q_norm_g.shape[1]
    KV = 2
    HG, DG = gdn_A_log.shape[1], gdn_norm_g.shape[1]
    GDN_W = HG * DG
    assert DG == P and 2 * DA == P and HG == 8 and HA == 8 and CONV_W == NB and HA * DA == NB

    AT_Q = 3 * CONV_W
    AT_K = AT_Q + HA * DA
    KVW = 2 * KV * DA
    GD_Q = AT_K + KVW
    GD_K, GD_V, GD_Z = GD_Q + GDN_W, GD_Q + 2 * GDN_W, GD_Q + 3 * GDN_W
    GD_B = GD_Q + 4 * GDN_W
    BA = 2 * HG
    BLOCKS = [("kv", AT_K), ("aq", AT_Q),
              ("gk", GD_K), ("gq", GD_Q), ("gv", GD_V),
              ("gk", GD_K + NB), ("gq", GD_Q + NB), ("gv", GD_V + NB),
              ("cc", CONV_W), ("cx", 2 * CONV_W), ("cb", 0),
              ("gz", GD_Z), ("gz", GD_Z + NB)]
    NBLK = len(BLOCKS)
    AT_KV, AT_AQ, AT_CC, AT_CX, AT_CB, AT_Z = 0, 1, 8, 9, 10, 11
    QUADS = [1, 0, 2, 3]
    CPG = CT // KPC
    NCB = D // NB
    C_OUT = NBLK * CPB
    C_MLP = C_OUT + len(QUADS) * NCB * CPG
    C_LAST_QUAD = C_MLP - NCB * CPG
    FB = FF // NB
    C_LOOP = C_MLP + CPB
    PER = CPB + NCB * CPG
    TURNS = FB - 1
    C_LAST = C_LOOP + PER * TURNS
    CHUNKS = C_LAST + NCB * CPG
    G_MLP = len(QUADS) * NCB
    assert PER % RING == 0 and C_LOOP % RING == 0

    A_KV = CPB + 1
    A_Q = 2 * CPB
    A_HEADS = A_Q + 4
    A_STEPS = 8
    A_NORM = A_HEADS + KV * A_STEPS
    GDN_START = [5 * CPB + 6, 5 * CPB + 6 + 29]
    SILU_AT = [5 * CPB + 2, 8 * CPB + 2]
    LEVELS = 7

    def after(b):
        return CPB * (b + 1)

    with ExitStack() as ctx:
        def sb(name, shape, dt=F32):
            return ctx.enter_context(nc.sbuf_tensor(name, shape, dt))

        def sem(name):
            return ctx.enter_context(nc.semaphore(name))

        raw = sb("raw", [P, RING, KPC, NB])
        w_hi = sb("w_hi", [P, RING, KPC, NB], F32R)
        w_lo = sb("w_lo", [P, RING, KPC, NB], F32R)
        x_sb = sb("x_sb", [P, MT, D])
        h_hi = sb("h_hi", [P, KT, S], F32R)
        h_lo = sb("h_lo", [P, KT, S], F32R)
        mix_hi = sb("mix_hi", [P, KT, S], F32R)
        mix_lo = sb("mix_lo", [P, KT, S], F32R)
        qkv = [[sb(f"gdn_{n}{b}", [P, CT, S]) for n in "kqv"] for b in range(2)]
        tok = sb("tok", [P, MT, NB])
        fm_a = sb("fm_a", [P, CT, S])
        fm_b = sb("fm_b", [P, CT, S])
        buf = [sb(f"buf{i}", [P, 2 * NB]) for i in range(4)]
        buf += [x_sb[:, i // 2, (i % 2) * 2 * NB:(i % 2 + 1) * 2 * NB] for i in range(4)]
        half = [sb(f"half{i}", [P, NB]) for i in range(6)]

        ident = sb("ident", [P, P])
        ones = sb("ones", [P, P])
        key_sums = sb("key_sums", [P, MT, KV])
        query_sums = sb("query_sums", [P, MT * HA])
        ones_r = sb("ones_r", [P, P], F32R)
        pair_ones_r = sb("pair_ones_r", [P, P], F32R)
        upper = sb("upper", [P, P])
        pair_ones = sb("pair_ones", [P, P])
        upper_add = sb("upper_add", [P, P])
        band = sb("band", [P, 2 * P])
        joins = sb("joins", [P, LEVELS, P])
        halves = sb("halves", [P, LEVELS - 1, P])
        eps_col = sb("eps_col", [P, 1])
        q_scale = sb("q_scale", [P, 1])

        rows_a = half[0][0:96, 0:P]
        rows_b = half[0][0:56, P:2 * P]
        rows_n = half[0][0:KT, 2 * P:3 * P]
        cols_a = sb("cols_a", [P, 96])
        cols_b = sb("cols_b", [P, 56])
        heads_bc = sb("heads_bc", [P, 3, HG])
        ss = sb("ss", [P, MT, NCB])
        ssum = sb("ssum", [P, MT])
        rstd = sb("rstd", [P, MT])
        ba = sb("ba", [P, MT, BA])
        sc = [sb(f"sc{i}", [P, HG, MT]) for i in range(12)]
        e_alog = sb("e_alog", [P, HG])
        beta = sb("beta", [P, HG, MT])
        gate = sb("gate", [P, HG, MT])
        gcum = sb("gcum", [P, HG, MT])
        kdecay = sb("kdecay", [P, HG])
        kdiff = sb("kdiff", [P, HG])
        mx, mxs, nmx, esi, es, den, dsum, rden = (sb(n, [P, 8]) for n in (
            "mx", "mxs", "nmx", "esi", "es", "den", "dsum", "rden"))

        main = ctx.enter_context(nc.psum_tensor("main", [P, 2, MT, NB], F32))
        side = ctx.enter_context(nc.psum_tensor("side", [P, 4, NB], F32))

        N1, N2, CW, CO, AO, GN, QG, KG = KT + 23, 0, KT, KT + 12, KT + 16, KT + 20, KT + 21, KT + 22
        NROWS_B = KG + 1
        GC_TILES = 3 * GDN_W // P

        raw_loaded = [sem(f"raw_loaded{i}") for i in range(RING)]
        hi_ready, lo_ready, chunk_done = sem("hi_ready"), sem("lo_ready"), sem("chunk_done")
        x_first_tile = sem("x_first_tile")
        x_loaded = [sem(f"x_loaded{i}") for i in range(NCB)]
        x_back, out_stored = sem("x_back"), sem("out_stored")
        rows_loaded, convw_loaded, heads_loaded = sem("rows_loaded"), sem("convw_loaded"), sem("heads_loaded")
        norm1_loaded = sem("norm1_loaded")
        const_step = sem("const_step")
        cols_turned, cols_ready = sem("cols_turned"), sem("cols_ready")
        ss_act, ss_dve, ssum_ready, rstd_ln, rstd_ready = (sem(n) for n in (
            "ss_act", "ss_dve", "ssum_ready", "rstd_ln", "rstd_ready"))
        h_turned, h_hi_ready, h_lo_ready = (sem(n) for n in ("h_turned", "h_hi_ready", "h_lo_ready"))
        blk_copied, blk_turned, pair_free, group_added = (sem(n) for n in (
            "blk_copied", "blk_turned", "pair_free", "group_added"))
        conv_first, conv_step, silu_done = sem("conv_first"), sem("conv_step"), sem("silu_done")
        gate_dve, gate_act, gate_pe = sem("gate_dve"), sem("gate_act"), sem("gate_pe")
        att_sq, att_sum, att_ln, att_rs, att_qk = (sem(n) for n in (
            "att_sq", "att_sum", "att_ln", "att_rs", "att_qk"))
        att_scores, att_sc, att_nm, att_exp, att_den, att_p = (sem(n) for n in (
            "att_scores", "att_sc", "att_nm", "att_exp", "att_den", "att_p"))
        att_pT, att_pT1, att_pT0, att_o, att_oe, att_on = (sem(n) for n in (
            "att_pT", "att_pT1", "att_pT0", "att_o", "att_oe", "att_on"))
        cm_a, cm_prod, cm_first, cm_step, cm_out, cm_sq, cm_sum, cm_ln, cm_rs, cm_on = (sem(n) for n in (
            "cm_a", "cm_prod", "cm_first", "cm_step", "cm_out", "cm_sq", "cm_sum", "cm_ln", "cm_rs", "cm_on"))
        z_silu, z_prod = sem("z_silu"), sem("z_prod")
        att_scaled = sem("att_scaled")
        ones_ready = sem("ones_ready")
        att_full, att_lo, cm_sqhi, cm_sqlo = (sem(n) for n in ("att_full", "att_lo", "cm_sqhi", "cm_sqlo"))
        mix_hi_ready, mix_lo_ready = sem("mix_hi_ready"), sem("mix_lo_ready")
        (gdn_sq, gdn_sqhi, gdn_sqlo, gdn_sum, gdn_ln, gdn_rs, gdn_kn, gdn_qn, gdn_grow, gdn_brow, gdn_rm, gdn_rm2,
         gdn_eg, gdn_dec, gdn_kb, gdn_vT, gdn_vb, gdn_kbe, gdn_gram, gdn_qk, gdn_AT, gdn_QKT, gdn_ktok,
         gdn_kdec, gdn_Ab, gdn_comb, gdn_combT, gdn_part0, gdn_inv, gdn_half, gdn_invT, gdn_turned,
         gdn_Al, gdn_Y, gdn_Ysb, gdn_upd, gdn_MT,
         gdn_v0ps, gdn_v0, gdn_Sps, gdn_S, gdn_o0, gdn_kSps, gdn_r1, gdn_v1ps, gdn_v1, gdn_o1ps, gdn_o1,
         gdn_osq, gdn_osqhi, gdn_osqlo, gdn_osum, gdn_oln, gdn_ors, gdn_on) = (sem("gdn_" + n) for n in (
            "sq", "sqhi", "sqlo", "sum", "ln", "rs", "kn", "qn", "grow", "brow", "rm", "rm2",
            "eg", "dec", "kb", "vT", "vb", "kbe", "gram", "qk", "AT", "QKT", "ktok",
            "kdec", "Ab", "comb", "combT", "part0", "inv", "half", "invT", "turned", "Al", "Y", "Ysb", "upd", "MT",
            "v0ps", "v0", "Sps", "S", "o0", "kSps", "r1", "v1ps", "v1", "o1ps", "o1",
            "osq", "osqhi", "osqlo", "osum", "oln", "ors", "on"))
        hid_relu, hid_turned, hid_sq, hid_hi, hid_lo = (sem(n) for n in (
            "hid_relu", "hid_turned", "hid_sq", "hid_hi", "hid_lo"))

        x_dram = x.rearrange("o (m p) d -> (o p) m d", p=P)
        out_dram = out.rearrange("o (m p) d -> (o p) m d", p=P)
        win_v = w_in.rearrange("o (t p) n -> (o p) t n", p=P)
        wout_v = w_out.rearrange("o (t p) n -> (o p) t n", p=P)
        wup_v = w_up.rearrange("o (t p) n -> (o p) t n", p=P)
        wdn_v = w_down.rearrange("o (t p) n -> (o p) t n", p=P)

        def flat(t):
            return t.rearrange("p a b -> p (a b)")

        def pair_ps(i):
            return main[:, i].rearrange("p m n -> p (m n)")

        def side_ps(i):
            return side[:, 2 * i:2 * i + 2].rearrange("p m n -> p (m n)")

        def tiles(t, n):
            return t.rearrange("p (a b) -> p a b", a=n)

        def over(t, n):
            return t.unsqueeze(1).to_broadcast([P, n, t.shape[1]])

        def along(t, w):
            return t.unsqueeze(2).to_broadcast([P, t.shape[1], w])

        keys_tok = tok[:, :, 0:KV * P].rearrange("p m (k d) -> p m k d", d=P)
        key_squares = buf[4][:, 0:MT * KV * DA].rearrange("p (m k d) -> p m k d", m=MT, k=KV)
        att_k = buf[1][:, 0:NB]
        vals = tiles(buf[1][:, NB:NB + MT * KV * DA], MT)
        p1 = tiles(buf[2][:], 4)
        p0 = tiles(half[0][:], 4)

        def turn_ps(which, j):
            if which == 0:
                return (side_ps(0), pair_ps(1), side_ps(1), side_ps(0))[j]
            return (side_ps(1), side_ps(0), side_ps(1), side_ps(1))[j]

        def turn_block_at(b):
            if b in (AT_KV, AT_AQ):
                return after(b) + 3
            return after(b) + (1 if b < AT_CC else 0)

        def turn_slot(n):
            return C_LAST_QUAD + CPG * n + CPG + (1 if n < NCB - 1 else 2)

        comb = buf[2][:, 0:NB]
        y_sb = buf[2][:, NB:2 * NB]
        inv = buf[3][:, 0:NB]
        inv_part = buf[3][:, NB:2 * NB]
        inv_turned = half[0][:]

        def part(l):
            return buf[1][:, (l % 2) * NB:(l % 2 + 1) * NB]

        def token_tile(t, m):
            return t.rearrange("p (h m t) -> p h m t", h=CT, m=MT)[:, :, m]

        def sq_parts(quad):
            quad_tiles = slice(CT * quad, CT * (quad + 1))
            return flat(mix_hi[:, quad_tiles]), flat(mix_lo[:, quad_tiles])

        def block_ps(b):
            return side_ps(0) if b == NBLK - 1 else pair_ps(b % 2)

        def tap(b, k, t):
            first = {"gq": 0, "gk": HG, "gv": 2 * HG}[BLOCKS[b][0]]
            return k * GC_TILES + first + CT * ((b - 2) // 3) + t

        def raw_value(c):
            return 16 * (c // RING + 1) + 16 * min(c // RING + 1, CPB // RING)

        block = ctx.enter_context(nc.Block())

        @block.sync
        def _(sp):
            def load(c, slot, src):
                if c is not None:
                    sp.wait_ge(lo_ready, c)
                sp.dma_start(raw[:, slot], src).then_inc(raw_loaded[slot], 16)

            for c in range(C_OUT):
                b, k = c // CPB, c % CPB
                kind, col = BLOCKS[b]
                rows = slice(KPC * k, KPC * (k + 1))
                if c == 0:
                    for m in range(MT):
                        sp.dma_start(x_sb[:, m, 0:NB], x_dram[:, m, 0:NB]).then_inc(
                            x_first_tile if m == 0 else x_loaded[0], 16)
                elif c < NCB:
                    sp.dma_start(x_sb[:, :, c * NB:(c + 1) * NB],
                                 x_dram[:, :, c * NB:(c + 1) * NB]).then_inc(x_loaded[c], 16)
                free = c - RING + 1 if c >= RING else None
                if kind == "kv":
                    if free is not None:
                        sp.wait_ge(lo_ready, free)
                    sp.dma_start(raw[:, c % RING, :, 0:KVW],
                                 win_v[:, rows, col:col + KVW]).then_inc(raw_loaded[c % RING], 16)
                    sp.dma_start(raw[:, c % RING, :, KVW:KVW + BA],
                                 win_v[:, rows, GD_B:GD_B + BA]).then_inc(raw_loaded[c % RING], 16)
                else:
                    load(free, c % RING, win_v[:, rows, col:col + NB])
            for c in range(C_OUT, C_MLP):
                g, k = (c - C_OUT) // CPG, (c - C_OUT) % CPG
                t = QUADS[g // NCB] * CT + k * KPC
                n = g % NCB
                load(c - RING + 1, c % RING, wout_v[:, t:t + KPC, n * NB:(n + 1) * NB])
            for c in range(C_MLP, C_LOOP):
                k = c - C_MLP
                load(c - RING + 1, c % RING, wup_v[:, KPC * k:KPC * (k + 1), 0:NB])
            with sp.Fori(0, TURNS) as it:
                for s in range(PER):
                    free = it * PER + (C_LOOP + s - RING + 1)
                    if s < CPB:
                        src = wup_v[:, KPC * s:KPC * (s + 1), bass.ds(it * NB + NB, NB)]
                    else:
                        n, k = (s - CPB) // CPG, (s - CPB) % CPG
                        src = wdn_v[:, bass.ds(it * CT + k * KPC, KPC), n * NB:(n + 1) * NB]
                    load(free, s % RING, src)
            for c in range(C_LAST, CHUNKS):
                n, k = (c - C_LAST) // CPG, (c - C_LAST) % CPG
                t = (FB - 1) * CT + k * KPC
                load(c - RING + 1, c % RING, wdn_v[:, t:t + KPC, n * NB:(n + 1) * NB])
            for n in range(NCB - 1):
                sp.wait_ge(group_added, G_MLP + NCB * (FB - 1) + n + 1)
                sp.dma_start(out_dram[:, :, n * NB:(n + 1) * NB],
                             x_sb[:, :, n * NB:(n + 1) * NB]).then_inc(out_stored, 16)
            for m in range(MT):
                sp.wait_ge(group_added, G_MLP + NCB * FB + m)
                sp.dma_start(out_dram[:, m, D - NB:D], x_sb[:, m, D - NB:D]).then_inc(out_stored, 16)
            sp.wait_ge(out_stored, 16 * (NCB - 1 + MT))

        N_BASE = 15
        N_CONST = N_BASE + 5 * LEVELS + 3 * (LEVELS - 1)

        @block.gpsimd
        def _(pool):
            steps = [0]

            def step(ins):
                steps[0] += 1
                ins.then_inc(const_step, 1)
                pool.wait_ge(const_step, steps[0])

            def where(t, base, pattern, mult, fill, op=ALU.is_ge):
                step(pool.affine_select(out=t, in_=t, compare_op=op, fill=fill, base=base,
                                        pattern=pattern, channel_multiplier=mult))

            step(pool.memset(ident[:], 1.0))
            where(ident[:], 0, [[-1, P]], 1, 0.0, ALU.is_equal)
            step(pool.memset(eps_col[:], EPS))
            for row, v in ((N2, norm2_g), (CO, conv_out_g), (AO, attn_out_g), (GN, gdn_norm_g)):
                n = v.shape[1] // P
                pool.dma_start(rows_b[row:row + n, :], v.rearrange("o (t n) -> (o t) n", n=P)).then_inc(rows_loaded, 16)
            pool.dma_start(rows_b[CW:CW + 3 * CT, :],
                           conv_w.rearrange("o k (t n) -> (o k t) n", n=P)).then_inc(rows_loaded, 16)
            for row, v in ((QG, q_norm_g), (KG, k_norm_g)):
                for j in range(2):
                    pool.dma_start(rows_b[row:row + 1, j * DA:(j + 1) * DA], v).then_inc(rows_loaded, 16)
            pool.dma_start(rows_a, gdn_conv_w.rearrange("o k (t n) -> (o k t) n", n=P)).then_inc(convw_loaded, 16)
            for i, v in enumerate((gdn_A_log, gdn_dt_bias, attn_sinks)):
                pool.dma_start(heads_bc[:, i], v[0].partition_broadcast(P)).then_inc(heads_loaded, 16)
            step(pool.memset(q_scale[:], -0.5 * log(DG)))
            step(pool.memset(ones[:], 1.0))
            step(pool.memset(upper[:], 1.0))
            where(upper[:], 0, [[1, P]], -1, 0.0)
            step(pool.memset(upper_add[:], 0.0))
            where(upper_add[:], 0, [[1, P]], -1, NEG)
            step(pool.memset(pair_ones[:], 0.0))
            step(pool.memset(pair_ones[0:DA, 0:DA], 1.0))
            step(pool.memset(pair_ones[DA:P, DA:P], 1.0))
            step(pool.memset(band[:], 0.0))
            where(band[:, 0:P], -1, [[1, P]], -1, NEG)
            where(band[:, P:2 * P], 0, [[-1, P]], 1, NEG)
            for l in range(LEVELS):
                w = 2 ** l
                n = P // (2 * w)
                step(pool.memset(joins[:, l], 1.0))
                blocks = joins[:, l].rearrange("p (n h w) -> p n h w", h=2, w=w)
                for j in range(2):
                    first = (1 - j) * w
                    where(blocks[:, :, j, :], -first, [[-2 * w, n], [0, w]], 1, 0.0)
                    where(blocks[:, :, j, :], first + w - 1, [[2 * w, n], [0, w]], -1, 0.0)
            for l in range(1, LEVELS):
                w = 2 ** l
                n = P // (2 * w)
                step(pool.memset(halves[:, l - 1], 1.0))
                blocks = halves[:, l - 1].rearrange("p (n h w) -> p n h w", h=2, w=w)
                where(blocks[:, :, 0, :], 0, [[-2 * w, n], [-1, w]], 1, 0.0)
                where(blocks[:, :, 1, :], w, [[2 * w, n], [1, w]], -1, 0.0)

            def square_of(dst, src, out_sem):
                pool.tensor_tensor(dst, src, src, ALU.mult).then_inc(out_sem, 1)

            def squares_of_keys_and_queries(b):
                if b == 0:
                    pool.wait_ge(att_on, 1)
                    pool.wait_ge(att_scores, KV)
                else:
                    pool.wait_ge(gdn_Y, 6 * b)
                for n in range(2):
                    pool.wait_ge(silu_done, 3 * b + n + 1)
                    square_of((buf[4], buf[0][:])[n], flat(qkv[b][n][:]), gdn_sq)

            pool.wait_ge(att_oe, KV)
            square_of(buf[5], flat(fm_b[:]), att_full)
            squares_of_keys_and_queries(0)

            for b in range(2):
                h = slice(4 * b, 4 * b + 4)
                units = 2 * CT
                pool.wait_ge(gate_dve, 13)
                if b == 0:
                    pool.wait_ge(att_scores, KV)
                    pool.wait_ge(att_o, KV)
                else:
                    pool.wait_ge(gdn_Y, 6 * b)
                pool.wait_ge(gdn_rm, b + 1)
                pool.tensor_tensor(tiles(buf[0][:], units), tiles(buf[0][:], units),
                                   along(flat(gcum[:, h]), P), ALU.subtract).then_inc(gdn_rm2, 1)
                pool.wait_ge(gdn_comb, b + 1)
                if b == 1:
                    pool.wait_ge(gdn_osqlo, 2 * b)
                for l in range(1, LEVELS):
                    if b == 1 and l == LEVELS - 1:
                        pool.wait_ge(cm_out, 1)
                        square_of(flat(fm_a[:]), flat(fm_b[:]), cm_sq)
                    if l == 2:
                        pool.wait_ge(gdn_inv, LEVELS * b + 1)
                    elif l > 2:
                        pool.wait_ge(gdn_Y, 6 * b + l - 2)
                    pool.tensor_tensor(tiles(part(l), CT), tiles(comb, CT), over(joins[:, l], CT),
                                       ALU.mult).then_inc(gdn_Al, 1)
                if b == 0:
                    squares_of_keys_and_queries(1)
                for m, done in enumerate((gdn_o0, gdn_o1)):
                    pool.wait_ge(done, b + 1)
                    square_of(token_tile(buf[1][:], m), qkv[b][1][:, :, m * P:(m + 1) * P], gdn_osq)

        @block.scalar
        def _(act):
            def hi(loaded, slot, n=NB, used=None):
                act.wait_ge(raw_loaded[slot], loaded)
                if used is not None:
                    act.wait_ge(chunk_done, used)
                act.activation(w_hi[:, slot, :, 0:n], raw[:, slot, :, 0:n], ACT.Copy).then_inc(hi_ready, 1)

            def hi_of(c):
                if c < CHUNKS:
                    hi(raw_value(c), c % RING, KVW + BA if c < CPB else NB, c - RING + 1 if c >= RING else None)

            def inverse_root(ps, tmp, scale, waited, value, ln_sem, out_sem, bias=0.0):
                act.wait_ge(waited, value)
                act.activation(tmp, ps, ACT.Ln, scale=scale, bias=eps_col[:, 0:1]).then_inc(ln_sem, 1)
                act.wait_ge(ln_sem, value)
                act.activation(tmp, tmp, ACT.Exp, scale=-0.5, bias=bias).then_inc(out_sem, 1)

            def square(which, n):
                q = which * NCB + n
                if which == 0:
                    act.wait_ge(x_loaded[n] if n else x_first_tile, 16)
                else:
                    act.wait_ge(group_added, G_MLP - NCB + n + 1)
                if q > 0:
                    act.wait_ge(ss_act, q)
                act.activation(fm_a[:, 0:2].rearrange("p a b -> p (a b)"), x_sb[:, 0, n * NB:(n + 1) * NB],
                               ACT.Square, accum_out=ss[:, 0, n:n + 1]).then_inc(ss_act, 1)

            def scale_of_tokens(which):
                act.wait_ge(ssum_ready, which + 1)
                act.activation(rstd[:], ssum[:], ACT.Ln, scale=1.0 / D, bias=eps_col[:, 0:1]).then_inc(rstd_ln, 1)
                act.wait_ge(rstd_ln, which + 1)
                act.activation(rstd[:], rstd[:], ACT.Exp, scale=-0.5).then_inc(rstd_ready, 1)

            def piece(which, j):
                ps = turn_ps(which, j)
                for t in range(CT):
                    k = CT * j + t
                    if t % KPC == 0:
                        act.wait_ge(h_turned, which * CPB + k // KPC + 1)
                    g = (N2 if which else N1) + k
                    last = act.activation(h_hi[:, k], ps[:, t * S:(t + 1) * S], ACT.Copy, scale=cols_b[:, g:g + 1])
                    if t % KPC == KPC - 1:
                        last.then_inc(h_hi_ready, 1)

            def mixed(order, first, src, gain, waited, value):
                act.wait_ge(waited, value)
                if gain is None:
                    act.activation(mix_hi[:, first:first + CT], src[:], ACT.Copy).then_inc(mix_hi_ready, 1)
                    return
                for t in range(CT):
                    last = act.activation(mix_hi[:, first + t], src[:, t], ACT.Copy,
                                          scale=cols_b[:, gain + t:gain + t + 1])
                last.then_inc(mix_hi_ready, 1)

            def copy_block(b):
                act.wait_ge(chunk_done, after(b))
                if b == 0:
                    act.wait_ge(rstd_ready, 1)
                for m in range(MT):
                    ps, scale = main[:, b % 2, m], rstd[:, m:m + 1]
                    if b == AT_KV:
                        keys = ps[:, 0:KV * DA].rearrange("p (k d) -> p k d", d=DA)
                        dup = tok[:, m, 0:KV * P].rearrange("p (k j d) -> p k j d", j=2, d=DA)
                        for j in range(2):
                            act.activation(dup[:, :, j], keys, ACT.Copy, scale=scale)
                        act.activation(vals[:, m], ps[:, KV * DA:KVW], ACT.Copy, scale=scale)
                        last = act.activation(ba[:, m], ps[:, KVW:KVW + BA], ACT.Copy, scale=scale)
                    else:
                        last = act.activation(tok[:, m], ps, ACT.Copy, scale=scale)
                last.then_inc(blk_copied, 1)

            def side_work(c):
                for b in range(NBLK):
                    if c == after(b):
                        copy_block(b)
                for n in range(NCB):
                    if c == C_LAST_QUAD + CPG * n + CPG - 1:
                        square(1, n)
                    if c == turn_slot(n) + 1:
                        piece(1, n)
                if c == C_MLP + 3:
                    scale_of_tokens(1)
                if c == after(AT_KV):
                    act.wait_ge(blk_copied, AT_KV + 1)
                    act.activation(key_squares, keys_tok[:, :, :, 0:DA], ACT.Square).then_inc(att_sq, 1)
                if c == A_KV + 1:
                    inverse_root(key_sums[:], key_sums[:], 1.0 / DA, att_sum, 1, att_ln, att_rs)
                if c == A_KV + 3:
                    act.wait_ge(blk_turned, AT_KV + 1)
                    act.activation(att_k, pair_ps(AT_KV)[:, 0:NB], ACT.Copy,
                                   scale=cols_b[:, KG:KG + 1]).then_inc(att_qk, 1)
                if c == A_KV + 3:
                    act.wait_ge(gate_dve, 3)
                    act.activation(sc[3][:], sc[0][:], ACT.Exp)
                    act.activation(sc[4][:], sc[2][:], ACT.Exp)
                    act.wait_ge(heads_loaded, 48)
                    act.activation(e_alog[:], heads_bc[:, 0], ACT.Exp).then_inc(gate_act, 1)
                if c == A_KV + 4:
                    act.wait_ge(gate_dve, 5)
                    act.activation(sc[7][:], sc[6][:], ACT.Ln).then_inc(gate_act, 1)
                if c == A_KV + 7:
                    act.wait_ge(gate_dve, 14)
                    act.activation(kdecay[:], kdiff[:], ACT.Exp).then_inc(gate_act, 1)
                if c == A_Q:
                    act.wait_ge(blk_copied, AT_AQ + 1)
                    act.activation(buf[4], flat(tok[:]), ACT.Square).then_inc(att_sq, 1)
                if c == A_Q + 2:
                    inverse_root(query_sums[:], query_sums[:], 1.0 / DA, att_sum, 2, att_ln, att_rs)
                if c == A_Q + 4:
                    act.wait_ge(blk_turned, AT_AQ + 1)
                    act.activation(buf[0][:], pair_ps(AT_AQ), ACT.Copy, scale=cols_b[:, QG:QG + 1]).then_inc(att_qk, 1)
                for kv in range(KV):
                    a = A_HEADS + A_STEPS * kv
                    if c == a + 2:
                        act.wait_ge(att_nm, 3 * (kv + 1))
                        for u in range(4):
                            act.activation(p1[:, u], p1[:, u], ACT.Exp, bias=nmx[:, u:u + 1], accum_out=den[:, u:u + 1])
                    if c == a + 3:
                        for u in range(4):
                            act.activation(p0[:, u], p0[:, u], ACT.Exp, bias=nmx[:, 4 + u:5 + u],
                                           accum_out=den[:, 4 + u:5 + u])
                        act.activation(es[:], esi[:], ACT.Exp).then_inc(att_exp, 1)
                    if c == a + 6:
                        act.wait_ge(att_pT, kv + 1)
                        act.activation(buf[3][:], side_ps(0), ACT.Copy).then_inc(att_pT1, 1)
                    if c == a + 7:
                        act.wait_ge(att_o, kv + 1)
                        act.activation(fm_b[:, 2 * kv:2 * kv + 2].rearrange("p r (m q) -> p m r q", m=MT),
                                       side[:, 3].rearrange("p (m r q) -> p m r q", m=MT, r=2),
                                       ACT.Copy).then_inc(att_oe, 1)
                if c == A_NORM:
                    act.wait_ge(att_oe, KV)
                    act.activation(sq_parts(3)[0], flat(fm_b[:]), ACT.Square).then_inc(att_sq, 1)
                if c == A_NORM + 2:
                    inverse_root(side_ps(0), buf[4], 1.0 / DA, att_sum, 3, att_ln, att_rs)
                if c == A_NORM + 3:
                    mixed(0, CT, fm_b, AO, att_on, 1)
                for b in range(2, 8):
                    if c == turn_block_at(b) + 1:
                        act.wait_ge(blk_turned, b + 1)
                        dst = qkv[(b - 2) // 3][(b - 2) % 3]
                        for t in range(CT):
                            w = tap(b, 3, t)
                            last = act.activation(dst[:, t], pair_ps(b % 2)[:, t * S:(t + 1) * S], ACT.Copy,
                                                  scale=cols_a[:, w:w + 1])
                        last.then_inc(conv_first, 1)
                for i in range(2):
                    if c == SILU_AT[i] - 3:
                        act.preload_act_table_set(SILU)
                    for n in range(3):
                        if c == SILU_AT[i] + n + (n == 2):
                            act.wait_ge(conv_step, 9 * i + 3 * (n + 1))
                            act.activation(flat(qkv[i][n][:]), flat(qkv[i][n][:]), ACT.Silu).then_inc(silu_done, 1)
                    for n in range(2):
                        if c == SILU_AT[i] + n + 1:
                            act.wait_ge(silu_done, 3 * i + n + 1)
                            act.activation(sq_parts(2 + n)[0], flat(qkv[i][n][:]), ACT.Square).then_inc(gdn_sqhi, 1)
                    if c == SILU_AT[i] + 4:
                        act.preload_act_table_set(LN_EXP)
                    gdn(i, c - GDN_START[i])
                if c == after(AT_CC) + 1:
                    act.wait_ge(blk_turned, AT_CC + 1)
                    act.activation(flat(fm_a[:]), pair_ps(AT_CC % 2), ACT.Copy).then_inc(cm_a, 1)
                if c == after(AT_CX) + 2:
                    act.wait_ge(cm_prod, 1)
                    for t in range(CT):
                        w = CW + 2 * CT + t
                        last = act.activation(fm_b[:, t], fm_a[:, t], ACT.Copy, scale=cols_b[:, w:w + 1])
                    last.then_inc(cm_first, 1)
                if c == after(AT_CB) + 1:
                    act.wait_ge(cm_out, 1)
                    act.activation(sq_parts(3)[0], flat(fm_b[:]), ACT.Square).then_inc(cm_sqhi, 1)
                if c == after(AT_CB) + 3:
                    act.wait_ge(cm_sum, 1)
                    act.activation(flat(tok[:]), pair_ps(AT_CB % 2), ACT.Ln, scale=1.0 / P,
                                   bias=eps_col[:, 0:1]).then_inc(cm_ln, 1)
                    act.wait_ge(cm_ln, 1)
                    act.activation(flat(tok[:]), flat(tok[:]), ACT.Exp, scale=-0.5).then_inc(cm_rs, 1)
                if c == after(AT_CB) + 5:
                    mixed(1, 0, fm_b, CO, cm_on, 1)
                for i in range(2):
                    b = AT_Z + i
                    if c == after(b) + 1:
                        act.wait_ge(blk_turned, b + 1)
                        if i == 1:
                            act.wait_ge(mix_lo_ready, 3)
                        act.activation(flat(fm_a[:]), block_ps(b), ACT.Silu).then_inc(z_silu, 1)
                    if c == after(b) - (3, 0)[i]:
                        act.preload_act_table_set(SILU)
                    if c == after(b) + 2 + 3 * i:
                        act.preload_act_table_set(LN_EXP)
                    if c == after(b) + 3:
                        mixed(2 + i, 2 * CT + CT * i, fm_a, None, z_prod, i + 1)
                if c == GDN_START[1] + 27:
                    act.wait_ge(gdn_o1ps, 2)
                    act.wait_ge(gdn_r1, 2)
                    act.dma_start(x_sb[:], x_dram).then_inc(x_back, 16)

            def gdn(i, s):
                k_t, q_t, v_t = qkv[i]
                if s == 1:
                    if i:
                        act.wait_ge(gdn_on, i)
                    inverse_root(side_ps(0), buf[2][:], 1.0, gdn_sum, 2 * i + 1, gdn_ln, gdn_rs)
                if s == 2:
                    inverse_root(side_ps(1), buf[3][:], 1.0, gdn_sum, 2 * i + 2, gdn_ln, gdn_rs, bias=q_scale[:, 0:1])
                if s == 3:
                    act.wait_ge(gdn_grow, i + 1)
                    act.activation(tiles(half[0][:], CT),
                                   side_ps(0).rearrange("p (h m t) -> p h m t", h=CT, m=MT)[:, :, 1],
                                   ACT.Exp).then_inc(gdn_eg, 1)
                if s == 5:
                    act.wait_ge(gdn_rm2, i + 1)
                    act.activation(buf[0][:], buf[0][:], ACT.Exp).then_inc(gdn_dec, 1)
                for l in range(1, LEVELS):
                    if s == 8 + 2 * l:
                        act.wait_ge(gdn_Y, 6 * i + l)
                        act.activation(y_sb, side[:, 0], ACT.Copy).then_inc(gdn_Ysb, 1)
                if s == 23:
                    act.wait_ge(gdn_v0ps, i + 1)
                    act.activation(half[4][:], side[:, 0], ACT.Copy).then_inc(gdn_v0, 1)
                if s == 26:
                    act.wait_ge(gdn_v1ps, i + 1)
                    act.activation(half[4][:], side[:, 0], ACT.Copy).then_inc(gdn_v1, 1)
                if s == 27:
                    act.wait_ge(gdn_o1ps, i + 1)
                    act.activation(q_t[:, :, P:S], tiles(side[:, 1], CT), ACT.Copy).then_inc(gdn_o1, 1)
                for m, done in enumerate((gdn_o0, gdn_o1)):
                    if s == 26 + m:
                        act.wait_ge(done, i + 1)
                        act.activation(token_tile(sq_parts(3 * i)[0], m), q_t[:, :, m * P:(m + 1) * P],
                                       ACT.Square).then_inc(gdn_osqhi, 1)
                if s == 29:
                    inverse_root(side_ps(1), buf[2][:], 1.0 / DG, gdn_osum, i + 1, gdn_oln, gdn_ors)

            act.dma_start(rows_n, norm1_g.rearrange("o (t n) -> (o t) n", n=P)).then_inc(norm1_loaded, 16)
            act.preload_act_table_set(LN_EXP)
            hi_of(0)
            act.wait_ge(cols_ready, 1)
            for j in range(2):
                piece(0, j)
                hi_of(j + 1)
            act.wait_ge(const_step, 3)
            for c in range(C_LOOP):
                if c < CPB or c >= C_OUT:
                    hi_of(c + AHEAD)
                if c < NCB - 2:
                    piece(0, c + 2)
                if 2 <= c < NCB + 2:
                    square(0, c - 2)
                if c == NCB + 3:
                    scale_of_tokens(0)
                side_work(c)
                if CPB <= c < C_OUT:
                    hi_of(c + AHEAD)

            def relu(value):
                act.wait_ge(chunk_done, value)
                for m in range(MT):
                    last = act.activation(tok[:, m], side[:, m], ACT.Relu, scale=rstd[:, m:m + 1])
                last.then_inc(hid_relu, 1)

            def square_hidden(value):
                act.wait_ge(hid_turned, value)
                act.activation(flat(fm_a[:]), side_ps(1), ACT.Square).then_inc(hid_sq, 1)

            def hidden_hi(value):
                act.wait_ge(hid_sq, value)
                act.activation(mix_hi[:, 0:CT], fm_a[:], ACT.Copy).then_inc(hid_hi, 1)

            relu(C_LOOP)
            square_hidden(1)

            def turn(it, last=False):
                for s in range(PER):
                    c = C_LOOP + s + AHEAD
                    hi(it * (16 * PER // RING) + raw_value(c), c % RING, NB, it * PER + (c - RING + 1))
                    if s == 0:
                        hidden_hi(it + 1)
                    if s == CPB:
                        relu(it * PER + (C_LOOP + CPB))
                    if s == CPB + 4:
                        act.wait_ge(hid_lo, it + 1)
                        square_hidden(it + 2)
                    if last and s == CPB + 5:
                        act.wait_ge(hid_sq, FB)
                        act.activation(mix_hi[:, CT:2 * CT], fm_a[:], ACT.Copy).then_inc(hid_hi, 1)

            with act.Fori(0, TURNS - 1) as it:
                turn(it)
            turn(TURNS - 1, last=True)
            for c in range(C_LAST, CHUNKS):
                hi_of(c + AHEAD)

        @block.vector
        def _(dve):
            def lo(ready, slot, n=NB):
                dve.wait_ge(hi_ready, ready)
                dve.tensor_tensor(w_lo[:, slot, :, 0:n], raw[:, slot, :, 0:n],
                                  w_hi[:, slot, :, 0:n].bitcast(F32), ALU.subtract).then_inc(lo_ready, 1)

            def lo_of(c):
                if c < CHUNKS:
                    lo(c + 1, c % RING, KVW + BA if c < CPB else NB)

            def square(which, n):
                q = which * NCB + n
                if which == 0:
                    dve.wait_ge(x_loaded[n], 16)
                else:
                    dve.wait_ge(group_added, G_MLP - NCB + n + 1)
                if q > 0:
                    dve.wait_ge(ss_dve, q)
                cols = x_sb[:, 1, n * NB:(n + 1) * NB]
                dve.tensor_tensor_reduce(fm_a[:, 2:4].rearrange("p a b -> p (a b)"), cols, cols, 1.0, 0.0,
                                         ALU.mult, ALU.add, ss[:, 1, n:n + 1]).then_inc(ss_dve, 1)

            def sum_of_squares(which):
                dve.wait_ge(ss_act, NCB * (which + 1))
                dve.wait_ge(ss_dve, NCB * (which + 1))
                dve.tensor_reduce(ssum[:], ss[:], AX_X, ALU.add).then_inc(ssum_ready, 1)

            def piece(which, j):
                ps = turn_ps(which, j)
                for t in range(CT):
                    k = CT * j + t
                    if t % KPC == 0:
                        dve.wait_ge(h_hi_ready, which * CPB + k // KPC + 1)
                    g = (N2 if which else N1) + k
                    last = dve.scalar_tensor_tensor(h_lo[:, k], ps[:, t * S:(t + 1) * S], cols_b[:, g:g + 1],
                                                    h_hi[:, k].bitcast(F32), ALU.mult, ALU.subtract)
                    if t % KPC == KPC - 1:
                        last.then_inc(h_lo_ready, 1)

            def mixed(order, first, src, gain):
                dve.wait_ge(mix_hi_ready, order + 1)
                if gain is None:
                    dve.tensor_tensor(mix_lo[:, first:first + CT], src[:],
                                      mix_hi[:, first:first + CT].bitcast(F32), ALU.subtract).then_inc(mix_lo_ready, 1)
                    return
                for t in range(CT):
                    last = dve.scalar_tensor_tensor(mix_lo[:, first + t], src[:, t], cols_b[:, gain + t:gain + t + 1],
                                                    mix_hi[:, first + t].bitcast(F32), ALU.mult, ALU.subtract)
                last.then_inc(mix_lo_ready, 1)

            def add_group(done, pair, n):
                dve.wait_ge(chunk_done, done)
                cols = x_sb[:, :, n * NB:(n + 1) * NB]
                dve.tensor_tensor(cols, main[:, pair], cols, ALU.add).then_inc(group_added, 1)

            def add_group_of(c):
                g = (c - C_OUT) // CPG
                add_group(c + 1, (g + 1) % 2, g % NCB)

            gates = [0]

            def gate_op(ins):
                gates[0] += 1
                ins.then_inc(gate_dve, 1)
                dve.wait_ge(gate_dve, gates[0])

            def side_work(c):
                if C_OUT <= c < C_MLP and c % CPG == CPG - 1:
                    if c == C_OUT + CPG - 1:
                        dve.wait_ge(x_back, 16)
                    add_group_of(c)
                for n in range(NCB):
                    if c == C_LAST_QUAD + CPG * n + CPG - 1:
                        square(1, n)
                    if c == turn_slot(n) + 1:
                        piece(1, n)
                if c == C_MLP + 2:
                    sum_of_squares(1)
                if c == 7:
                    dve.wait_ge(cols_turned, 3)
                    dve.tensor_copy(cols_b[:, 0:NROWS_B], side[:, 3, 0:NROWS_B]).then_inc(cols_ready, 1)
                    dve.tensor_copy(cols_a[:], side[:, 3, P:P + 96]).then_inc(cols_ready, 1)
                if c == A_KV:
                    dve.wait_ge(att_sq, 1)
                    dve.tensor_reduce(key_sums[:], key_squares, AX_X, ALU.add).then_inc(att_sum, 1)
                if c == A_KV + 2:
                    dve.wait_ge(att_rs, 1)
                    dve.tensor_tensor(keys_tok, keys_tok, key_sums[:].unsqueeze(3).to_broadcast([P, MT, KV, P]),
                                      ALU.mult).then_inc(att_scaled, 1)
                if c == A_KV + 4:
                    dve.wait_ge(att_qk, 1)
                    dve.engine_nop().then_inc(pair_free, 1)
                if c == A_KV + 8:
                    dve.tensor_copy(ones_r[:], ones[:])
                    dve.tensor_copy(pair_ones_r[:], pair_ones[:]).then_inc(ones_ready, 1)
                if c == A_KV + 1:
                    dve.wait_ge(blk_copied, 1)
                    dve.wait_ge(heads_loaded, 48)
                    b_in = ba[:, :, 0:HG].rearrange("p m h -> p h m")
                    a_in = ba[:, :, HG:BA].rearrange("p m h -> p h m")
                    gate_op(dve.tensor_scalar(sc[0][:], b_in, -1.0, 87.0, ALU.mult, ALU.min))
                    gate_op(dve.tensor_tensor(sc[1][:], a_in, along(heads_bc[:, 1], MT), ALU.add))
                    gate_op(dve.scalar_tensor_tensor(sc[2][:], sc[1][:], -1.0, sc[1][:], ALU.mult, ALU.min))
                if c == A_KV + 3:
                    dve.wait_ge(gate_act, 1)
                    gate_op(dve.tensor_scalar(sc[5][:], sc[3][:], 1.0, None, ALU.add))
                    gate_op(dve.tensor_scalar(sc[6][:], sc[4][:], 1.0, None, ALU.add))
                    gate_op(dve.reciprocal(beta[:], sc[5][:]))
                    gate_op(dve.scalar_tensor_tensor(sc[8][:], sc[6][:], 1.0, sc[4][:], ALU.subtract, ALU.subtract))
                    gate_op(dve.reciprocal(sc[9][:], sc[6][:]))
                    gate_op(dve.tensor_tensor(sc[10][:], sc[8][:], sc[9][:], ALU.mult))
                if c == A_KV + 5:
                    dve.wait_ge(gate_act, 2)
                    gate_op(dve.tensor_tensor(sc[11][:], sc[7][:], sc[10][:], ALU.subtract))
                    gate_op(dve.scalar_tensor_tensor(sc[0][:], sc[1][:], 0.0, sc[11][:], ALU.max, ALU.add))
                    gate_op(dve.scalar_tensor_tensor(gate[:], sc[0][:], -1.0, along(e_alog[:], MT), ALU.mult, ALU.mult))
                if c == A_KV + 6:
                    dve.wait_ge(gate_pe, 1)
                    gate_op(dve.tensor_copy(flat(gcum[:]), side[:, 3, 0:HG * MT]))
                    gate_op(dve.tensor_tensor(kdiff[:], side[:, 3, HG * MT:HG * MT + HG], gcum[:, :, 0], ALU.subtract))
                if c == A_Q + 1:
                    dve.wait_ge(att_sq, 2)
                    dve.tensor_reduce(query_sums[:], tiles(buf[4], MT * HA), AX_X, ALU.add).then_inc(att_sum, 1)
                if c == A_Q + 3:
                    dve.wait_ge(att_rs, 2)
                    dve.tensor_tensor(tiles(flat(tok[:]), MT * HA), tiles(flat(tok[:]), MT * HA),
                                      along(query_sums[:], DA), ALU.mult).then_inc(att_scaled, 1)
                if c == A_Q + 5:
                    dve.wait_ge(att_qk, 2)
                    dve.engine_nop().then_inc(pair_free, 1)
                for kv in range(KV):
                    a = A_HEADS + A_STEPS * kv
                    sink = heads_bc[:, 2, 4 * kv:4 * kv + 4].rearrange("p (r a) -> p a r", a=2)
                    if c == a + 1:
                        dve.wait_ge(att_scores, kv + 1)
                        for u in range(4):
                            dve.tensor_tensor_reduce(p1[:, u], side[:, u // 2, (u % 2) * S:(u % 2 + 1) * S], band[:],
                                                     DA ** -0.5, LOWEST, ALU.add, ALU.max, mx[:, u:u + 1])
                            last = dve.tensor_tensor_reduce(p0[:, u], side[:, 2 + u // 2, (u % 2) * P:(u % 2 + 1) * P],
                                                            band[:, P:2 * P], DA ** -0.5, LOWEST, ALU.add, ALU.max,
                                                            mx[:, 4 + u:5 + u])
                        last.then_inc(att_sc, 1)
                    if c == a + 2:
                        dve.wait_ge(att_sc, kv + 1)
                        for m in range(MT):
                            last = dve.tensor_tensor(mxs[:, 4 * m:4 * m + 4].rearrange("p (a r) -> p a r", a=2),
                                                     mx[:, 4 * m:4 * m + 4].rearrange("p (a r) -> p a r", a=2),
                                                     sink, ALU.max)
                        last.then_inc(att_nm, 1)
                        dve.wait_ge(att_nm, 3 * kv + 1)
                        dve.tensor_scalar(nmx[:], mxs[:], -1.0, None, ALU.mult).then_inc(att_nm, 1)
                        dve.wait_ge(att_nm, 3 * kv + 2)
                        for m in range(MT):
                            last = dve.tensor_tensor(esi[:, 4 * m:4 * m + 4].rearrange("p (a r) -> p a r", a=2),
                                                     nmx[:, 4 * m:4 * m + 4].rearrange("p (a r) -> p a r", a=2),
                                                     sink, ALU.add)
                        last.then_inc(att_nm, 1)
                    if c == a + 4:
                        dve.wait_ge(att_exp, kv + 1)
                        dve.tensor_tensor(dsum[:], den[:], es[:], ALU.add).then_inc(att_den, 1)
                        dve.wait_ge(att_den, 2 * kv + 1)
                        dve.reciprocal(rden[:], dsum[:]).then_inc(att_den, 1)
                        dve.wait_ge(att_den, 2 * kv + 2)
                        dve.tensor_tensor(p1, p1, along(rden[:, 0:4], S), ALU.mult)
                        dve.tensor_tensor(p0, p0, along(rden[:, 4:8], P), ALU.mult).then_inc(att_p, 1)
                    if c == a + 6:
                        dve.wait_ge(att_pT, kv + 1)
                        dve.tensor_copy(half[1][:], side[:, 2]).then_inc(att_pT0, 1)
                if c == A_NORM + 1:
                    dve.wait_ge(att_full, 1)
                    dve.wait_ge(att_sq, 3)
                    rounded, rest = sq_parts(3)
                    dve.tensor_tensor(rest, buf[5], rounded.bitcast(F32), ALU.subtract).then_inc(att_lo, 1)
                if c == A_NORM + 2:
                    dve.wait_ge(att_rs, 3)
                    dve.tensor_tensor(flat(fm_b[:]), flat(fm_b[:]), buf[4], ALU.mult).then_inc(att_on, 1)
                if c == A_NORM + 3:
                    mixed(0, CT, fm_b, AO)
                for i in (1, 0):
                    gdn(i, c - GDN_START[i])
                for b in range(2, 8):
                    j = c - turn_block_at(b)
                    if 1 <= j <= 3:
                        if j == 1:
                            dve.wait_ge(conv_first, b - 1)
                        else:
                            dve.wait_ge(conv_step, 3 * (b - 2) + j - 1)
                        dst = qkv[(b - 2) // 3][(b - 2) % 3]
                        for t in range(CT):
                            w = tap(b, 3 - j, t)
                            last = dve.scalar_tensor_tensor(dst[:, t, j:S], pair_ps(b % 2)[:, t * S:(t + 1) * S - j],
                                                            cols_a[:, w:w + 1], dst[:, t, j:S], ALU.mult, ALU.add)
                        last.then_inc(conv_step, 1)
                        if j == 3:
                            dve.wait_ge(conv_step, 3 * (b - 1))
                            dve.engine_nop().then_inc(pair_free, 1)
                if c == after(AT_CX) + 1:
                    dve.wait_ge(blk_turned, AT_CX + 1)
                    dve.wait_ge(cm_a, 1)
                    dve.tensor_tensor(flat(fm_a[:]), pair_ps(AT_CX % 2), flat(fm_a[:]), ALU.mult).then_inc(cm_prod, 1)
                    dve.wait_ge(cm_prod, 1)
                    dve.engine_nop().then_inc(pair_free, 1)
                for j in (1, 2):
                    if c == after(AT_CX) + 1 + j:
                        if j == 1:
                            dve.wait_ge(cm_first, 1)
                        else:
                            dve.wait_ge(cm_step, 1)
                        for t in range(CT):
                            w = CW + (2 - j) * CT + t
                            last = dve.scalar_tensor_tensor(fm_b[:, t, j:S], fm_a[:, t, 0:S - j], cols_b[:, w:w + 1],
                                                            fm_b[:, t, j:S], ALU.mult, ALU.add)
                        last.then_inc(cm_step, 1)
                if c == after(AT_CC) + 1:
                    dve.wait_ge(cm_a, 1)
                    dve.engine_nop().then_inc(pair_free, 1)
                if c == after(AT_CB) + 1:
                    dve.wait_ge(blk_turned, AT_CB + 1)
                    dve.wait_ge(cm_step, 2)
                    dve.tensor_tensor(flat(fm_b[:]), pair_ps(AT_CB % 2), flat(fm_b[:]), ALU.mult).then_inc(cm_out, 1)
                if c == after(AT_CB) + 2:
                    dve.wait_ge(cm_sqhi, 1)
                    dve.wait_ge(cm_sq, 1)
                    rounded, rest = sq_parts(3)
                    dve.tensor_tensor(rest, flat(fm_a[:]), rounded.bitcast(F32), ALU.subtract).then_inc(cm_sqlo, 1)
                if c == after(AT_CB) + 4:
                    dve.wait_ge(cm_rs, 1)
                    dve.engine_nop().then_inc(pair_free, 1)
                    dve.tensor_tensor(flat(fm_b[:]), flat(fm_b[:]), flat(tok[:]), ALU.mult).then_inc(cm_on, 1)
                if c == after(AT_CB) + 5:
                    mixed(1, 0, fm_b, CO)
                for i in range(2):
                    b = AT_Z + i
                    if b == NBLK - 1 and c == after(b):
                        dve.wait_ge(blk_copied, NBLK)
                        dve.engine_nop().then_inc(pair_free, 1)
                    if c == after(b) + 2:
                        dve.wait_ge(z_silu, i + 1)
                        if b < NBLK - 1:
                            dve.engine_nop().then_inc(pair_free, 1)
                        dve.wait_ge(gdn_on, i + 1)
                        dve.tensor_tensor(flat(fm_a[:]), flat(fm_a[:]), flat(qkv[i][1][:]), ALU.mult).then_inc(z_prod, 1)
                    if c == after(b) + 3:
                        mixed(2 + i, 2 * CT + CT * i, fm_a, None)

            def half_of_inverse(i, l):
                dve.wait_ge(gdn_inv, LEVELS * i + l)
                dve.tensor_tensor(tiles(inv_part, CT), tiles(inv, CT), over(halves[:, l - 1], CT),
                                  ALU.mult).then_inc(gdn_half, 1)

            def gdn(i, s):
                k_t, q_t, v_t = qkv[i]
                units = 2 * CT
                h = slice(4 * i, 4 * i + 4)
                for n in range(2):
                    if s == n - 1 - 2 * i:
                        rounded, rest = sq_parts(2 + n)
                        dve.wait_ge(gdn_sq, 2 * i + n + 1)
                        dve.wait_ge(gdn_sqhi, 2 * i + n + 1)
                        dve.tensor_tensor(rest, (buf[4], buf[0][:])[n], rounded.bitcast(F32),
                                          ALU.subtract).then_inc(gdn_sqlo, 1)
                if s == 2:
                    dve.wait_ge(gdn_rs, 2 * i + 1)
                    dve.tensor_tensor(flat(k_t[:]), flat(k_t[:]), buf[2][:], ALU.mult).then_inc(gdn_kn, 1)
                if s == 3:
                    dve.wait_ge(gdn_rs, 2 * i + 2)
                    dve.tensor_tensor(flat(q_t[:]), flat(q_t[:]), buf[3][:], ALU.mult).then_inc(gdn_qn, 1)
                    dve.wait_ge(gdn_eg, i + 1)
                    if i == 0:
                        dve.wait_ge(att_scores, KV)
                    else:
                        dve.wait_ge(gdn_Y, 6 * i)
                    dve.tensor_tensor(tiles(buf[0][:], units), tiles(side_ps(0), units), over(upper_add[:], units),
                                      ALU.add).then_inc(gdn_rm, 1)
                if s == 4:
                    dve.wait_ge(gdn_brow, i + 1)
                    dve.wait_ge(gdn_kn, i + 1)
                    dve.wait_ge(gdn_qn, i + 1)
                    dve.tensor_tensor(buf[3][:], side_ps(1), flat(k_t[:]), ALU.mult).then_inc(gdn_kb, 1)
                if s == 5:
                    dve.wait_ge(gdn_vT, i + 1)
                    dve.tensor_tensor(tiles(buf[6], units), tiles(side_ps(0), units), along(flat(beta[:, h]), P),
                                      ALU.mult).then_inc(gdn_vb, 1)
                    dve.wait_ge(gdn_kb, i + 1)
                    dve.wait_ge(gdn_eg, i + 1)
                    kb = buf[3][:].rearrange("p (h m t) -> p h m t", h=CT, m=MT)[:, :, 1]
                    dve.tensor_tensor(tiles(half[1][:], CT), kb, tiles(half[0][:], CT), ALU.mult).then_inc(gdn_kbe, 1)
                    dve.tensor_tensor(tiles(half[2][:], CT), q_t[:, :, P:S], tiles(half[0][:], CT),
                                      ALU.mult).then_inc(gdn_kbe, 1)
                if s == 6:
                    dve.wait_ge(gdn_gram, i + 1)
                    dve.wait_ge(gdn_dec, i + 1)
                    dve.tensor_tensor(buf[4], side_ps(1), buf[0][:], ALU.mult).then_inc(gdn_AT, 1)
                if s == 7:
                    dve.wait_ge(gdn_qk, i + 1)
                    dve.tensor_tensor(buf[5], side_ps(0), buf[0][:], ALU.mult).then_inc(gdn_QKT, 1)
                if s == 8:
                    dve.wait_ge(gdn_ktok, i + 1)
                    dve.wait_ge(gate_act, 3)
                    dve.tensor_tensor(tiles(half[3][:], CT), tiles(side[:, 2], CT), along(kdecay[:, h], P),
                                      ALU.mult).then_inc(gdn_kdec, 1)
                    dve.wait_ge(gdn_Ab, i + 1)
                    dve.wait_ge(gdn_AT, i + 1)
                    dve.tensor_tensor(tiles(comb, CT), token_tile(buf[4], 0), tiles(side[:, 3], CT),
                                      ALU.add).then_inc(gdn_comb, 1)
                if s == 9:
                    if i == 0:
                        dve.wait_ge(const_step, N_CONST)
                        dve.wait_ge(att_o, KV)
                    else:
                        dve.wait_ge(gdn_osqlo, 2 * i)
                    dve.wait_ge(gdn_combT, i + 1)
                    dve.tensor_tensor(tiles(part(0), CT), tiles(side[:, 0], CT), over(joins[:, 0], CT),
                                      ALU.mult).then_inc(gdn_part0, 1)
                    dve.wait_ge(gdn_part0, i + 1)
                    dve.wait_ge(gdn_kbe, 2 * i + 2)
                    dve.tensor_tensor(tiles(inv, CT), over(ident[:], CT), tiles(part(0), CT),
                                      ALU.subtract).then_inc(gdn_inv, 1)
                    half_of_inverse(i, 1)
                for l in range(1, LEVELS):
                    if s == 8 + 2 * l:
                        dve.wait_ge(gdn_invT, LEVELS * i + l)
                        dve.tensor_tensor(tiles(inv_turned, CT), tiles(side[:, 1], CT), over(halves[:, l - 1], CT),
                                          ALU.mult).then_inc(gdn_turned, 1)
                    if s == 9 + 2 * l:
                        dve.wait_ge(gdn_upd, 6 * i + l)
                        dve.wait_ge(gdn_half, 6 * i + l)
                        dve.tensor_tensor(inv, inv, side[:, 2], ALU.subtract).then_inc(gdn_inv, 1)
                        if l < LEVELS - 1:
                            half_of_inverse(i, l + 1)
                if s == 22:
                    dve.wait_ge(gdn_invT, LEVELS * (i + 1))
                    dve.wait_ge(gdn_inv, LEVELS * (i + 1))
                    dve.tensor_tensor(token_tile(buf[7], 0), tiles(side[:, 1], CT), over(upper[:], CT),
                                      ALU.mult).then_inc(gdn_MT, 1)
                    dve.tensor_tensor(token_tile(buf[7], 1), tiles(inv, CT), over(upper[:], CT),
                                      ALU.mult).then_inc(gdn_MT, 1)
                if s == 24:
                    dve.wait_ge(gdn_Sps, i + 1)
                    dve.tensor_copy(half[5][:], side[:, 1]).then_inc(gdn_S, 1)
                    dve.tensor_copy(q_t[:, :, 0:P], tiles(side[:, 2], CT)).then_inc(gdn_o0, 1)
                if s == 25:
                    dve.wait_ge(gdn_kSps, i + 1)
                    vb = buf[6].rearrange("p (h m t) -> p h m t", h=CT, m=MT)[:, :, 1]
                    dve.tensor_tensor(tiles(half[0][:], CT), vb, tiles(side[:, 3], CT), ALU.subtract).then_inc(gdn_r1, 1)
                for m in range(MT):
                    if s == 27 + m:
                        rounded, rest = (token_tile(part_of, m) for part_of in sq_parts(3 * i))
                        dve.wait_ge(gdn_osq, 2 * i + m + 1)
                        dve.wait_ge(gdn_osqhi, 2 * i + m + 1)
                        dve.tensor_tensor(rest, token_tile(buf[1][:], m), rounded.bitcast(F32),
                                          ALU.subtract).then_inc(gdn_osqlo, 1)
                if s == 29:
                    dve.wait_ge(gdn_ors, i + 1)
                    dve.scalar_tensor_tensor(flat(q_t[:]), flat(q_t[:]), cols_b[:, GN:GN + 1], buf[2][:],
                                             ALU.mult, ALU.mult).then_inc(gdn_on, 1)

            dve.wait_ge(cols_turned, 1)
            dve.tensor_copy(cols_b[:, N1:N1 + KT], main[:, 0, 0, 0:KT]).then_inc(cols_ready, 1)
            lo_of(0)
            for j in range(2):
                piece(0, j)
                lo_of(j + 1)
            for c in range(C_LOOP):
                if c < CPB or c >= C_OUT:
                    lo_of(c + AHEAD)
                if c < NCB - 2:
                    piece(0, c + 2)
                if 2 <= c < NCB + 2:
                    square(0, c - 2)
                if c == NCB + 2:
                    sum_of_squares(0)
                side_work(c)
                if CPB <= c < C_OUT:
                    lo_of(c + AHEAD)

            def hidden_lo(value):
                dve.wait_ge(hid_hi, value)
                dve.tensor_tensor(mix_lo[:, 0:CT], fm_a[:], mix_hi[:, 0:CT].bitcast(F32),
                                  ALU.subtract).then_inc(hid_lo, 1)

            def turn(it, last=False):
                for s in range(PER):
                    lo(it * PER + (C_LOOP + s + AHEAD + 1), (s + AHEAD) % RING)
                    if s == 0:
                        hidden_lo(it + 1)
                    if s >= CPB and (s - CPB) % CPG == CPG - 1:
                        n = (s - CPB) // CPG
                        add_group(it * PER + (C_LOOP + s + 1), (G_MLP + n + 1) % 2, n)
                    if last and s == CPB + 6:
                        dve.wait_ge(hid_hi, FB)
                        dve.tensor_tensor(mix_lo[:, CT:2 * CT], fm_a[:], mix_hi[:, CT:2 * CT].bitcast(F32),
                                          ALU.subtract).then_inc(hid_lo, 1)

            with dve.Fori(0, TURNS - 1) as it:
                turn(it)
            turn(TURNS - 1, last=True)
            for c in range(C_LAST, CHUNKS):
                lo_of(c + AHEAD)
                n = (c - C_LAST) // CPG
                if (c - C_LAST) % CPG == CPG - 1 and n < NCB - 1:
                    add_group(c + 1, (G_MLP + n + 1) % 2, n)
            for m in range(MT):
                dve.wait_ge(chunk_done, CHUNKS + m)
                cols = x_sb[:, m, D - NB:D]
                dve.tensor_tensor(cols, main[:, (G_MLP + NCB) % 2, m], cols, ALU.add).then_inc(group_added, 1)

        @block.tensor
        def _(pe):
            def chunk(ready, slot, lhs, k, banks, n, first, last, by_tile=False):
                hi_t, lo_t = lhs
                pe.wait_ge(lo_ready, ready)
                steps = [(j, m) for j in range(KPC) for m in range(MT)]
                for j, m in sorted(steps, key=lambda step: step[1]) if by_tile else steps:
                    a_hi = hi_t[:, k + j, m * P:(m + 1) * P]
                    a_lo = lo_t[:, k + j, m * P:(m + 1) * P]
                    w_h, w_l = w_hi[:, slot, j, 0:n], w_lo[:, slot, j, 0:n]
                    o = banks[:, m, 0:n]
                    end = last and j == KPC - 1
                    pe.matmul(o, a_hi, w_h, start=first and j == 0, stop=False)
                    pe.matmul(o, a_hi, w_l, start=False, stop=False)
                    ins = pe.matmul(o, a_lo, w_h, start=False, stop=end)
                    if by_tile and (j, m) == (KPC - 1, 0):
                        ins.then_inc(chunk_done, 1)
                ins.then_inc(chunk_done, 1)

            h_t, mix_t = (h_hi, h_lo), (mix_hi, mix_lo)

            def turn_piece(which, j):
                if which == 0:
                    if j == 0:
                        pe.wait_ge(x_first_tile, 16)
                    if j == 3:
                        pe.wait_ge(h_lo_ready, CPG)
                else:
                    pe.wait_ge(group_added, G_MLP - NCB + j + 1)
                    if j == 1:
                        pe.wait_ge(z_silu, 2)
                    if j > 1:
                        pe.wait_ge(h_lo_ready, CPB + CPG * (j - (j == 2)))
                ps = turn_ps(which, j)
                for m in range(MT):
                    if which == 0 and m == (1 if j == 0 else 0):
                        pe.wait_ge(x_loaded[j], 16)
                    for t in range(CT):
                        ins = pe.transpose(ps[:, t * S + m * P:t * S + (m + 1) * P],
                                           x_sb[:, m, (CT * j + t) * P:(CT * j + t + 1) * P], ident[:])
                        if m == MT - 1 and t % KPC == KPC - 1:
                            ins.then_inc(h_turned, 1)

            def turn_block(b):
                if b in (AT_KV, AT_AQ):
                    pe.wait_ge(att_scaled, b + 1)
                else:
                    pe.wait_ge(blk_copied, b + 1)
                if b == NBLK - 1:
                    pe.wait_ge(gdn_o1, 2)
                ps = block_ps(b)
                if b == AT_KV:
                    for k in range(KV):
                        for m in range(MT):
                            ins = pe.transpose(ps[:, k * S + m * P:k * S + (m + 1) * P],
                                               tok[:, m, k * P:(k + 1) * P], ident[:])
                else:
                    for t in range(CT):
                        for m in range(MT):
                            ins = pe.transpose(ps[:, t * S + m * P:t * S + (m + 1) * P],
                                               tok[:, m, t * P:(t + 1) * P], ident[:])
                ins.then_inc(blk_turned, 1)

            def split_sums(ps, weights, hi_part, lo_part):
                for j in range(2):
                    cols = slice(j * NB, (j + 1) * NB)
                    pe.matmul(ps[:, cols], weights[:], hi_part[:, cols],
                              start=True, stop=False)
                    ins = pe.matmul(ps[:, cols], weights[:], lo_part[:, cols],
                                    start=False, stop=True)
                return ins

            def side_work(c):
                for b in range(NBLK):
                    if c == turn_block_at(b):
                        turn_block(b)
                for n in range(NCB):
                    if c == turn_slot(n):
                        turn_piece(1, n)
                if c < NCB - 2:
                    turn_piece(0, c + 2)
                if c == 6:
                    pe.wait_ge(h_lo_ready, 3 * CPG)
                    pe.wait_ge(rows_loaded, 16 * 9)
                    pe.transpose(side[:, 3, 0:NROWS_B], rows_b[0:NROWS_B, :],
                                 ident[0:NROWS_B, 0:NROWS_B]).then_inc(cols_turned, 1)
                    pe.wait_ge(convw_loaded, 16)
                    pe.transpose(side[:, 3, P:P + 96], rows_a, ident[0:96, 0:96]).then_inc(cols_turned, 1)
                if c == A_KV + 5:
                    pe.wait_ge(gate_dve, 12)
                    pe.wait_ge(const_step, N_BASE)
                    pe.matmul(side[:, 3, 0:HG * MT], upper[:], flat(gate[:]), start=True, stop=True)
                    pe.matmul(side[:, 3, HG * MT:HG * MT + HG], ones[:], gate[:, :, 0],
                              start=True, stop=True).then_inc(gate_pe, 1)
                for kv in range(KV):
                    a = A_HEADS + A_STEPS * kv
                    q_fm = tiles(buf[0][:], CT)
                    if c == a:
                        pe.wait_ge(att_qk, 2)
                        if kv == 0:
                            pe.wait_ge(gate_dve, 14)
                        else:
                            pe.wait_ge(att_oe, kv)
                        for u in range(4):
                            par, pr = u // 2, u % 2
                            rows = slice(par * DA, (par + 1) * DA)
                            q_h = q_fm[rows, 2 * kv + pr]
                            pe.matmul(side[:, par, pr * S:(pr + 1) * S], q_h[:, P:S],
                                      att_k[rows, kv * S:(kv + 1) * S], start=True, stop=True)
                            ins = pe.matmul(side[:, 2 + par, pr * P:(pr + 1) * P], q_h[:, 0:P],
                                            att_k[rows, kv * S:kv * S + P], start=True, stop=True)
                        ins.then_inc(att_scores, 1)
                    if c == a + 5:
                        pe.wait_ge(att_p, kv + 1)
                        for u in range(4):
                            for kt in range(2):
                                pe.transpose(side[:, kt, u * P:(u + 1) * P], p1[:, u, kt * P:(kt + 1) * P], ident[:])
                            ins = pe.transpose(side[:, 2, u * P:(u + 1) * P], p0[:, u], ident[:])
                        ins.then_inc(att_pT, 1)
                    if c == a + 6:
                        pe.wait_ge(att_pT1, kv + 1)
                        pe.wait_ge(att_pT0, kv + 1)
                        pt1 = buf[3][:].rearrange("p (k u q) -> p k u q", k=2, u=4)
                        pt0 = tiles(half[1][:], 4)
                        for par in range(2):
                            o = side[par * DA:(par + 1) * DA, 3]
                            two = slice(2 * par, 2 * par + 2)
                            v_h = vals[:, :, kv * DA:(kv + 1) * DA]
                            pe.matmul(o[:, 0:S], v_h[:, 0], pt0[:, two], start=True, stop=True)
                            pe.matmul(o[:, S:2 * S], v_h[:, 0], pt1[:, 0, two], start=True, stop=False)
                            ins = pe.matmul(o[:, S:2 * S], v_h[:, 1], pt1[:, 1, two], start=False, stop=True)
                        ins.then_inc(att_o, 1)
                if c == A_NORM + 1:
                    pe.wait_ge(att_lo, 1)
                    pe.wait_ge(ones_ready, 1)
                    split_sums(side_ps(0), pair_ones_r, *sq_parts(3)).then_inc(att_sum, 1)
                for i in range(2):
                    gdn(i, c - GDN_START[i])
                if c == after(AT_CB) + 2:
                    pe.wait_ge(cm_sqlo, 1)
                    split_sums(pair_ps(AT_CB % 2), ones_r, *sq_parts(3)).then_inc(cm_sum, 1)

            def gdn(i, s):
                k_t, q_t, v_t = qkv[i]
                units = [(h, m) for h in range(CT) for m in range(MT)]

                def unit(t, h, m):
                    return t[:, (2 * h + m) * P:(2 * h + m + 1) * P]

                def head(t, h):
                    return t[:, h * P:(h + 1) * P]

                def turn_inverse():
                    for h in range(CT):
                        ins = pe.transpose(head(side[:, 1], h), head(inv, h), ident[:])
                    ins.then_inc(gdn_invT, 1)

                def column(t, h, m):
                    return t[:, 4 * i + h, m:m + 1].to_broadcast([P, P])

                if s == 0:
                    pe.wait_ge(gdn_sqlo, 2 * i + 1)
                    split_sums(side_ps(0), ones_r, *sq_parts(2)).then_inc(gdn_sum, 1)
                    if i:
                        pe.wait_ge(gdn_oln, i)
                    pe.wait_ge(gdn_sqlo, 2 * i + 2)
                    split_sums(side_ps(1), ones_r, *sq_parts(3)).then_inc(gdn_sum, 1)
                if s == 2:
                    pe.wait_ge(gate_dve, 13)
                    pe.wait_ge(gdn_ln, 2 * i + 1)
                    for h, m in units:
                        ins = pe.transpose(unit(side_ps(0), h, m), column(gcum, h, m), ident[:])
                    ins.then_inc(gdn_grow, 1)
                if s == 3:
                    pe.wait_ge(gdn_ln, 2 * i + 2)
                    for h, m in units:
                        ins = pe.transpose(unit(side_ps(1), h, m), column(beta, h, m), ident[:])
                    ins.then_inc(gdn_brow, 1)
                if s == 4:
                    pe.wait_ge(gdn_rm, i + 1)
                    pe.wait_ge(gdn_eg, i + 1)
                    for h, m in units:
                        ins = pe.transpose(unit(side_ps(0), h, m), v_t[:, h, m * P:(m + 1) * P], ident[:])
                    ins.then_inc(gdn_vT, 1)
                if s == 5:
                    pe.wait_ge(gdn_kb, i + 1)
                    for h, m in units:
                        ins = pe.matmul(unit(side_ps(1), h, m), k_t[:, h, m * P:(m + 1) * P],
                                        unit(buf[3], h, m), start=True, stop=True)
                    ins.then_inc(gdn_gram, 1)
                if s == 6:
                    pe.wait_ge(gdn_vb, i + 1)
                    pe.wait_ge(gdn_qn, i + 1)
                    for h, m in units:
                        ins = pe.matmul(unit(side_ps(0), h, m), k_t[:, h, m * P:(m + 1) * P],
                                        q_t[:, h, m * P:(m + 1) * P], start=True, stop=True)
                    ins.then_inc(gdn_qk, 1)
                if s == 7:
                    pe.wait_ge(gdn_AT, i + 1)
                    for h in range(CT):
                        ins = pe.transpose(head(side[:, 2], h), k_t[:, h, 0:P], ident[:])
                    ins.then_inc(gdn_ktok, 1)
                    for h in range(CT):
                        ins = pe.transpose(head(side[:, 3], h), unit(buf[4], h, 1), ident[:])
                    ins.then_inc(gdn_Ab, 1)
                if s == 8:
                    pe.wait_ge(gdn_comb, i + 1)
                    pe.wait_ge(gdn_QKT, i + 1)
                    for h in range(CT):
                        ins = pe.transpose(head(side[:, 0], h), head(comb, h), ident[:])
                    ins.then_inc(gdn_combT, 1)
                for l in range(1, LEVELS):
                    if s == 7 + 2 * l:
                        pe.wait_ge(gdn_inv, LEVELS * i + l)
                        turn_inverse()
                        pe.wait_ge(gdn_half, 6 * i + l)
                        pe.wait_ge(gdn_Al, 6 * i + l)
                        for h in range(CT):
                            ins = pe.matmul(head(side[:, 0], h), head(part(l), h), head(inv_part, h),
                                            start=True, stop=True)
                        ins.then_inc(gdn_Y, 1)
                    if s == 8 + 2 * l:
                        if l == 1:
                            pe.wait_ge(gdn_kdec, i + 1)
                        pe.wait_ge(gdn_turned, 6 * i + l)
                        pe.wait_ge(gdn_Ysb, 6 * i + l)
                        for h in range(CT):
                            ins = pe.matmul(head(side[:, 2], h), head(inv_turned, h), head(y_sb, h),
                                            start=True, stop=True)
                        ins.then_inc(gdn_upd, 1)
                if s == 21:
                    pe.wait_ge(gdn_inv, LEVELS * (i + 1))
                    turn_inverse()
                if s == 22:
                    pe.wait_ge(gdn_MT, 2 * (i + 1))
                    for h in range(CT):
                        ins = pe.matmul(head(side[:, 0], h), unit(buf[7], h, 0), unit(buf[6], h, 0),
                                        start=True, stop=True)
                    ins.then_inc(gdn_v0ps, 1)
                if s == 23:
                    pe.wait_ge(gdn_v0, i + 1)
                    for h in range(CT):
                        pe.matmul(head(side[:, 1], h), head(half[3], h), head(half[4], h), start=True, stop=True)
                    for h in range(CT):
                        ins = pe.matmul(head(side[:, 2], h), head(half[4], h), unit(buf[5], h, 0),
                                        start=True, stop=True)
                    ins.then_inc(gdn_Sps, 1)
                if s == 24:
                    pe.wait_ge(gdn_S, i + 1)
                    for h in range(CT):
                        ins = pe.matmul(head(side[:, 3], h), head(half[1], h), head(half[5], h),
                                        start=True, stop=True)
                    ins.then_inc(gdn_kSps, 1)
                if s == 25:
                    pe.wait_ge(gdn_r1, i + 1)
                    for h in range(CT):
                        ins = pe.matmul(head(side[:, 0], h), unit(buf[7], h, 1), head(half[0], h),
                                        start=True, stop=True)
                    ins.then_inc(gdn_v1ps, 1)
                if s == 26:
                    pe.wait_ge(gdn_v1, i + 1)
                    for h in range(CT):
                        pe.matmul(head(side[:, 1], h), head(half[5], h), head(half[2], h), start=True, stop=False)
                        ins = pe.matmul(head(side[:, 1], h), head(half[4], h), unit(buf[5], h, 1),
                                        start=False, stop=True)
                    ins.then_inc(gdn_o1ps, 1)
                if s == 28:
                    pe.wait_ge(gdn_osqlo, 2 * (i + 1))
                    split_sums(side_ps(1), ones_r, *sq_parts(3 * i)).then_inc(gdn_osum, 1)

            pe.wait_ge(const_step, 2)
            turn_piece(0, 0)
            pe.wait_ge(norm1_loaded, 16)
            pe.transpose(main[:, 0, 0, 0:KT], rows_n, ident[0:KT, 0:KT]).then_inc(cols_turned, 1)
            turn_piece(0, 1)
            pe.wait_ge(cols_ready, 1)
            for c in range(C_OUT):
                b, k = c // CPB, c % CPB
                if k == 0 and b >= 2:
                    pe.wait_ge(pair_free, b - 1)
                if b == 0:
                    pe.wait_ge(h_lo_ready, k + 1)
                n = KVW + BA if b == AT_KV else NB
                chunk(c + 1, c % RING, h_t, k * KPC, main[:, b % 2], n, k == 0, k == CPB - 1)
                side_work(c)
            for c in range(C_OUT, C_MLP):
                g, k = (c - C_OUT) // CPG, (c - C_OUT) % CPG
                if k == 0:
                    if g < 2:
                        pe.wait_ge(pair_free, NBLK - 1 + g)
                    else:
                        pe.wait_ge(group_added, g - 1)
                    if g % NCB == 0:
                        pe.wait_ge(mix_lo_ready, g // NCB + 1)
                chunk(c + 1, c % RING, mix_t, QUADS[g // NCB] * CT + k * KPC, main[:, (g + 1) % 2], NB,
                      k == 0, k == CPG - 1)
                side_work(c)
            def turn_hidden(value):
                pe.wait_ge(hid_relu, value)
                for t in range(CT):
                    for m in range(MT):
                        ins = pe.transpose(side_ps(1)[:, t * S + m * P:t * S + (m + 1) * P],
                                           tok[:, m, t * P:(t + 1) * P], ident[:])
                ins.then_inc(hid_turned, 1)

            for k in range(CPB):
                pe.wait_ge(h_lo_ready, CPB + max(k + 1, 2 * CPG))
                chunk(C_MLP + k + 1, (C_MLP + k) % RING, h_t, k * KPC, side[:, 0:2], NB, k == 0, k == CPB - 1)
                side_work(C_MLP + k)
            turn_hidden(1)
            with pe.Fori(0, TURNS) as it:
                pe.wait_ge(hid_relu, it + 1)
                for s in range(CPB):
                    chunk(it * PER + (C_LOOP + s + 1), s % RING, h_t, s * KPC, side[:, 0:2], NB,
                          s == 0, s == CPB - 1)
                pe.wait_ge(hid_lo, it + 1)
                for s in range(CPB, PER):
                    n, k = (s - CPB) // CPG, (s - CPB) % CPG
                    if k == 0:
                        pe.wait_ge(group_added, it * NCB + (G_MLP + n - 1))
                    chunk(it * PER + (C_LOOP + s + 1), s % RING, mix_t, k * KPC, main[:, (G_MLP + n + 1) % 2], NB,
                          k == 0, k == CPG - 1)
                    if s == CPB + 2:
                        turn_hidden(it + 2)
            pe.wait_ge(hid_lo, FB)
            for c in range(C_LAST, CHUNKS):
                n, k = (c - C_LAST) // CPG, (c - C_LAST) % CPG
                if k == 0:
                    pe.wait_ge(group_added, G_MLP + NCB * (FB - 1) + n - 1)
                chunk(c + 1, c % RING, mix_t, CT + k * KPC, main[:, (G_MLP + n + 1) % 2], NB,
                      k == 0, k == CPG - 1, by_tile=c == CHUNKS - 1)


_INS = ["x", "norm1_g", "w_in", "conv_w", "conv_out_g", "q_norm_g", "k_norm_g", "attn_sinks", "attn_out_g",
        "gdn_conv_w", "gdn_A_log", "gdn_dt_bias", "gdn_norm_g", "w_out", "norm2_g", "w_up", "w_down"]


def kernel(**inputs):
    import numpy as np
    import concourse.bacc as bacc
    from concourse.bass_utils import run_bass_kernel_spmd

    nc = bacc.Bacc("TRN2", target_bir_lowering=False, num_devices=1)
    arrays, args = {}, []
    for name in _INS:
        a = np.ascontiguousarray(inputs[name])
        arrays[f"in_{name}"] = a
        args.append(nc.dram_tensor(f"in_{name}", a.shape, mybir.dt.from_np(a.dtype), kind="ExternalInput").ap())
    args.append(nc.dram_tensor("out_0", inputs["x"].shape, F32, kind="ExternalOutput").ap())
    build(nc, *args)
    r = run_bass_kernel_spmd(nc, [arrays], core_ids=[0])
    return r.results[0]["out_0"]
```
